# Optimizing a Trainium2 kernel written in Bass

```python
import math
import jax
import jax.numpy as jnp
from jax import lax
import numpy as np

D_MODEL = 1024
BATCH = 1
SEQ = 1024
DEPTH = 2
DEC_BATCH = 8
DEC_SEQ = 4
PAST_LEN = 8192
PAGE_SIZE = 128

N_EVEN = (DEPTH + 1) // 2
N_ODD = DEPTH // 2

MLA_HEADS = 8
MLA_NOPE = 64
MLA_ROPE = 32
MLA_V = 64
MLA_Q_LORA = 384
MLA_KV_LORA = 256
MLA_WIDTH = MLA_HEADS * MLA_V
MLA_SCALE = (MLA_NOPE + MLA_ROPE) ** -0.5
ROPE_THETA = 10000.0

S5_GROUPS = 32
S5_GROUP_CH = 16
S5_STATE = 64
S5_WIDTH = S5_GROUPS * S5_GROUP_CH

NSA_HEADS = 16
NSA_KV_GROUPS = 2
NSA_REP = NSA_HEADS // NSA_KV_GROUPS
NSA_HEAD_DIM = 64
NSA_WIDTH = NSA_HEADS * NSA_HEAD_DIM
NSA_KV_WIDTH = NSA_KV_GROUPS * NSA_HEAD_DIM
NSA_BLOCK = 64
NSA_TOPK = 16
NSA_WINDOW = 512
NSA_QCHUNK = 64
NSA_SCALE = NSA_HEAD_DIM ** -0.5
FORCED_BONUS = float(NSA_REP + 1)

Q_BLOCK = 128
EPS = 1e-6

EVEN_SIZES = (MLA_Q_LORA, MLA_KV_LORA, MLA_ROPE, MLA_WIDTH, S5_WIDTH, S5_WIDTH)
EVEN_IN = sum(EVEN_SIZES)
ODD_SIZES = (NSA_WIDTH,) + (NSA_KV_WIDTH,) * 6 + (3 * NSA_HEADS, NSA_WIDTH)
ODD_IN = sum(ODD_SIZES)

kernel_name = 'hybrid_mla_s5_nsa_step'

def _split_points(sizes):
    return [int(s) for s in np.cumsum(sizes)[:-1]]

def rmsnorm(x, g):
    xf = x.astype(jnp.float32)
    y = xf * lax.rsqrt(jnp.mean(xf * xf, axis=-1, keepdims=True) + EPS)
    return (y * g.astype(jnp.float32)).astype(x.dtype)

def rope(x, pos):
    half = x.shape[-1] // 2
    inv = ROPE_THETA ** (-jnp.arange(half, dtype=jnp.float32) / half)
    ang = pos.astype(jnp.float32)[:, None] * inv[None, :]
    ang = ang.reshape((pos.shape[0],) + (1,) * (x.ndim - 3) + (half,))
    cos, sin = jnp.cos(ang), jnp.sin(ang)
    xf = x.astype(jnp.float32)
    x1, x2 = xf[..., :half], xf[..., half:]
    return jnp.concatenate([x1 * cos - x2 * sin, x1 * sin + x2 * cos], axis=-1).astype(x.dtype)

def alibi_slopes(n_heads):
    return 2.0 ** (-8.0 * jnp.arange(1, n_heads + 1, dtype=jnp.float32) / n_heads)

def masked_softmax(s, mask):
    s = jnp.where(mask, s, -jnp.inf)
    m = jnp.max(s, axis=-1, keepdims=True)
    m = jnp.where(jnp.isfinite(m), m, 0.0)
    e = jnp.exp(s - m)
    den = jnp.sum(e, axis=-1, keepdims=True)
    return e / jnp.where(den > 0, den, 1.0)

def mla_core(q_lat, q_rope, ckv, krope, qpos, kpos):
    s = (jnp.einsum('bqhc,bkc->bhqk', q_lat, ckv)
         + jnp.einsum('bqhr,bkr->bhqk', q_rope, krope)).astype(jnp.float32) * MLA_SCALE
    s = jnp.where(kpos[None, None, None, :] <= qpos[None, None, :, None], s, -jnp.inf)
    p = jax.nn.softmax(s, axis=-1).astype(ckv.dtype)
    return jnp.einsum('bhqk,bkc->bqhc', p, ckv)

def mla_prompt(q_lat, q_rope, ckv, krope, pos):
    B, T = q_lat.shape[:2]
    nb = T // Q_BLOCK
    qb = q_lat.reshape(B, nb, Q_BLOCK, MLA_HEADS, MLA_KV_LORA).swapaxes(0, 1)
    rb = q_rope.reshape(B, nb, Q_BLOCK, MLA_HEADS, MLA_ROPE).swapaxes(0, 1)
    pb = pos.reshape(nb, Q_BLOCK)
    o = lax.map(lambda a: mla_core(a[0], a[1], ckv, krope, a[2], pos), (qb, rb, pb))
    return o.swapaxes(0, 1).reshape(B, T, MLA_HEADS, MLA_KV_LORA)

def _linear_combine(left, right):
    a_l, b_l = left
    a_r, b_r = right
    return a_r * a_l, a_r * b_l + b_r

def s5_scan(u, h0, lam_re, lam_im, log_dt, b_re, b_im, c_re, c_im, d_skip):
    B, T, _ = u.shape
    f32 = jnp.float32
    uf = u.astype(f32).reshape(B, T, S5_GROUPS, S5_GROUP_CH)
    lam = lax.complex(lam_re.astype(f32), lam_im.astype(f32))
    dt = jnp.exp(log_dt.astype(f32))[:, None]
    lam_dt = lam * dt
    lam_bar = jnp.exp(lam_dt)
    b_bar = ((lam_bar - 1.0) / lam)[:, :, None] * lax.complex(b_re.astype(f32), b_im.astype(f32))
    bu = jnp.einsum('gnp,btgp->btgn', b_bar, uf.astype(jnp.complex64))
    a = jnp.broadcast_to(lam_bar, bu.shape)
    _, h = lax.associative_scan(_linear_combine, (a, bu), axis=1)
    if h0 is not None:
        steps = jnp.arange(1, T + 1, dtype=f32)[:, None, None]
        h = h + jnp.exp(lam_dt[None] * steps)[None] * h0[:, None]
    c = lax.complex(c_re.astype(f32), c_im.astype(f32))
    y = jnp.einsum('gpn,btgn->btgp', c, h).real + d_skip.astype(f32) * uf
    return y.reshape(B, T, S5_WIDTH).astype(u.dtype), h[:, -1]

def even_mixer(x, pos, w, mla_past, s5_h0):
    (norm_g, w_in, g_q, g_kv, w_uq, w_uk, w_uv, lam_re, lam_im, log_dt,
     b_re, b_im, c_re, c_im, d_skip, w_glu, b_glu, w_out) = w
    B, T, _ = x.shape
    h = rmsnorm(x, norm_g)
    proj = jnp.einsum('btd,de->bte', h, w_in)
    cq_raw, ckv_raw, kr_raw, z_a, u, z_b = jnp.split(proj, _split_points(EVEN_SIZES), axis=-1)
    cq = rmsnorm(cq_raw, g_q)
    q = jnp.einsum('btc,chd->bthd', cq, w_uq)
    q_lat = jnp.einsum('bthn,chn->bthc', q[..., :MLA_NOPE], w_uk)
    q_rope = rope(q[..., MLA_NOPE:], pos)
    ckv = rmsnorm(ckv_raw, g_kv)
    krope = rope(kr_raw, pos)
    new_rows = jnp.concatenate([ckv, krope], axis=-1)
    if mla_past is None:
        o_lat = mla_prompt(q_lat, q_rope, ckv, krope, pos)
    else:
        rows = jnp.concatenate([mla_past, new_rows], axis=1)
        kpos = jnp.arange(rows.shape[1], dtype=jnp.int32)
        o_lat = mla_core(q_lat, q_rope, rows[..., :MLA_KV_LORA], rows[..., MLA_KV_LORA:], pos, kpos)
    o_a = jnp.einsum('bthc,chv->bthv', o_lat, w_uv).reshape(B, T, MLA_WIDTH)
    y5, h_last = s5_scan(u, s5_h0, lam_re, lam_im, log_dt, b_re, b_im, c_re, c_im, d_skip)
    g5 = jax.nn.gelu(y5)
    o_b = g5 * jax.nn.sigmoid(g5 @ w_glu + b_glu)
    mix = jnp.concatenate([o_a * jax.nn.silu(z_a), o_b * jax.nn.silu(z_b)], axis=-1)
    state = jnp.stack([h_last.real, h_last.imag], axis=-1).astype(x.dtype)
    return x + mix @ w_out, new_rows, state

def gqa_attend(q, k, v, qpos, kpos, mask, slopes):
    s = jnp.einsum('...qgrd,...kgd->...grqk', q, k).astype(jnp.float32) * NSA_SCALE
    dist = (qpos[..., :, None] - kpos[..., None, :]).astype(jnp.float32)
    s = s - slopes[:, :, None, None] * dist[..., None, None, :, :]
    p = masked_softmax(s, mask[..., None, None, :, :])
    o = jnp.einsum('...grqk,...kgd->...qgrd', p.astype(v.dtype), v)
    return o, p

def nsa_compress(k, pe, phi1, phi2):
    B, L, G, d = k.shape
    nc = L // NSA_BLOCK
    kb = k[:, :nc * NSA_BLOCK].reshape(B, nc, NSA_BLOCK, G, d) + pe[None, None, :, None, :]
    kb = kb.transpose(0, 1, 3, 2, 4).reshape(B, nc, G, NSA_BLOCK * d)
    return jax.nn.silu(kb @ phi1) @ phi2

def nsa_select(p_cmp, qpos, n_sel, k_eff):
    imp = jnp.sum(p_cmp, axis=2)
    imp = jnp.pad(imp, ((0, 0), (0, 0), (0, 0), (0, n_sel - imp.shape[-1])))
    blk = jnp.arange(n_sel)[None, :]
    cur = (qpos // NSA_BLOCK)[:, None]
    forced = (blk == 0) | (blk == cur) | (blk == cur - 1)
    score = jnp.where(blk <= cur, imp + jnp.where(forced, FORCED_BONUS, 0.0), -jnp.inf)
    _, idx = lax.top_k(score, k_eff)
    return idx

def sel_attend(q, kg, vg, qpos, blk_idx, slopes):
    B, G, Tq, kk, _, d = kg.shape
    kpos = (blk_idx[..., None] * NSA_BLOCK + jnp.arange(NSA_BLOCK)).reshape(B, G, Tq, kk * NSA_BLOCK)
    kg = kg.reshape(B, G, Tq, kk * NSA_BLOCK, d)
    vg = vg.reshape(B, G, Tq, kk * NSA_BLOCK, d)
    s = jnp.einsum('bqgrd,bgqmd->bgrqm', q, kg).astype(jnp.float32) * NSA_SCALE
    dist = (qpos[None, None, :, None] - kpos).astype(jnp.float32)
    s = s - slopes[None, :, :, None, None] * dist[:, :, None]
    p = masked_softmax(s, (dist >= 0)[:, :, None])
    return jnp.einsum('bgrqm,bgqmd->bqgrd', p.astype(vg.dtype), vg)

def window_prompt(q, k, v, slopes):
    B, T = q.shape[:2]
    G, R, d = NSA_KV_GROUPS, NSA_REP, NSA_HEAD_DIM
    nb = T // Q_BLOCK
    span = NSA_WINDOW + Q_BLOCK
    kp = jnp.pad(k, ((0, 0), (NSA_WINDOW, 0), (0, 0), (0, 0)))
    vp = jnp.pad(v, ((0, 0), (NSA_WINDOW, 0), (0, 0), (0, 0)))
    qb = q.reshape(B, nb, Q_BLOCK, G, R, d).swapaxes(0, 1)

    def band(a):
        qi, i = a
        start = i * Q_BLOCK
        ki = lax.dynamic_slice_in_dim(kp, start, span, axis=1)
        vi = lax.dynamic_slice_in_dim(vp, start, span, axis=1)
        qpos = start + jnp.arange(Q_BLOCK)
        kpos = start - NSA_WINDOW + jnp.arange(span)
        mask = (kpos[None] >= 0) & (kpos[None] <= qpos[:, None]) & (qpos[:, None] - kpos[None] <= NSA_WINDOW)
        return gqa_attend(qi, ki, vi, qpos, kpos, mask, slopes)[0]

    o = lax.map(band, (qb, jnp.arange(nb)))
    return o.swapaxes(0, 1).reshape(B, T, G, R, d)

def nsa_mixer(x, pos, w, past):
    norm_g, w_in, pe_k, pe_v, phi1_k, phi2_k, phi1_v, phi2_v, w_out = w
    B, T, _ = x.shape
    G, R, d = NSA_KV_GROUPS, NSA_REP, NSA_HEAD_DIM
    h = rmsnorm(x, norm_g)
    proj = jnp.einsum('btd,de->bte', h, w_in)
    q, kc, vc, ks, vs, kw, vw, gate, z = jnp.split(proj, _split_points(ODD_SIZES), axis=-1)
    q = q.reshape(B, T, G, R, d)
    kc, vc, ks, vs, kw, vw = [t.reshape(B, T, G, d) for t in (kc, vc, ks, vs, kw, vw)]
    gate = jax.nn.sigmoid(gate.astype(jnp.float32)).reshape(B, T, 3, G, R, 1)
    slopes = alibi_slopes(NSA_HEADS).reshape(G, R)
    new_rows = jnp.stack([kc, vc, ks, vs], axis=2)
    bi = jnp.arange(B)[:, None, None, None]
    gi = jnp.arange(G)[None, :, None, None]

    if past is None:
        kc_all, vc_all = kc, vc
    else:
        cache_kv, li, page_table, win = past
        old = cache_kv[li, page_table, :, 0:2].reshape(B, PAST_LEN, 2, G, d)
        kc_all = jnp.concatenate([old[:, :, 0], kc], axis=1)
        vc_all = jnp.concatenate([old[:, :, 1], vc], axis=1)
    kcb = nsa_compress(kc_all, pe_k, phi1_k, phi2_k)
    vcb = nsa_compress(vc_all, pe_v, phi1_v, phi2_v)
    cpos = jnp.arange(kcb.shape[1]) * NSA_BLOCK + (NSA_BLOCK - 1)
    o_cmp, p_cmp = gqa_attend(q, kcb, vcb, pos, cpos, cpos[None, :] <= pos[:, None], slopes)

    n_sel = -(-kc_all.shape[1] // NSA_BLOCK)
    idx = nsa_select(p_cmp, pos, n_sel, min(NSA_TOPK, n_sel))
    k_eff = idx.shape[-1]
    if past is None:
        nblk = T // NSA_BLOCK
        ksb = ks.reshape(B, nblk, NSA_BLOCK, G, d)
        vsb = vs.reshape(B, nblk, NSA_BLOCK, G, d)
        nch = T // NSA_QCHUNK
        qc = q.reshape(B, nch, NSA_QCHUNK, G, R, d).swapaxes(0, 1)
        ic = idx.reshape(B, G, nch, NSA_QCHUNK, k_eff).transpose(2, 0, 1, 3, 4)
        pc = pos.reshape(nch, NSA_QCHUNK)

        def sel_chunk(a):
            qi, ii, pi = a
            return sel_attend(qi, ksb[bi, ii, :, gi], vsb[bi, ii, :, gi], pi, ii, slopes)

        o_sel = lax.map(sel_chunk, (qc, ic, pc)).swapaxes(0, 1).reshape(B, T, G, R, d)
    else:
        nbp = PAST_LEN // NSA_BLOCK
        sub = PAGE_SIZE // NSA_BLOCK
        nbn = -(-T // NSA_BLOCK)
        pad = nbn * NSA_BLOCK - T
        ksn = jnp.pad(ks, ((0, 0), (0, pad), (0, 0), (0, 0))).reshape(B, nbn, NSA_BLOCK, G, d)
        vsn = jnp.pad(vs, ((0, 0), (0, pad), (0, 0), (0, 0))).reshape(B, nbn, NSA_BLOCK, G, d)
        is_past = (idx < nbp)[..., None, None]
        ip = jnp.minimum(idx, nbp - 1)
        page = page_table[bi, ip // sub][..., None]
        rows = (ip % sub)[..., None] * NSA_BLOCK + jnp.arange(NSA_BLOCK)
        gsel = gi[..., None]
        kp = cache_kv[li, page, rows, 2, gsel]
        vp = cache_kv[li, page, rows, 3, gsel]
        inew = jnp.clip(idx - nbp, 0, nbn - 1)
        kg = jnp.where(is_past, kp, ksn[bi, inew, :, gi])
        vg = jnp.where(is_past, vp, vsn[bi, inew, :, gi])
        o_sel = sel_attend(q, kg, vg, pos, idx, slopes)

    if past is None:
        o_win = window_prompt(q, kw, vw, slopes)
        wrows = jnp.stack([kw, vw], axis=2)[:, -NSA_WINDOW:]
        new_win = jnp.pad(wrows, ((0, 0), (NSA_WINDOW - wrows.shape[1], 0), (0, 0), (0, 0), (0, 0)))
    else:
        kw_all = jnp.concatenate([win[:, :, 0], kw], axis=1)
        vw_all = jnp.concatenate([win[:, :, 1], vw], axis=1)
        wpos = jnp.concatenate([PAST_LEN - NSA_WINDOW + jnp.arange(NSA_WINDOW, dtype=jnp.int32), pos])
        mask = (wpos[None] >= 0) & (wpos[None] <= pos[:, None]) & (pos[:, None] - wpos[None] <= NSA_WINDOW)
        o_win, _ = gqa_attend(q, kw_all, vw_all, pos, wpos, mask, slopes)
        new_win = jnp.stack([kw_all[:, -NSA_WINDOW:], vw_all[:, -NSA_WINDOW:]], axis=2)

    o = gate[:, :, 0] * o_cmp + gate[:, :, 1] * o_sel + gate[:, :, 2] * o_win
    o = o.reshape(B, T, NSA_WIDTH).astype(x.dtype) * jax.nn.silu(z)
    return x + o @ w_out, new_rows, new_win

def setup_inputs(seed: int = 0) -> dict:
    key = jax.random.key(seed)
    ks = list(jax.random.split(key, 40))
    f32 = jnp.float32

    def nrm(k, shape, scale):
        return jax.random.normal(k, shape, f32) * scale

    n_pages = PAST_LEN // PAGE_SIZE
    n_pool = (DEC_BATCH * n_pages * 5 + 3) // 4
    G, d = NSA_KV_GROUPS, NSA_HEAD_DIM
    inp = {}
    inp['x_prompt'] = nrm(ks[0], (BATCH, SEQ, D_MODEL), 1.0)
    inp['x_sample'] = nrm(ks[1], (DEC_BATCH, DEC_SEQ, D_MODEL), 1.0)
    inp['cache_mla'] = nrm(ks[2], (N_EVEN, n_pool, PAGE_SIZE, MLA_KV_LORA + MLA_ROPE), 1.0)
    inp['state_s5'] = nrm(ks[3], (N_EVEN, DEC_BATCH, S5_GROUPS, S5_STATE, 2), 0.1)
    inp['cache_nsa_kv'] = nrm(ks[4], (N_ODD, n_pool, PAGE_SIZE, 4, G, d), 1.0)
    inp['state_nsa_win'] = nrm(ks[5], (N_ODD, DEC_BATCH, NSA_WINDOW, 2, G, d), 1.0)
    perm = jax.random.permutation(ks[6], n_pool)
    inp['page_table'] = perm[:DEC_BATCH * n_pages].reshape(DEC_BATCH, n_pages).astype(jnp.int32)
    inp['norm_even'] = 1.0 + nrm(ks[7], (N_EVEN, D_MODEL), 0.05)
    inp['w_in_even'] = nrm(ks[8], (N_EVEN, D_MODEL, EVEN_IN), D_MODEL ** -0.5)
    inp['mla_g_q'] = 1.0 + nrm(ks[9], (N_EVEN, MLA_Q_LORA), 0.05)
    inp['mla_g_kv'] = 1.0 + nrm(ks[10], (N_EVEN, MLA_KV_LORA), 0.05)
    inp['mla_w_uq'] = nrm(ks[11], (N_EVEN, MLA_Q_LORA, MLA_HEADS, MLA_NOPE + MLA_ROPE), MLA_Q_LORA ** -0.5)
    inp['mla_w_uk'] = nrm(ks[12], (N_EVEN, MLA_KV_LORA, MLA_HEADS, MLA_NOPE), MLA_KV_LORA ** -0.5)
    inp['mla_w_uv'] = nrm(ks[13], (N_EVEN, MLA_KV_LORA, MLA_HEADS, MLA_V), MLA_KV_LORA ** -0.5)
    inp['s5_lambda_re'] = -0.5 + nrm(ks[14], (N_EVEN, S5_GROUPS, S5_STATE), 0.01)
    inp['s5_lambda_im'] = math.pi * jnp.arange(S5_STATE, dtype=f32)[None, None, :] + nrm(ks[15], (N_EVEN, S5_GROUPS, S5_STATE), 0.01)
    inp['s5_log_dt'] = jax.random.uniform(ks[16], (N_EVEN, S5_GROUPS), f32, math.log(1e-3), math.log(1e-1))
    inp['s5_b_re'] = nrm(ks[17], (N_EVEN, S5_GROUPS, S5_STATE, S5_GROUP_CH), (2 * S5_GROUP_CH) ** -0.5)
    inp['s5_b_im'] = nrm(ks[18], (N_EVEN, S5_GROUPS, S5_STATE, S5_GROUP_CH), (2 * S5_GROUP_CH) ** -0.5)
    inp['s5_c_re'] = nrm(ks[19], (N_EVEN, S5_GROUPS, S5_GROUP_CH, S5_STATE), (2 * S5_STATE) ** -0.5)
    inp['s5_c_im'] = nrm(ks[20], (N_EVEN, S5_GROUPS, S5_GROUP_CH, S5_STATE), (2 * S5_STATE) ** -0.5)
    inp['s5_d'] = nrm(ks[21], (N_EVEN, S5_GROUPS, S5_GROUP_CH), 1.0)
    inp['s5_w_glu'] = nrm(ks[22], (N_EVEN, S5_WIDTH, S5_WIDTH), S5_WIDTH ** -0.5)
    inp['s5_b_glu'] = nrm(ks[23], (N_EVEN, S5_WIDTH), 0.01)
    inp['w_out_even'] = nrm(ks[24], (N_EVEN, MLA_WIDTH + S5_WIDTH, D_MODEL), (MLA_WIDTH + S5_WIDTH) ** -0.5)
    inp['norm_odd'] = 1.0 + nrm(ks[25], (N_ODD, D_MODEL), 0.05)
    inp['w_in_odd'] = nrm(ks[26], (N_ODD, D_MODEL, ODD_IN), D_MODEL ** -0.5)
    inp['nsa_pe_k'] = nrm(ks[27], (N_ODD, NSA_BLOCK, d), 0.5)
    inp['nsa_pe_v'] = nrm(ks[28], (N_ODD, NSA_BLOCK, d), 0.5)
    inp['nsa_phi1_k'] = nrm(ks[29], (N_ODD, NSA_BLOCK * d, d), (NSA_BLOCK * d) ** -0.5)
    inp['nsa_phi2_k'] = nrm(ks[30], (N_ODD, d, d), d ** -0.5)
    inp['nsa_phi1_v'] = nrm(ks[31], (N_ODD, NSA_BLOCK * d, d), (NSA_BLOCK * d) ** -0.5)
    inp['nsa_phi2_v'] = nrm(ks[32], (N_ODD, d, d), d ** -0.5)
    inp['w_out_odd'] = nrm(ks[33], (N_ODD, NSA_WIDTH, D_MODEL), NSA_WIDTH ** -0.5)
    inp['norm_final'] = 1.0 + nrm(ks[34], (D_MODEL,), 0.05)
    return inp

def reference(x_prompt, x_sample, cache_mla, state_s5, cache_nsa_kv, state_nsa_win, page_table,
              norm_even, w_in_even, mla_g_q, mla_g_kv, mla_w_uq, mla_w_uk, mla_w_uv,
              s5_lambda_re, s5_lambda_im, s5_log_dt, s5_b_re, s5_b_im, s5_c_re, s5_c_im, s5_d,
              s5_w_glu, s5_b_glu, w_out_even,
              norm_odd, w_in_odd, nsa_pe_k, nsa_pe_v, nsa_phi1_k, nsa_phi2_k, nsa_phi1_v, nsa_phi2_v,
              w_out_odd, norm_final):
    pos_p = jnp.arange(x_prompt.shape[1], dtype=jnp.int32)
    pos_s = PAST_LEN + jnp.arange(x_sample.shape[1], dtype=jnp.int32)
    db = x_sample.shape[0]
    xp, xs = x_prompt, x_sample
    mla_p, mla_s, s5_p, s5_s, nsa_p, nsa_s, win_p, win_s = [], [], [], [], [], [], [], []
    for layer in range(DEPTH):
        li = layer // 2
        if layer % 2 == 0:
            w = (norm_even[li], w_in_even[li], mla_g_q[li], mla_g_kv[li], mla_w_uq[li], mla_w_uk[li],
                 mla_w_uv[li], s5_lambda_re[li], s5_lambda_im[li], s5_log_dt[li], s5_b_re[li], s5_b_im[li],
                 s5_c_re[li], s5_c_im[li], s5_d[li], s5_w_glu[li], s5_b_glu[li], w_out_even[li])
            xp, rows_p, st_p = even_mixer(xp, pos_p, w, None, None)
            mla_past = cache_mla[li, page_table].reshape(db, PAST_LEN, MLA_KV_LORA + MLA_ROPE)
            st = state_s5[li].astype(jnp.float32)
            h0 = lax.complex(st[..., 0], st[..., 1])
            xs, rows_s, st_s = even_mixer(xs, pos_s, w, mla_past, h0)
            mla_p.append(rows_p)
            mla_s.append(rows_s)
            s5_p.append(st_p)
            s5_s.append(st_s)
        else:
            w = (norm_odd[li], w_in_odd[li], nsa_pe_k[li], nsa_pe_v[li], nsa_phi1_k[li], nsa_phi2_k[li],
                 nsa_phi1_v[li], nsa_phi2_v[li], w_out_odd[li])
            xp, rows_p, wn_p = nsa_mixer(xp, pos_p, w, None)
            xs, rows_s, wn_s = nsa_mixer(xs, pos_s, w, (cache_nsa_kv, li, page_table, state_nsa_win[li]))
            nsa_p.append(rows_p)
            nsa_s.append(rows_s)
            win_p.append(wn_p)
            win_s.append(wn_s)
    y_prompt = rmsnorm(xp, norm_final)
    y_sample = rmsnorm(xs, norm_final)
    return (y_prompt, y_sample, jnp.stack(mla_p), jnp.stack(mla_s), jnp.stack(s5_p), jnp.stack(s5_s),
            jnp.stack(nsa_p), jnp.stack(nsa_s), jnp.stack(win_p), jnp.stack(win_s))


_drawn_inputs = setup_inputs


def setup_inputs(seed=0):
    import zlib

    import numpy as np

    out = dict(_drawn_inputs(seed))
    spreads = {}
    factors = {'cache_mla': 6.991,
     'mla_g_q': 8.0,
     's5_lambda_re': 15.798,
     's5_c_re': 17.191,
     's5_c_im': 16.898,
     's5_b_glu': 64.0,
     'nsa_pe_k': 25.337}
    for name, (base, spread) in spreads.items():
        noise = np.random.default_rng([zlib.crc32(name.encode()), seed]).standard_normal(out[name].shape)
        drawn = base * np.exp(spread * noise) if base else spread * noise
        out[name] = jnp.asarray(drawn.astype(out[name].dtype))
    for name, factor in factors.items():
        out[name] = (out[name] * factor).astype(out[name].dtype)
    return out
```

```python
from contextlib import ExitStack

import numpy as np

import concourse.bass as bass
import concourse.mybir as mybir

F32 = mybir.dt.float32
I32 = mybir.dt.int32
ALU = mybir.AluOpType
ACT = mybir.ActivationFunctionType
AX = mybir.AxisListType.X
ds = bass.ds

P = 128
D_MODEL, SEQ, DB, DT = 1024, 1024, 8, 4
NS = DB * DT
NTOK = SEQ + NS
NTILE = SEQ // P
KD = D_MODEL // P
PAST, PAGE = 8192, 128
NPAGE = PAST // PAGE
POOL = (DB * NPAGE * 5 + 3) // 4
EPS = 1e-6
NEG = -1e30

MH, NOPE, ROPE, MV = 8, 64, 32, 64
QL, KVL = 384, 256
ROW = KVL + ROPE
QD = NOPE + ROPE
MLA_SCALE = QD ** -0.5
LOW = QL + KVL + ROPE
MW, SW = MH * MV, 512
EVEN_IN = LOW + MW + 2 * SW

SG, SC, SN = 32, 16, 64
CH = 8
NCH = SEQ // CH
NPAIR = SG // 2

NH, NG, HD = 16, 2, 64
NR = NH // NG
NW = NH * HD
KVW = NG * HD
ODD_TOK = 6 * KVW + 3 * NH + NW
ODD_IN = NW + ODD_TOK
NSA_SCALE = HD ** -0.5
BLK, WIN = 64, 512
NBLK = PAST // BLK


class Chain:

    def __init__(self, engine, sem):
        self.engine, self.sem, self.n = engine, sem, 0

    def __call__(self, ins):
        self.n += 1
        ins.then_inc(self.sem, 1)
        self.engine.wait_ge(self.sem, self.n)


def next_iteration(nc, sems):
    for s in sems:
        nc.gpsimd.sem_clear(s)
    nc.all_engine_barrier()


def cleared(nc, ctx, name):
    sem = ctx.enter_context(nc.semaphore(name))
    ctx.callback(nc.gpsimd.sem_clear, sem)
    return sem


def load_constants(nc, a, c):
    with ExitStack() as ctx:
        ctx.callback(nc.all_engine_barrier)
        s_load = cleared(nc, ctx, "s_const")
        block = ctx.enter_context(nc.Block())

        @block.sync
        def _(sp):
            sp.dma_start(c["ident"][:], a["c_ident"]).then_inc(s_load, 16)
            sp.dma_start(c["causal"][:], a["c_causal"]).then_inc(s_load, 16)
            sp.dma_start(c["winlow"][:], a["c_winlow"]).then_inc(s_load, 16)
            sp.dma_start(c["pages"][:], a["page_table"].rearrange("b p -> (b p)").unsqueeze(0)).then_inc(s_load, 16)
            sp.wait_ge(s_load, 64)


def even_projection(nc, a, d, c, act_t):
    zaT, zbT, cqT, ckvT, krT = (act_t[k] for k in ("zaT", "zbT", "cqT", "ckvT", "krT"))
    with ExitStack() as ctx:
        ctx.callback(nc.all_engine_barrier)
        def sb(name, shape):
            return ctx.enter_context(nc.sbuf_tensor(name, shape, F32))

        w = sb("ev_w", [P, KD, EVEN_IN])
        g = sb("ev_g", [P, KD])
        gq = sb("ev_gq", [P, QL // P])
        gkv = sb("ev_gkv", [P, KVL])
        x = sb("ev_x", [P, D_MODEL])
        h = sb("ev_h", [P, D_MODEL])
        hT = sb("ev_hT", [P, KD, P])
        low = sb("ev_low", [P, LOW])
        cqn = sb("ev_cqn", [P, QL])
        rows = sb("ev_rows", [P, ROW])
        uS = sb("ev_uS", [P, 4, P])
        trig = sb("ev_trig", [P, 2, ROPE // 2])
        rt = sb("ev_rt", [P, 4, ROPE // 2])
        st = sb("ev_st", [P, 8])
        s_w = cleared(nc, ctx, "ev_s_w")
        names = ["x", "ss", "ms", "sd", "rs", "T", "hT", "tok", "fm", "low", "ss2", "cqn", "rows", "T2", "u", "out", "dv", "ac"]
        S = {n: cleared(nc, ctx, "ev_s_" + n) for n in names}
        bank = c["bank"]

        with nc.Block() as block:
            @block.sync
            def _(sp):
                for k in range(KD):
                    sp.dma_start(w[:, k, :], a["w_in_even"][0, k * P:(k + 1) * P, :]).then_inc(s_w, 16)
                sp.dma_start(g[:], a["norm_even"][0].rearrange("(k p) -> p k", p=P), allow_slow_non_contiguous=True).then_inc(s_w, 16)
                sp.dma_start(gq[:], a["mla_g_q"][0].rearrange("(k p) -> p k", p=P), allow_slow_non_contiguous=True).then_inc(s_w, 16)
                sp.dma_start(gkv[:], a["mla_g_kv"][0].partition_broadcast(P)).then_inc(s_w, 16)
                sp.wait_ge(s_w, 16 * (KD + 3))

        def tile(n, tok0, prompt, i):
            with nc.Block() as block:
                @block.sync
                def _(sp):
                    src = a["x_prompt"][0, ds(tok0, n), :] if prompt else a["x_sample"].rearrange("b t d -> (b t) d")
                    sp.dma_start(x[:n], src).then_inc(S["x"], 16)
                    sp.dma_start(trig[:n], a["c_rope"][ds(tok0, n)]).then_inc(S["x"], 16)
                    sp.wait_ge(S["rows"], 1)
                    dst = a["o_mla_rows_prompt"][0, 0, ds(tok0, n), :] if prompt else a["o_mla_rows_sample"][0].rearrange("b t r -> (b t) r")
                    sp.dma_start(dst, rows[:n]).then_inc(S["out"], 16)
                    sp.wait_ge(S["u"], 4)
                    for e in range(4):
                        if prompt:
                            dst = d["u"][ds(P * e, P), :, ds(i * (P // CH), P // CH)]
                            sp.dma_start(dst, uS[:, e, :].rearrange("p (j k) -> p j k", j=CH)).then_inc(S["out"], 16)
                        else:
                            sp.dma_start(d["us"][P * e:P * (e + 1)], uS[:, e, :n].rearrange("p (t b) -> p t b", t=DT)).then_inc(S["out"], 16)
                    sp.wait_ge(S["out"], 16 * 5)

                @block.scalar
                def _(act):
                    act.wait_ge(S["x"], 32)
                    nc.scalar.activation(h[:n], x[:n], ACT.Square, accum_out=st[:n, 0:1]).then_inc(S["ss"], 1)
                    act.wait_ge(S["ms"], 1)
                    nc.scalar.activation(st[:n, 2:3], st[:n, 1:2], ACT.Sqrt).then_inc(S["sd"], 1)
                    act.wait_ge(S["low"], 2)
                    nc.scalar.activation(cqn[:n], low[:n, 0:QL], ACT.Square, accum_out=st[:n, 4:5]).then_inc(S["ss2"], 1)
                    nc.scalar.activation(rows[:n, 0:KVL], low[:n, QL:QL + KVL], ACT.Square, accum_out=st[:n, 5:6]).then_inc(S["ss2"], 1)
                    act.wait_ge(S["ms"], 2)
                    nc.scalar.activation(st[:n, 4:6], st[:n, 6:8], ACT.Sqrt).then_inc(S["sd"], 1)
                    act.wait_ge(S["fm"], 3)
                    nc.scalar.activation(zaT[:, :, ds(tok0, n)], bank[:, 4, :4 * n].rearrange("p (e t) -> p e t", e=4), ACT.Silu).then_inc(S["ac"], 1)
                    nc.scalar.activation(zbT[:, :, ds(tok0, n)], bank[:, 6, :4 * n].rearrange("p (e t) -> p e t", e=4), ACT.Silu).then_inc(S["ac"], 1)

                @block.tensor
                def _(pe):
                    pe.wait_ge(S["rs"], 2)
                    for k in range(KD):
                        t = nc.tensor.transpose(bank[:, k // 4, (k % 4) * n:(k % 4 + 1) * n], h[:n, k * P:(k + 1) * P], c["ident"][:n, :n])
                    t.then_inc(S["T"], 1)
                    pe.wait_ge(S["hT"], 2)
                    for b, (lo, hi) in ((2, (0, 512)), (3, (512, LOW))):
                        for k in range(KD):
                            t = nc.tensor.matmul(bank[:n, b, 0:hi - lo], hT[:, k, :n], w[:, k, lo:hi], start=k == 0, stop=k == KD - 1)
                    t.then_inc(S["tok"], 1)
                    for part in range(3):
                        for e in range(4):
                            col = LOW + 512 * part + P * e
                            for k in range(KD):
                                t = nc.tensor.matmul(bank[:, 4 + part, e * n:(e + 1) * n], w[:, k, col:col + P], hT[:, k, :n], start=k == 0, stop=k == KD - 1)
                        t.then_inc(S["fm"], 1)
                    pe.wait_ge(S["cqn"], 1)
                    for k in range(QL // P):
                        t = nc.tensor.transpose(bank[:, 7, k * n:(k + 1) * n], cqn[:n, k * P:(k + 1) * P], c["ident"][:n, :n])
                    pe.wait_ge(S["rows"], 1)
                    for k in range(2):
                        t = nc.tensor.transpose(bank[:, 0, k * n:(k + 1) * n], rows[:n, k * P:(k + 1) * P], c["ident"][:n, :n])
                    t = nc.tensor.transpose(bank[:QD, 0, 2 * n:3 * n], rows[:n, ROW - QD:ROW], c["ident"][:n, :n])
                    t.then_inc(S["T2"], 1)

                @block.vector
                def _(dve):
                    link = Chain(dve, S["dv"])
                    dve.wait_ge(S["ss"], 1)
                    nc.vector.tensor_scalar(st[:n, 1:2], st[:n, 0:1], 1.0 / D_MODEL, EPS, ALU.mult, ALU.add).then_inc(S["ms"], 1)
                    dve.wait_ge(S["sd"], 1)
                    nc.vector.reciprocal(st[:n, 3:4], st[:n, 2:3]).then_inc(S["rs"], 1)
                    dve.wait_ge(S["rs"], 1)
                    nc.vector.tensor_scalar(h[:n], x[:n], st[:n, 3:4], None, ALU.mult).then_inc(S["rs"], 1)
                    dve.wait_ge(S["T"], 1)
                    for b in range(2):
                        nc.vector.tensor_tensor(hT[:, 4 * b:4 * b + 4, :n], bank[:, b, :4 * n].rearrange("p (k t) -> p k t", k=4),
                                                g[:, 4 * b:4 * b + 4].unsqueeze(2).broadcast_to((P, 4, n)), ALU.mult).then_inc(S["hT"], 1)
                    dve.wait_ge(S["tok"], 1)
                    nc.vector.tensor_copy(low[:n, 0:512], bank[:n, 2, :]).then_inc(S["low"], 1)
                    nc.vector.tensor_copy(low[:n, 512:LOW], bank[:n, 3, 0:LOW - 512]).then_inc(S["low"], 1)
                    dve.wait_ge(S["ss2"], 2)
                    link(nc.vector.tensor_scalar(st[:n, 6:7], st[:n, 4:5], 1.0 / QL, EPS, ALU.mult, ALU.add))
                    nc.vector.tensor_scalar(st[:n, 7:8], st[:n, 5:6], 1.0 / KVL, EPS, ALU.mult, ALU.add).then_inc(S["ms"], 1)
                    dve.wait_ge(S["low"], 2)
                    hr = ROPE // 2
                    x1, x2 = low[:n, QL + KVL:QL + KVL + hr], low[:n, QL + KVL + hr:LOW]
                    nc.vector.tensor_tensor(rt[:n, 0], x1, trig[:n, 0], ALU.mult)
                    nc.vector.tensor_tensor(rt[:n, 1], x2, trig[:n, 1], ALU.mult)
                    nc.vector.tensor_tensor(rt[:n, 2], x1, trig[:n, 1], ALU.mult)
                    link(nc.vector.tensor_tensor(rt[:n, 3], x2, trig[:n, 0], ALU.mult))
                    nc.vector.tensor_tensor(rows[:n, KVL:KVL + hr], rt[:n, 0], rt[:n, 1], ALU.subtract)
                    link(nc.vector.tensor_tensor(rows[:n, KVL + hr:ROW], rt[:n, 2], rt[:n, 3], ALU.add))
                    dve.wait_ge(S["sd"], 2)
                    link(nc.vector.reciprocal(st[:n, 6:8], st[:n, 4:6]))
                    nc.vector.tensor_scalar(cqn[:n], low[:n, 0:QL], st[:n, 6:7], None, ALU.mult).then_inc(S["cqn"], 1)
                    nc.vector.scalar_tensor_tensor(out=rows[:n, 0:KVL], in0=low[:n, QL:QL + KVL], scalar=st[:n, 7:8],
                                                   in1=gkv[:n], op0=ALU.mult, op1=ALU.mult).then_inc(S["rows"], 1)
                    dve.wait_ge(S["fm"], 2)
                    for e in range(4):
                        src = bank[:, 5, e * n:(e + 1) * n]
                        if prompt:
                            nc.vector.tensor_copy(uS[:, e, :].rearrange("p (j k) -> p j k", j=CH), src.rearrange("p (k j) -> p j k", j=CH)).then_inc(S["u"], 1)
                        else:
                            nc.vector.tensor_copy(uS[:, e, :n].rearrange("p (t b) -> p t b", t=DT), src.rearrange("p (b t) -> p t b", t=DT)).then_inc(S["u"], 1)
                    dve.wait_ge(S["T2"], 1)
                    nc.vector.tensor_tensor(cqT[:, :, ds(tok0, n)], bank[:, 7, :3 * n].rearrange("p (k t) -> p k t", k=3),
                                            gq[:].unsqueeze(2).broadcast_to((P, 3, n)), ALU.mult)
                    nc.vector.tensor_copy(ckvT[:, :, ds(tok0, n)], bank[:, 0, :2 * n].rearrange("p (k t) -> p k t", k=2))
                    link(nc.vector.tensor_copy(krT[NOPE:QD, ds(tok0, n)], bank[NOPE:QD, 0, 2 * n:3 * n]))

        with nc.Fori(0, NTILE) as i:
            tile(P, i * P, True, i)
            next_iteration(nc, S.values())
        tile(NS, SEQ, False, None)


def attention(nc, c, block, S, buf, units, qT, kdim):
    bank = c["bank"]
    p, pT, nmax, den, rden = (buf[k] for k in ("p", "pT", "nmax", "den", "rden"))
    n = len(units)

    def width(u):
        return units[u]["nblk"] * P

    def scores_ps(u):
        return bank[:, 2 * (u % 2):2 * (u % 2) + 2, :].rearrange("p a b -> p (a b)")

    pT_ps = bank[:, 4:6, :].rearrange("p a b -> p (a b)")

    def o_ps(u):
        return bank[:, 6, (u % 2) * HD:(u % 2 + 1) * HD]

    @block.tensor
    def _(pe):
        def scores(u):
            unit = units[u]
            pe.wait_ge(S["qk"], buf["qk_ready"])
            if u >= 2:
                pe.wait_ge(S["exp"], u - 1)
            w = width(u)
            for lo in range(0, w, 512):
                hi = min(w, lo + 512)
                t = nc.tensor.matmul(scores_ps(u)[:, lo:hi], qT[:kdim, unit["q0"]:unit["q0"] + P], unit["kT"][:, lo:hi], start=True, stop=True)
            t.then_inc(S["sc"], 1)

        def values(u):
            unit = units[u]
            pe.wait_ge(S["exp"], u + 1)
            if u >= 1:
                pe.wait_ge(S["pT"], u)
            for b in range(unit["nblk"]):
                t = nc.tensor.transpose(pT_ps[:, b * P:(b + 1) * P], p[:, u % 2, b * P:(b + 1) * P], c["ident"][:])
            t.then_inc(S["tr"], 1)

        def weighted(u):
            unit = units[u]
            pe.wait_ge(S["pT"], u + 1)
            if u >= 2:
                pe.wait_ge(S["o"], u - 1)
            for b in range(unit["nblk"]):
                t = nc.tensor.matmul(o_ps(u), pT[:, u % 2, b * P:(b + 1) * P], unit["v"](b), start=b == 0, stop=b == unit["nblk"] - 1)
            t.then_inc(S["pv"], 1)

        buf["pe_before"](pe)
        scores(0)
        for u in range(n):
            if u + 1 < n:
                scores(u + 1)
            values(u)
            if u >= 1:
                weighted(u - 1)
        weighted(n - 1)

    @block.scalar
    def _(act):
        if "act_before" in buf:
            buf["act_before"](act)
        for u in range(n):
            act.wait_ge(S["mx"], u + 1)
            if u >= 2:
                act.wait_ge(S["tr"], u - 1)
                act.wait_ge(S["rd"], u - 1)
            nc.scalar.activation(p[:, u % 2, :width(u)], scores_ps(u)[:, :width(u)], ACT.Exp, bias=nmax[:, u % 2:u % 2 + 1],
                                 accum_out=den[:, u % 2:u % 2 + 1]).then_inc(S["exp"], 1)

    @block.vector
    def _(dve):
        link = Chain(dve, S["dv"])

        def maximum(u):
            dve.wait_ge(S["sc"], u + 1)
            for lo, m in units[u]["masks"]:
                link(nc.vector.tensor_tensor(scores_ps(u)[:, lo:lo + P], scores_ps(u)[:, lo:lo + P], m, ALU.add))
            nc.vector.tensor_reduce(nmax[:, u % 2:u % 2 + 1], scores_ps(u)[:, :width(u)], AX, ALU.max, negate=True).then_inc(S["mx"], 1)

        def turned(u):
            dve.wait_ge(S["exp"], u + 1)
            nc.vector.reciprocal(rden[:, u % 2:u % 2 + 1], den[:, u % 2:u % 2 + 1]).then_inc(S["rd"], 1)
            dve.wait_ge(S["tr"], u + 1)
            if u >= 2:
                dve.wait_ge(S["pv"], u - 1)
            nc.vector.tensor_copy(pT[:, u % 2, :width(u)], pT_ps[:, :width(u)]).then_inc(S["pT"], 1)

        def out(u):
            dve.wait_ge(S["pv"], u + 1)
            dve.wait_ge(S["rd"], u + 1)
            units[u]["finish"](o_ps(u), rden[:, u % 2:u % 2 + 1], link).then_inc(S["o"], 1)

        buf["dve_before"](dve, link)
        maximum(0)
        for u in range(n):
            if u + 1 < n:
                maximum(u + 1)
            if u >= 1:
                out(u - 1)
            turned(u)
        out(n - 1)
        dve.wait_ge(S["o"], n)


ATT_SEMS = ["qk", "sc", "mx", "exp", "tr", "rd", "pT", "pv", "o", "dv"]


def mla_prompt(nc, a, d, c, act_t):
    cqT, ckvT, krT, oa, qlat, qrope = (act_t[k] for k in ("cqT", "ckvT", "krT", "oa", "qlat", "qrope"))
    bank = c["bank"]
    with ExitStack() as ctx:
        ctx.callback(nc.all_engine_barrier)
        def sb(name, shape):
            return ctx.enter_context(nc.sbuf_tensor(name, shape, F32))

        cosT = sb("mp_cos", [P, NTOK])
        sinT = sb("mp_sin", [P, NTOK])
        rt = sb("mp_rt", [P, 2, 512])
        wq = sb("mp_wq", [P, 3, QD + ROPE])
        wk = sb("mp_wk", [P, 2, NOPE])
        wkT = sb("mp_wkT", [NOPE, 2, P])
        wv = sb("mp_wv", [P, 2, MV])
        qT = sb("mp_qT", [P, NTOK])
        v = sb("mp_v", [P, NTILE, MV])
        buf = {"p": sb("mp_p", [P, 2, SEQ]), "pT": sb("mp_pT", [P, 2, SEQ]), "nmax": sb("mp_nmax", [P, 2]),
               "den": sb("mp_den", [P, 2]), "rden": sb("mp_rden", [P, 2])}
        S = {n: cleared(nc, ctx, "mp_s_" + n) for n in ["tab", "w", "pre", "ev"] + ATT_SEMS}
        half = ROPE // 2

        with nc.Block() as block:
            @block.sync
            def _(sp):
                sp.dma_start(cosT[NOPE:QD], a["c_rope_cosT"]).then_inc(S["tab"], 16)
                sp.dma_start(sinT[NOPE:QD], a["c_rope_sinT"]).then_inc(S["tab"], 16)
                sp.wait_ge(S["tab"], 32)

        with nc.Fori(0, MH) as h:
            with nc.Block() as block:
                @block.sync
                def _(sp):
                    uq = a["mla_w_uq"][0].rearrange("(k p) h e -> p k h e", p=P)
                    sp.dma_start(wq[:, :, 0:QD], uq[:, :, ds(h, 1), :].rearrange("p k h e -> p k (h e)")).then_inc(S["w"], 16)
                    for lo, src in ((QD, NOPE + half), (QD + half, NOPE)):
                        sp.dma_start(wq[:, :, lo:lo + half], uq[:, :, ds(h, 1), src:src + half].rearrange("p k h e -> p k (h e)")).then_inc(S["w"], 16)
                    for dst, src in ((wk, a["mla_w_uk"]), (wv, a["mla_w_uv"])):
                        sp.dma_start(dst[:], src[0].rearrange("(k p) h e -> p k h e", p=P)[:, :, ds(h, 1), :].rearrange("p k h e -> p k (h e)")).then_inc(S["w"], 16)

                parts = ((0, 512), (512, 512), (SEQ, NS))

                def pe_before(pe):
                    pe.wait_ge(S["w"], 80)
                    for j, (t0, n) in enumerate(parts):
                        for k in range(3):
                            nc.tensor.matmul(bank[:QD, 2 * j, :n], wq[:, k, 0:QD], cqT[:, k, t0:t0 + n], start=k == 0, stop=k == 2)
                        for k in range(3):
                            t = nc.tensor.matmul(bank[NOPE:QD, 2 * j + 1, :n], wq[:, k, QD:QD + ROPE], cqT[:, k, t0:t0 + n], start=k == 0, stop=k == 2)
                        t.then_inc(S["pre"], 1)
                    for i in range(NTILE):
                        for k in range(2):
                            t = nc.tensor.matmul(bank[:, 6, i * MV:(i + 1) * MV], ckvT[:, k, i * P:(i + 1) * P], wv[:, k, :], start=k == 0, stop=k == 1)
                    for k in range(2):
                        t = nc.tensor.transpose(bank[:NOPE, 7, k * P:(k + 1) * P], wk[:, k, :], c["ident"][:])
                    t.then_inc(S["pre"], 1)
                    pe.wait_ge(S["ev"], 2)
                    for j in range(2):
                        for k in range(2):
                            t = nc.tensor.matmul(bank[:NOPE, 2 * j, :], wk[:, k, :], ckvT[:, k, j * 512:(j + 1) * 512], start=k == 0, stop=k == 1)
                        t.then_inc(S["pre"], 1)
                    pe.wait_ge(S["ev"], 5)
                    for k in range(2):
                        t = nc.tensor.matmul(bank[:, 4, k * NS:(k + 1) * NS], wkT[:, k, :], qT[:NOPE, SEQ:NTOK], start=True, stop=True)
                    t.then_inc(S["pre"], 1)

                def dve_before(dve, link):
                    for j, (t0, n) in enumerate(parts):
                        dve.wait_ge(S["pre"], j + 1)
                        nc.vector.tensor_scalar(qT[:NOPE, t0:t0 + n], bank[:NOPE, 2 * j, :n], MLA_SCALE, None, ALU.mult)
                        nc.vector.scalar_tensor_tensor(out=rt[NOPE:QD, 0, :n], in0=bank[NOPE:QD, 2 * j, :n], scalar=MLA_SCALE,
                                                       in1=cosT[NOPE:QD, t0:t0 + n], op0=ALU.mult, op1=ALU.mult)
                        link(nc.vector.scalar_tensor_tensor(out=rt[NOPE:QD, 1, :n], in0=bank[NOPE:QD, 2 * j + 1, :n], scalar=MLA_SCALE,
                                                            in1=sinT[NOPE:QD, t0:t0 + n], op0=ALU.mult, op1=ALU.mult))
                        nc.vector.tensor_tensor(qT[NOPE:QD, t0:t0 + n], rt[NOPE:QD, 0, :n], rt[NOPE:QD, 1, :n], ALU.add).then_inc(S["ev"], 1)
                        dve.wait_ge(S["ev"], j + 1)
                    dve.wait_ge(S["pre"], 4)
                    nc.vector.tensor_copy(v[:].rearrange("p i e -> p (i e)"), bank[:, 6, :]).then_inc(S["ev"], 1)
                    nc.vector.tensor_copy(wkT[:].rearrange("p k e -> p (k e)"), bank[:NOPE, 7, 0:2 * P]).then_inc(S["ev"], 1)
                    for j in range(2):
                        dve.wait_ge(S["pre"], 5 + j)
                        nc.vector.tensor_copy(krT[:NOPE, j * 512:(j + 1) * 512], bank[:NOPE, 2 * j, :]).then_inc(S["qk"], 1)
                    dve.wait_ge(S["pre"], 7)
                    link(nc.vector.tensor_copy(qlat[:, :, ds(h, 1), :].rearrange("p k h t -> p k (h t)"), bank[:, 4, 0:2 * NS].rearrange("p (k t) -> p k t", k=2)))
                    nc.vector.tensor_copy(qrope[NOPE:QD, ds(h, 1), :].rearrange("p h t -> p (h t)"), qT[NOPE:QD, SEQ:NTOK]).then_inc(S["qk"], 1)

                def finish(i):
                    def f(o, r, link):
                        return nc.vector.tensor_scalar(oa[:, i, ds(h * MV, MV)], o, r, None, ALU.mult)
                    return f

                units = [{"q0": i * P, "nblk": i + 1, "kT": krT[:QD, :], "v": (lambda b: v[:, b, :]),
                          "masks": [(i * P, c["causal"][:])], "finish": finish(i)} for i in range(NTILE)]
                buf.update(pe_before=pe_before, dve_before=dve_before, qk_ready=3)
                attention(nc, c, block, S, buf, units, qT, QD)
            next_iteration(nc, [s for n, s in S.items() if n != "tab"])


def mla_sample(nc, a, d, c, act_t):
    ckvT, krT, oa, qlat, qrope = (act_t[k] for k in ("ckvT", "krT", "oa", "qlat", "qrope"))
    bank = c["bank"]
    NQ = MH * DT
    GP = 4
    NG4 = NPAGE // GP
    with ExitStack() as ctx:
        ctx.callback(nc.all_engine_barrier)
        def sb(name, shape):
            return ctx.enter_context(nc.sbuf_tensor(name, shape, F32))

        pg = sb("ms_pg", [P, NPAGE, ROW])
        kT = sb("ms_kT", [P, 2, 2, GP * P])
        rT = sb("ms_rT", [P, 2, GP * P])
        s = sb("ms_s", [NQ, PAST])
        sn = sb("ms_sn", [NQ, DT])
        mask = sb("ms_mask", [NQ, DT])
        q = sb("ms_q", [P, 2, NQ])
        qr = sb("ms_qr", [P, NQ])
        knew = sb("ms_knew", [P, DT])
        new = sb("ms_new", [DT, ROW])
        gmax = sb("ms_gmax", [NQ, NG4 + 1])
        nmax = sb("ms_nmax", [NQ, 1])
        gden = sb("ms_gden", [NQ, NG4 + 1])
        den = sb("ms_den", [NQ, 2])
        pT = sb("ms_pT", [P, 2, 512])
        pnT = sb("ms_pnT", [DT, NQ])
        ol = sb("ms_ol", [NQ, KVL])
        olT = sb("ms_olT", [P, 2, MH, DB, DT])
        s_w = cleared(nc, ctx, "ms_s_w")
        s_page = cleared(nc, ctx, "ms_s_page")
        names = ["new", "q", "tr", "kT", "kR", "sc", "s", "mx", "exp", "pt", "pT", "pv", "ol", "olt", "dv", "done"]
        S = {n: cleared(nc, ctx, "ms_s_" + n) for n in names}
        s_group = [cleared(nc, ctx, f"ms_s_group{i}") for i in range(NG4)]

        def load_group(sp, b, gi):
            for j in range(GP):
                page = sp.value_load(c["pages"][0:1, ds(b * NPAGE + GP * gi + j, 1)], min_val=0, max_val=POOL - 1)
                sp.dma_start(pg[:, GP * gi + j, :], a["cache_mla"][0, ds(page, 1)].rearrange("a p r -> (a p) r")).then_inc(s_group[gi], 16)

        with nc.Block() as block:
            @block.sync
            def _(sp):
                sp.dma_start(mask[:], a["c_mla_new"]).then_inc(s_w, 16)
                sp.wait_ge(s_w, 16)
                for gi in range(NG4):
                    load_group(sp, 0, gi)

        with nc.Fori(0, DB) as b:
            with nc.Block() as block:
                @block.sync
                def _(sp):
                    sp.dma_start(new[:], a["o_mla_rows_sample"][0, ds(b, 1)].rearrange("b t r -> (b t) r")).then_inc(S["new"], 16)
                    nxt = sp.snap((b + 1) % DB)
                    for gi in range(NG4):
                        sp.wait_ge(S["pv"], gi + 1)
                        sp.sem_clear(s_group[gi])
                        load_group(sp, nxt, gi)

                @block.scalar
                def _(act):
                    for gi in range(NG4):
                        act.wait_ge(S["tr"], gi + 1)
                        if gi >= 2:
                            act.wait_ge(S["sc"], gi - 1)
                        nc.scalar.activation(rT[NOPE:QD, gi % 2, :], bank[NOPE:QD, 3 * (gi % 2) + 2, :], ACT.Copy).then_inc(S["kR"], 1)
                        if gi >= 1:
                            act.wait_ge(S["sc"], gi)
                            nc.scalar.activation(s[:, (gi - 1) * 512:gi * 512], bank[:NQ, 6 + (gi - 1) % 2, :], ACT.Copy).then_inc(S["s"], 1)
                    act.wait_ge(S["sc"], NG4)
                    nc.scalar.activation(s[:, (NG4 - 1) * 512:], bank[:NQ, 6 + (NG4 - 1) % 2, :], ACT.Copy).then_inc(S["s"], 1)
                    act.wait_ge(S["mx"], NG4 + 2)
                    act.wait_ge(S["s"], NG4)
                    nc.scalar.activation(sn[:], sn[:], ACT.Exp, bias=nmax[:], accum_out=gden[:, NG4:NG4 + 1]).then_inc(S["exp"], 1)
                    for gi in range(NG4):
                        nc.scalar.activation(s[:, gi * 512:(gi + 1) * 512], s[:, gi * 512:(gi + 1) * 512], ACT.Exp, bias=nmax[:],
                                             accum_out=gden[:, gi:gi + 1]).then_inc(S["exp"], 1)

                @block.tensor
                def _(pe):
                    def turn(gi):
                        pe.wait_ge(s_group[gi], 16 * GP)
                        if gi >= 2:
                            pe.wait_ge(S["kT"], 2 * (gi - 1))
                            pe.wait_ge(S["kR"], gi - 1)
                        for j in range(GP):
                            for k in range(2):
                                nc.tensor.transpose(bank[:, 3 * (gi % 2) + k, j * P:(j + 1) * P], pg[:, GP * gi + j, k * P:(k + 1) * P], c["ident"][:])
                            t = nc.tensor.transpose(bank[:QD, 3 * (gi % 2) + 2, j * P:(j + 1) * P], pg[:, GP * gi + j, ROW - QD:ROW], c["ident"][:])
                        t.then_inc(S["tr"], 1)

                    def score(gi):
                        pe.wait_ge(S["kT"], 2 * (gi + 1))
                        pe.wait_ge(S["kR"], gi + 1)
                        if gi >= 2:
                            pe.wait_ge(S["s"], gi - 1)
                        o = bank[:NQ, 6 + gi % 2, :]
                        for k in range(2):
                            nc.tensor.matmul(o, q[:, k, :], kT[:, gi % 2, k, :], start=k == 0, stop=False)
                        nc.tensor.matmul(o, qr[NOPE:QD, :], rT[NOPE:QD, gi % 2, :], start=False, stop=True).then_inc(S["sc"], 1)

                    turn(0)
                    pe.wait_ge(S["q"], 1)
                    for gi in range(NG4):
                        if gi + 1 < NG4:
                            turn(gi + 1)
                        score(gi)
                    pe.wait_ge(S["kT"], 2 * NG4)
                    o = bank[:NQ, 0, 0:DT]
                    for k in range(2):
                        nc.tensor.matmul(o, q[:, k, :], ckvT[:, k, ds(SEQ + b * DT, DT)], start=k == 0, stop=False)
                    nc.tensor.matmul(o, qr[NOPE:QD, :], knew[NOPE:QD, :], start=False, stop=True).then_inc(S["sc"], 1)

                    def probs(gi):
                        pe.wait_ge(S["exp"], gi + 2)
                        if gi >= 2:
                            pe.wait_ge(S["pT"], gi - 1)
                        for j in range(GP):
                            t = nc.tensor.transpose(bank[:, 1 + gi % 2, j * NQ:(j + 1) * NQ], s[:, (GP * gi + j) * P:(GP * gi + j + 1) * P], c["ident"][:NQ, :NQ])
                        t.then_inc(S["pt"], 1)

                    pe.wait_ge(S["exp"], 1)
                    nc.tensor.transpose(bank[:DT, 3, 0:NQ], sn[:], c["ident"][:NQ, :NQ]).then_inc(S["pt"], 1)
                    probs(0)
                    for gi in range(NG4):
                        if gi + 1 < NG4:
                            probs(gi + 1)
                        pe.wait_ge(S["pT"], gi + 2)
                        if gi == 0:
                            pe.wait_ge(S["new"], 16)
                            nc.tensor.matmul(bank[:NQ, 4, 0:KVL], pnT[:], new[:, 0:KVL], start=True, stop=False)
                        for j in range(GP):
                            t = nc.tensor.matmul(bank[:NQ, 4, 0:KVL], pT[:, gi % 2, j * NQ:(j + 1) * NQ], pg[:, GP * gi + j, 0:KVL],
                                                 start=False, stop=gi == NG4 - 1 and j == GP - 1)
                        t.then_inc(S["pv"], 1)
                    pe.wait_ge(S["ol"], 1)
                    for k in range(2):
                        t = nc.tensor.transpose(bank[:, 5, k * NQ:(k + 1) * NQ], ol[:, k * P:(k + 1) * P], c["ident"][:NQ, :NQ])
                    t.then_inc(S["olt"], 1)

                @block.vector
                def _(dve):
                    link = Chain(dve, S["dv"])
                    for k in range(2):
                        nc.vector.tensor_copy(q[:, k, :].rearrange("p (h t) -> p h t", t=DT), qlat[:, k, :, ds(b * DT, DT)])
                    nc.vector.tensor_copy(knew[NOPE:QD, :], krT[NOPE:QD, ds(SEQ + b * DT, DT)])
                    nc.vector.tensor_copy(qr[NOPE:QD, :].rearrange("p (h t) -> p h t", t=DT), qrope[NOPE:QD, :, ds(b * DT, DT)]).then_inc(S["q"], 1)
                    for gi in range(NG4):
                        dve.wait_ge(S["tr"], gi + 1)
                        if gi >= 2:
                            dve.wait_ge(S["sc"], gi - 1)
                        for k in range(2):
                            nc.vector.tensor_copy(kT[:, gi % 2, k, :], bank[:, 3 * (gi % 2) + k, :]).then_inc(S["kT"], 1)
                        if gi >= 1:
                            dve.wait_ge(S["s"], gi)
                            nc.vector.tensor_reduce(gmax[:, gi - 1:gi], s[:, (gi - 1) * 512:gi * 512], AX, ALU.max).then_inc(S["mx"], 1)
                    dve.wait_ge(S["s"], NG4)
                    nc.vector.tensor_reduce(gmax[:, NG4 - 1:NG4], s[:, (NG4 - 1) * 512:NG4 * 512], AX, ALU.max).then_inc(S["mx"], 1)
                    dve.wait_ge(S["sc"], NG4 + 1)
                    link(nc.vector.tensor_tensor(sn[:], bank[:NQ, 0, 0:DT], mask[:], ALU.add))
                    nc.vector.tensor_reduce(gmax[:, NG4:NG4 + 1], sn[:], AX, ALU.max).then_inc(S["mx"], 1)
                    dve.wait_ge(S["mx"], NG4 + 1)
                    nc.vector.tensor_reduce(nmax[:], gmax[:], AX, ALU.max, negate=True).then_inc(S["mx"], 1)
                    dve.wait_ge(S["pt"], 1)
                    nc.vector.tensor_copy(pnT[:], bank[:DT, 3, 0:NQ]).then_inc(S["pT"], 1)
                    for gi in range(NG4):
                        dve.wait_ge(S["pt"], gi + 2)
                        if gi >= 2:
                            dve.wait_ge(S["pv"], gi - 1)
                        nc.vector.tensor_copy(pT[:, gi % 2, 0:GP * NQ], bank[:, 1 + gi % 2, 0:GP * NQ]).then_inc(S["pT"], 1)
                    dve.wait_ge(S["exp"], NG4 + 1)
                    link(nc.vector.tensor_reduce(den[:, 0:1], gden[:], AX, ALU.add))
                    link(nc.vector.reciprocal(den[:, 1:2], den[:, 0:1]))
                    dve.wait_ge(S["pv"], NG4)
                    nc.vector.tensor_scalar(ol[:], bank[:NQ, 4, 0:KVL], den[:, 1:2], None, ALU.mult).then_inc(S["ol"], 1)
                    dve.wait_ge(S["olt"], 1)
                    for k in range(2):
                        link(nc.vector.tensor_copy(olT[:, k, :, ds(b, 1), :].rearrange("p h b t -> p h (b t)"),
                                                   bank[:, 5, k * NQ:(k + 1) * NQ].rearrange("p (h t) -> p h t", h=MH)))
            next_iteration(nc, S.values())

        wv = [pg[:, 2 * k:2 * k + 2, :].rearrange("p j r -> p (j r)")[:, 0:MW] for k in range(2)]
        with nc.Block() as block:
            @block.sync
            def _(sp):
                for gi in range(NG4):
                    sp.wait_ge(s_group[gi], 16 * GP)
                for k in range(2):
                    sp.dma_start(wv[k], a["mla_w_uv"][0, k * P:(k + 1) * P].rearrange("p h e -> p (h e)")).then_inc(s_w, 16)

            @block.tensor
            def _(pe):
                pe.wait_ge(s_w, 48)
                for h in range(MH):
                    for k in range(2):
                        t = nc.tensor.matmul(bank[:NS, 0, h * MV:(h + 1) * MV], olT[:, k, h].rearrange("p b t -> p (b t)"), wv[k][:, h * MV:(h + 1) * MV],
                                             start=k == 0, stop=k == 1)
                t.then_inc(S["pv"], 1)

            @block.vector
            def _(dve):
                dve.wait_ge(S["pv"], 1)
                nc.vector.tensor_copy(oa[:NS, NTILE, :], bank[:NS, 0, :]).then_inc(S["done"], 1)
                dve.wait_ge(S["done"], 1)


def s5_matrices(nc, a, d, c, m):
    bank = c["bank"]
    with ExitStack() as ctx:
        ctx.callback(nc.all_engine_barrier)
        def sb(name, shape):
            return ctx.enter_context(nc.sbuf_tensor(name, shape, F32))

        lam = sb("sm_lam", [P, 2, NPAIR])
        ldt = sb("sm_ldt", [P, NPAIR])
        b_in = sb("sm_b", [P, 2, NPAIR, SC])
        c_in = sb("sm_c", [P, 2, 2, P])
        cT = sb("sm_cT", [P, 2, NPAIR, SC])
        dskip = sb("sm_d", [SC, SG])
        w = sb("sm_w", [P, 12, NPAIR])
        pw = sb("sm_pw", [P, 2, CH + 1, NPAIR])
        pr = sb("sm_pr", [P, 2, CH, NPAIR])
        bb = sb("sm_bb", [P, 2, NPAIR, SC])
        t1 = sb("sm_t1", [P, NPAIR, CH + 1, SC])
        t2 = sb("sm_t2", [P, NPAIR, CH + 1, SC])
        xb = sb("sm_xb", [P, 2, NPAIR, CH, SC])
        kern = sb("sm_kern", [SC, SG, P])
        s_ld = cleared(nc, ctx, "sm_s_ld")
        s_dv = cleared(nc, ctx, "sm_s_dv")
        s_cT = cleared(nc, ctx, "sm_s_cT")
        s_act = cleared(nc, ctx, "sm_s_act")
        s_arg = cleared(nc, ctx, "sm_s_arg")
        s_xb = cleared(nc, ctx, "sm_s_xb")
        s_out = cleared(nc, ctx, "sm_s_out")
        s_tb = cleared(nc, ctx, "sm_s_tb")
        s_te = cleared(nc, ctx, "sm_s_te")
        s_k = cleared(nc, ctx, "sm_s_k")
        s_ke = cleared(nc, ctx, "sm_s_ke")
        s_kern = cleared(nc, ctx, "sm_s_kern")
        s_zero = cleared(nc, ctx, "sm_s_zero")
        s_toep = cleared(nc, ctx, "sm_s_toep")
        out, binT, toep = m["out"], m["binT"], m["toep"]
        NLOAD = 3 * 2 + 2 * 2 + 2 * NPAIR + 1

        with nc.Block() as block:
            @block.sync
            def _(sp):
                for r in range(2):
                    rows = slice(r * SN, (r + 1) * SN)
                    for i, key in enumerate(("s5_lambda_re", "s5_lambda_im")):
                        sp.dma_start(lam[rows, i], a[key][0].rearrange("(k r) n -> r n k", r=2)[r], allow_slow_non_contiguous=True).then_inc(s_ld, 16)
                    sp.dma_start(ldt[rows], a["s5_log_dt"][0].rearrange("(k r) -> r k", r=2)[r].partition_broadcast(SN), allow_slow_non_contiguous=True).then_inc(s_ld, 16)
                    for i, key in enumerate(("s5_b_re", "s5_b_im")):
                        sp.dma_start(b_in[rows, i], a[key][0].rearrange("(k r) n q -> r n k q", r=2)[r]).then_inc(s_ld, 16)
                for i, key in enumerate(("s5_c_re", "s5_c_im")):
                    for k in range(NPAIR):
                        sp.dma_start(c_in[SC * (k % 8):SC * (k % 8 + 1), i, k // 8, :].rearrange("p (r n) -> p r n", r=2),
                                     a[key][0, 2 * k:2 * k + 2].rearrange("r p n -> p r n")).then_inc(s_ld, 16)
                sp.dma_start(dskip[:], a["s5_d"][0].rearrange("g p -> p g"), allow_slow_non_contiguous=True).then_inc(s_ld, 16)
                sp.wait_ge(s_kern, 1)
                sp.wait_ge(s_zero, 1)
                for j in range(CH):
                    sp.dma_start(toep[SC * j:SC * (j + 1), :, SC * j:P], kern[:, :, 0:P - SC * j]).then_inc(s_toep, 16)
                sp.wait_ge(s_toep, 16 * CH)

            @block.gpsimd
            def _(pool):
                nc.gpsimd.memset(toep[:], 0.0).then_inc(s_zero, 1)

            @block.scalar
            def _(act):
                act.wait_ge(s_ld, 16 * NLOAD)
                nc.scalar.activation(w[:, 0], ldt[:], ACT.Exp).then_inc(s_act, 1)
                act.wait_ge(s_arg, 1)
                nc.scalar.activation(w[:, 2], w[:, 1], ACT.Exp).then_inc(s_act, 1)
                act.wait_ge(s_arg, 2)
                nc.scalar.activation(m["rot"][:, 1], w[:, 4], ACT.Sin).then_inc(s_act, 1)
                nc.scalar.activation(w[:, 5], w[:, 4], ACT.Sin, scale=0.5).then_inc(s_act, 1)

            @block.tensor
            def _(pe):
                pe.wait_ge(s_ld, 16 * NLOAD)
                for i in range(2):
                    for hf in range(2):
                        t = nc.tensor.transpose(bank[:, 0, (2 * i + hf) * P:(2 * i + hf + 1) * P], c_in[:, i, hf, :], c["ident"][:])
                t.then_inc(s_cT, 1)
                pe.wait_ge(s_xb, 2)
                for i in range(2):
                    for k in range(NPAIR):
                        t = nc.tensor.transpose(bank[:, 4 * i + k // 4, (k % 4) * P:(k % 4 + 1) * P], xb[:, i, k].rearrange("p j q -> p (j q)"), c["ident"][:])
                        if k % 4 == 3:
                            t.then_inc(s_tb, 1)
                pe.wait_ge(s_out, 2)
                pe.wait_ge(s_te, 8)
                for r in range(2):
                    rows = slice(r * SN, (r + 1) * SN)
                    for k in range(NPAIR):
                        for i in range(2):
                            t = nc.tensor.matmul(bank[:SC, 4 * r + k // 4, (k % 4) * P:(k % 4 + 1) * P], bb[rows, i, k, :],
                                                 out[rows, i, k, 0:CH, :].rearrange("p t q -> p (t q)"), start=i == 0, stop=i == 1)
                        if k % 4 == 3:
                            t.then_inc(s_k, 1)

            @block.vector
            def _(dve):
                link = Chain(dve, s_dv)
                V = nc.vector

                def cmul(o_re, o_im, a_re, a_im, b_re, b_im, u1, u2):
                    link(V.tensor_tensor(u1, a_re, b_re, ALU.mult))
                    link(V.tensor_tensor(u2, a_im, b_im, ALU.mult))
                    link(V.tensor_tensor(o_re, u1, u2, ALU.subtract))
                    link(V.tensor_tensor(u1, a_re, b_im, ALU.mult))
                    link(V.tensor_tensor(u2, a_im, b_re, ALU.mult))
                    link(V.tensor_tensor(o_im, u1, u2, ALU.add))

                dve.wait_ge(s_act, 1)
                V.tensor_tensor(w[:, 1], lam[:, 0], w[:, 0], ALU.mult).then_inc(s_arg, 1)
                turn = 6.283185307179586
                hi = 6.28125
                magic = 12582912.0
                link(V.tensor_tensor(w[:, 3], lam[:, 1], w[:, 0], ALU.mult))
                link(V.tensor_scalar(w[:, 6], w[:, 3], 1.0 / turn, None, ALU.mult))
                link(V.tensor_scalar(w[:, 6], w[:, 6], magic, magic, ALU.add, ALU.subtract))
                link(V.scalar_tensor_tensor(out=w[:, 3], in0=w[:, 6], scalar=-hi, in1=w[:, 3], op0=ALU.mult, op1=ALU.add))
                link(V.scalar_tensor_tensor(out=w[:, 3], in0=w[:, 6], scalar=-(turn - hi), in1=w[:, 3], op0=ALU.mult, op1=ALU.add))
                V.tensor_scalar(w[:, 4], w[:, 3], 3.1415925, -3.1415925, ALU.min, ALU.max).then_inc(s_arg, 1)
                dve.wait_ge(s_act, 4)
                link(V.tensor_tensor(w[:, 6], w[:, 5], w[:, 5], ALU.mult))
                link(V.tensor_scalar(m["rot"][:, 0], w[:, 6], -2.0, 1.0, ALU.mult, ALU.add))
                link(V.memset(pw[:, 0, 0], 1.0))
                link(V.memset(pw[:, 1, 0], 0.0))
                for i in range(2):
                    link(V.tensor_tensor(pw[:, i, 1], m["rot"][:, i], w[:, 2], ALU.mult))
                n = 1
                while n < CH:
                    cmul(pw[:, 0, n + 1:2 * n + 1], pw[:, 1, n + 1:2 * n + 1], pw[:, 0, 1:n + 1], pw[:, 1, 1:n + 1],
                         pw[:, 0, n:n + 1].broadcast_to((P, n, NPAIR)), pw[:, 1, n:n + 1].broadcast_to((P, n, NPAIR)),
                         t1[:, 0:n, 0, :], t2[:, 0:n, 0, :])
                    n *= 2
                for i in range(2):
                    link(V.tensor_copy(m["l4"][:, i], pw[:, i, DT]))
                    for j in range(CH):
                        link(V.tensor_copy(pr[:, i, j], pw[:, i, CH - 1 - j]))
                link(V.tensor_tensor(w[:, 7], w[:, 2], w[:, 2], ALU.mult))
                link(V.tensor_tensor(w[:, 8], w[:, 7], w[:, 7], ALU.mult))
                link(V.tensor_tensor(m["l8"][:], w[:, 8], w[:, 8], ALU.mult))
                link(V.tensor_tensor(w[:, 5], lam[:, 0], lam[:, 0], ALU.mult))
                link(V.tensor_tensor(w[:, 6], lam[:, 1], lam[:, 1], ALU.mult))
                link(V.tensor_tensor(w[:, 5], w[:, 5], w[:, 6], ALU.add))
                link(V.reciprocal(w[:, 7], w[:, 5]))
                link(V.tensor_scalar(w[:, 8], pw[:, 0, 1], -1.0, None, ALU.add))
                link(V.tensor_tensor(w[:, 9], lam[:, 0], w[:, 7], ALU.mult))
                link(V.scalar_tensor_tensor(out=w[:, 10], in0=lam[:, 1], scalar=-1.0, in1=w[:, 7], op0=ALU.mult, op1=ALU.mult))
                cmul(w[:, 0], w[:, 1], w[:, 8], pw[:, 1, 1], w[:, 9], w[:, 10], w[:, 5], w[:, 6])
                fr = [w[:, i].unsqueeze(2).broadcast_to((P, NPAIR, SC)) for i in range(2)]
                cmul(bb[:, 0], bb[:, 1], b_in[:, 0], b_in[:, 1], fr[0], fr[1], t1[:, :, 0, :], t2[:, :, 0, :])
                bx = [bb[:, i].unsqueeze(2).broadcast_to((P, NPAIR, CH, SC)) for i in range(2)]
                px = [pr[:, i].rearrange("p j k -> p k j").unsqueeze(3).broadcast_to((P, NPAIR, CH, SC)) for i in range(2)]
                cmul(xb[:, 0], xb[:, 1], bx[0], bx[1], px[0], px[1], t1[:, :, 0:CH, :], t2[:, :, 0:CH, :])
                dve.wait_ge(s_cT, 1)
                link(V.tensor_copy(cT[:].rearrange("p i k q -> p (i k q)"), bank[:, 0, :]))
                V.memset(w[:, 11], 0.0).then_inc(s_xb, 2)
                cx = [cT[:, i].unsqueeze(2).broadcast_to((P, NPAIR, CH + 1, SC)) for i in range(2)]
                px = [pw[:, i].rearrange("p j k -> p k j").unsqueeze(3).broadcast_to((P, NPAIR, CH + 1, SC)) for i in range(2)]
                link(V.tensor_tensor(t1[:], cx[0], px[0], ALU.mult))
                link(V.tensor_tensor(t2[:], cx[1], px[1], ALU.mult))
                link(V.tensor_tensor(out[:, 0], t1[:], t2[:], ALU.subtract))
                link(V.tensor_tensor(t1[:], cx[0], px[1], ALU.mult))
                link(V.tensor_tensor(t2[:], cx[1], px[0], ALU.mult))
                V.scalar_tensor_tensor(out=out[:, 1], in0=t1[:], scalar=-1.0, in1=t2[:], op0=ALU.mult, op1=ALU.subtract).then_inc(s_out, 2)
                for g4 in range(8):
                    dve.wait_ge(s_tb, g4 + 1)
                    V.tensor_copy(binT[:, g4 // 4, 4 * (g4 % 4):4 * (g4 % 4) + 4, :].rearrange("p k n -> p (k n)"), bank[:, g4, :]).then_inc(s_te, 1)
                for g4 in range(8):
                    dve.wait_ge(s_k, g4 + 1)
                    link(V.tensor_copy(kern[:].rearrange("q (k r) n -> q r k n", r=2)[:, g4 // 4, 4 * (g4 % 4):4 * (g4 % 4) + 4, :],
                                       bank[:SC, g4, :].rearrange("q (k n) -> q k n", k=4)))
                link(V.tensor_tensor(t1[:SC].rearrange("q k t p -> q (k t p)")[:, 0:SG * SC].rearrange("q (g p) -> q g p", g=SG),
                                     c["ident"][:SC, :SC].unsqueeze(1).broadcast_to((SC, SG, SC)),
                                     dskip[:].unsqueeze(2).broadcast_to((SC, SG, SC)), ALU.mult))
                V.tensor_tensor(kern[:, :, 0:SC], kern[:, :, 0:SC],
                                t1[:SC].rearrange("q k t p -> q (k t p)")[:, 0:SG * SC].rearrange("q (g p) -> q g p", g=SG), ALU.add).then_inc(s_kern, 1)


def s5_prompt(nc, a, d, c, m, hlast):
    bank = c["bank"]
    HK = NPAIR // 2
    HG = SG // 2
    out, binT, toep = m["out"], m["binT"], m["toep"]
    with ExitStack() as ctx:
        ctx.callback(nc.all_engine_barrier)
        def sb(name, shape):
            return ctx.enter_context(nc.sbuf_tensor(name, shape, F32))

        u = sb("sp_u", [P, HG, NCH])
        e = sb("sp_e", [P, 2, HK, NCH])
        e8 = sb("sp_e8", [P, 4, HK])
        decay = sb("sp_decay", [P, HK, NCH])
        t1 = sb("sp_t1", [P, HK, NCH])
        t2 = sb("sp_t2", [P, HK, NCH])
        s = sb("sp_s", [P, 2, HK, NCH])
        hs = sb("sp_h", [P, 2, HK, NCH + 1])
        y = sb("sp_y", [P, HG, NCH])
        names = ["u", "s", "ev", "h", "y", "g", "st", "dv"]
        S = {n: cleared(nc, ctx, "sp_s_" + n) for n in names}

        for hf in range(2):
            k0 = HK * hf
            with nc.Block() as block:
                @block.sync
                def _(sp):
                    for j in range(CH):
                        sp.dma_start(u[SC * j:SC * (j + 1)], d["u"].rearrange("(g q) j k -> q g j k", q=SC)[:, HG * hf:HG * (hf + 1), j, :]).then_inc(S["u"], 16)
                    for q4 in range(4):
                        sp.wait_ge(S["g"], q4 + 1)
                        for i in range(CH):
                            sp.dma_start(d["y"].rearrange("(k r p) i c -> p r k i c", p=SC, r=2)[:, q4 // 2, k0 + 4 * (q4 % 2):k0 + 4 * (q4 % 2) + 4, i, :],
                                         y[SC * i:SC * (i + 1), 4 * q4:4 * q4 + 4, :]).then_inc(S["st"], 16)
                    sp.wait_ge(S["st"], 16 * CH * 4)

                @block.tensor
                def _(pe):
                    pe.wait_ge(S["u"], 16 * CH)
                    for kk in range(HK):
                        for i in range(2):
                            for r in range(2):
                                t = nc.tensor.matmul(bank[r * SN:(r + 1) * SN, 2 * (kk // 4) + i, (kk % 4) * NCH:(kk % 4 + 1) * NCH],
                                                     binT[:, i, k0 + kk, r * SN:(r + 1) * SN], u[:, 2 * kk + r, :], start=True, stop=True)
                        if kk % 4 == 3:
                            t.then_inc(S["s"], 1)
                    pe.wait_ge(S["h"], 1)
                    for j in range(HG):
                        kk, r = j % HK, j // HK
                        g = 2 * kk + r
                        rows = slice(r * SN, (r + 1) * SN)
                        o = bank[:, 4 + j // 4, (j % 4) * NCH:(j % 4 + 1) * NCH]
                        nc.tensor.matmul(o, toep[:, HG * hf + g, :], u[:, g, :], start=True, stop=False)
                        for i in range(2):
                            t = nc.tensor.matmul(o, out[rows, i, k0 + kk, 1:CH + 1, :].rearrange("p t q -> p (t q)"), hs[rows, i, kk, 0:NCH],
                                                 start=False, stop=i == 1)
                        if j % 4 == 3:
                            t.then_inc(S["y"], 1)

                @block.scalar
                def _(act):
                    for q4 in range(4):
                        act.wait_ge(S["y"], q4 + 1)
                        nc.scalar.activation(y[:, 4 * q4:4 * q4 + 4, :].rearrange("p g k -> p (g k)"), bank[:, 4 + q4, :], ACT.Gelu_apprx_tanh).then_inc(S["g"], 1)

                @block.vector
                def _(dve):
                    link = Chain(dve, S["dv"])
                    V = nc.vector

                    def cmul(o_re, o_im, a_re, a_im, b_re, b_im, u1, u2):
                        link(V.tensor_tensor(u1, a_re, b_re, ALU.mult))
                        link(V.tensor_tensor(u2, a_im, b_im, ALU.mult))
                        link(V.tensor_tensor(o_re, u1, u2, ALU.subtract))
                        link(V.tensor_tensor(u1, a_re, b_im, ALU.mult))
                        link(V.tensor_tensor(u2, a_im, b_re, ALU.mult))
                        link(V.tensor_tensor(o_im, u1, u2, ALU.add))

                    rot = [m["rot"][:, i, k0:k0 + HK] for i in range(2)]
                    cmul(e8[:, 0], e8[:, 1], rot[0], rot[1], rot[0], rot[1], t1[:, :, 0], t2[:, :, 0])
                    cmul(e8[:, 2], e8[:, 3], e8[:, 0], e8[:, 1], e8[:, 0], e8[:, 1], t1[:, :, 0], t2[:, :, 0])
                    cmul(e[:, 0, :, 0], e[:, 1, :, 0], e8[:, 2], e8[:, 3], e8[:, 2], e8[:, 3], t1[:, :, 0], t2[:, :, 0])
                    n = 1
                    while n < NCH:
                        last = [e[:, i, :, n - 1:n].broadcast_to((P, HK, n)) for i in range(2)]
                        cmul(e[:, 0, :, n:2 * n], e[:, 1, :, n:2 * n], e[:, 0, :, 0:n], e[:, 1, :, 0:n], last[0], last[1], t1[:, :, 0:n], t2[:, :, 0:n])
                        n *= 2
                    link(V.tensor_copy(decay[:], m["l8"][:, k0:k0 + HK].unsqueeze(2).broadcast_to((P, HK, NCH))))
                    link(V.memset(decay[:, :, 0:1], 0.0))
                    link(V.memset(hs[:, :, :, 0:1], 0.0))
                    for b2 in range(2):
                        dve.wait_ge(S["s"], b2 + 1)
                        sr, si = (bank[:, 2 * b2 + i, :].rearrange("p (k c) -> p k c", k=4) for i in range(2))
                        kk = slice(4 * b2, 4 * b2 + 4)
                        link(V.tensor_tensor(t1[:, kk], sr, e[:, 0, kk], ALU.mult))
                        link(V.tensor_tensor(t2[:, kk], si, e[:, 1, kk], ALU.mult))
                        link(V.tensor_tensor(s[:, 0, kk], t1[:, kk], t2[:, kk], ALU.add))
                        link(V.tensor_tensor(t1[:, kk], si, e[:, 0, kk], ALU.mult))
                        link(V.tensor_tensor(t2[:, kk], sr, e[:, 1, kk], ALU.mult))
                        link(V.tensor_tensor(s[:, 1, kk], t1[:, kk], t2[:, kk], ALU.subtract))
                    flat = "p k c -> p (k c)"
                    link(V.tensor_tensor_scan(t1[:].rearrange(flat), decay[:].rearrange(flat), s[:, 0].rearrange(flat), 0.0, ALU.mult, ALU.add))
                    link(V.tensor_tensor_scan(t2[:].rearrange(flat), decay[:].rearrange(flat), s[:, 1].rearrange(flat), 0.0, ALU.mult, ALU.add))
                    link(V.tensor_tensor(s[:, 0], t1[:], e[:, 0], ALU.mult))
                    link(V.tensor_tensor(s[:, 1], t2[:], e[:, 1], ALU.mult))
                    link(V.tensor_tensor(hs[:, 0, :, 1:NCH + 1], s[:, 0], s[:, 1], ALU.subtract))
                    link(V.tensor_tensor(s[:, 0], t1[:], e[:, 1], ALU.mult))
                    link(V.tensor_tensor(s[:, 1], t2[:], e[:, 0], ALU.mult))
                    V.tensor_tensor(hs[:, 1, :, 1:NCH + 1], s[:, 0], s[:, 1], ALU.add).then_inc(S["h"], 1)
                    dve.wait_ge(S["h"], 1)
                    link(V.tensor_copy(hlast[:, :, k0:k0 + HK], hs[:, :, :, NCH]))
            next_iteration(nc, S.values())


def s5_sample(nc, a, d, c, m, hlast):
    bank = c["bank"]
    out, binT, toep = m["out"], m["binT"], m["toep"]
    LO = P - DT * SC
    with ExitStack() as ctx:
        ctx.callback(nc.all_engine_barrier)
        def sb(name, shape):
            return ctx.enter_context(nc.sbuf_tensor(name, shape, F32))

        u = sb("ss_u", [P, SG, DB])
        st_in = sb("ss_in", [P, P, 2])
        h0 = sb("ss_h0", [P, 2, NPAIR, DB])
        hl = sb("ss_hl", [P, 2, DB, NPAIR])
        t = sb("ss_t", [P, 4, NPAIR, DB])
        y = sb("ss_y", [P, SG, DB])
        st_s = sb("ss_os", [P, P, 2])
        st_p = sb("ss_op", [NPAIR, P, 2])
        names = ["ld", "h0t", "h0", "y", "g", "hl", "stt", "so", "st", "dv"]
        S = {n: cleared(nc, ctx, "ss_s_" + n) for n in names}

        with nc.Block() as block:
            @block.sync
            def _(sp):
                for t4 in range(DT):
                    sp.dma_start(u[LO + SC * t4:LO + SC * (t4 + 1)], d["us"].rearrange("(g q) t b -> q g t b", q=SC)[:, :, t4, :]).then_inc(S["ld"], 16)
                sp.dma_start(st_in[:], a["state_s5"][0].rearrange("b (k r) n c -> (b k) (r n) c", r=2)).then_inc(S["ld"], 16)
                sp.wait_ge(S["g"], 2)
                for t4 in range(DT):
                    sp.dma_start(d["ys"].rearrange("(g p) t b -> p g t b", p=SC)[:, :, t4, :], y[LO + SC * t4:LO + SC * (t4 + 1)]).then_inc(S["st"], 16)
                sp.wait_ge(S["so"], 2)
                sp.dma_start(a["o_s5_state_sample"][0].rearrange("b (k r) n c -> (b k) (r n) c", r=2), st_s[:]).then_inc(S["st"], 16)
                sp.dma_start(a["o_s5_state_prompt"][0, 0].rearrange("(k r) n c -> k (r n) c", r=2), st_p[:]).then_inc(S["st"], 16)
                sp.wait_ge(S["st"], 16 * (DT + 2))

            @block.tensor
            def _(pe):
                pe.wait_ge(S["ld"], 16 * (DT + 1))
                for i in range(2):
                    x = nc.tensor.transpose(bank[:, 0, i * P:(i + 1) * P], st_in[:, :, i], c["ident"][:])
                x.then_inc(S["h0t"], 1)
                pe.wait_ge(S["h0"], 3)
                for g in range(SG):
                    k, r = g // 2, g % 2
                    rows = slice(r * SN, (r + 1) * SN)
                    o = bank[LO:P, 6 + r, k * DB:(k + 1) * DB]
                    nc.tensor.matmul(o, toep[:, g, LO:P], u[:, g, :], start=True, stop=False)
                    for i in range(2):
                        nc.tensor.matmul(o, out[rows, i, k, 1:DT + 1, :].rearrange("p t q -> p (t q)"), h0[rows, i, k, :], start=False, stop=i == 1)
                    for i in range(2):
                        x = nc.tensor.matmul(bank[rows, 2 + i, k * DB:(k + 1) * DB], binT[:, i, k, rows], u[:, g, :], start=True, stop=True)
                x.then_inc(S["y"], 1)
                pe.wait_ge(S["hl"], 2)
                for i in range(2):
                    nc.tensor.transpose(bank[:, 4, i * P:(i + 1) * P], hl[:, i].rearrange("p b k -> p (b k)"), c["ident"][:])
                    x = nc.tensor.transpose(bank[:NPAIR, 5, i * P:(i + 1) * P], hlast[:, i, :], c["ident"][:])
                x.then_inc(S["stt"], 1)

            @block.scalar
            def _(act):
                act.wait_ge(S["y"], 1)
                for r in range(2):
                    nc.scalar.activation(y[LO:P].rearrange("p (k r) b -> p r k b", r=2)[:, r], bank[LO:P, 6 + r, 0:NPAIR * DB].rearrange("p (k b) -> p k b", b=DB),
                                         ACT.Gelu_apprx_tanh).then_inc(S["g"], 1)

            @block.vector
            def _(dve):
                link = Chain(dve, S["dv"])
                V = nc.vector
                V.memset(u[0:LO], 0.0).then_inc(S["h0"], 1)
                dve.wait_ge(S["h0t"], 1)
                for i in range(2):
                    V.tensor_copy(h0[:, i], bank[:, 0, i * P:(i + 1) * P].rearrange("p (b k) -> p k b", b=DB)).then_inc(S["h0"], 1)
                dve.wait_ge(S["y"], 1)
                dve.wait_ge(S["h0"], 3)
                l4 = [m["l4"][:, i].unsqueeze(2).broadcast_to((P, NPAIR, DB)) for i in range(2)]
                for j, (x, l) in enumerate(((0, 0), (1, 1), (0, 1), (1, 0))):
                    link(V.tensor_tensor(t[:, j], h0[:, x], l4[l], ALU.mult))
                link(V.tensor_tensor(t[:, 0], t[:, 0], t[:, 1], ALU.subtract))
                link(V.tensor_tensor(t[:, 2], t[:, 2], t[:, 3], ALU.add))
                for i in range(2):
                    V.tensor_tensor(hl[:, i].rearrange("p b k -> p k b"), t[:, 2 * i], bank[:, 2 + i, 0:NPAIR * DB].rearrange("p (k b) -> p k b", b=DB), ALU.add).then_inc(S["hl"], 1)
                dve.wait_ge(S["stt"], 1)
                V.tensor_copy(st_s[:].rearrange("p n c -> p c n"), bank[:, 4, 0:2 * P].rearrange("p (c n) -> p c n", c=2)).then_inc(S["so"], 1)
                V.tensor_copy(st_p[:].rearrange("p n c -> p c n"), bank[:NPAIR, 5, 0:2 * P].rearrange("p (c n) -> p c n", c=2)).then_inc(S["so"], 1)


def even_output(nc, a, d, c, act_t):
    zaT, zbT, oa = act_t["zaT"], act_t["zbT"], act_t["oa"]
    bank = c["bank"]
    with ExitStack() as ctx:
        ctx.callback(nc.all_engine_barrier)
        def sb(name, shape):
            return ctx.enter_context(nc.sbuf_tensor(name, shape, F32))

        gT = sb("eo_g", [P, 4, 512])
        sg = sb("eo_sg", [P, 2, 512])
        wg = sb("eo_wg", [P, 4, SW])
        bg = sb("eo_bg", [P, 4])
        wo = sb("eo_wo", [P, KD, D_MODEL])
        mixa = sb("eo_mixa", [P, 4, P])
        mixb = sb("eo_mixb", [P, 4, P])
        x = sb("eo_x", [P, D_MODEL])
        x1 = sb("eo_x1", [P, D_MODEL])
        s_wg = cleared(nc, ctx, "eo_s_wg")
        s_wo = cleared(nc, ctx, "eo_s_wo")
        names = ["g", "mm", "sg", "dv", "x", "T", "mix", "o", "x1", "st"]
        S = {n: cleared(nc, ctx, "eo_s_" + n) for n in names}

        with nc.Block() as block:
            @block.sync
            def _(sp):
                sp.dma_start(wg[:], a["s5_w_glu"][0].rearrange("(k p) n -> p k n", p=P)).then_inc(s_wg, 16)
                sp.dma_start(bg[:], a["s5_b_glu"][0].rearrange("(k p) -> p k", p=P), allow_slow_non_contiguous=True).then_inc(s_wg, 16)
                for k in range(KD):
                    sp.dma_start(wo[:, k], a["w_out_even"][0, k * P:(k + 1) * P, :]).then_inc(s_wo, 16)

        for j, n in ((0, 512), (1, 512), (2, NS)):
            with nc.Block() as block:
                @block.sync
                def _(sp):
                    sp.wait_ge(s_wg, 32)
                    if j < 2:
                        for i in range(CH):
                            src = d["y"].rearrange("(e p) i k -> p e i k", p=P)[:, :, i, j * 64:(j + 1) * 64]
                            sp.dma_start(gT[:, :, i * 64:(i + 1) * 64], src).then_inc(S["g"], 16)
                    else:
                        sp.dma_start(gT[:, :, 0:NS], d["ys"].rearrange("(e p) t b -> p e (t b)", p=P)).then_inc(S["g"], 16)

                @block.tensor
                def _(pe):
                    pe.wait_ge(S["g"], 16 * (CH if j < 2 else 1))
                    pe.wait_ge(s_wg, 32)
                    for e in range(4):
                        for k in range(4):
                            t = nc.tensor.matmul(bank[:, e, :n], wg[:, k, e * P:(e + 1) * P], gT[:, k, :n], start=k == 0, stop=k == 3)
                        t.then_inc(S["mm"], 1)

                @block.scalar
                def _(act):
                    for e in range(4):
                        act.wait_ge(S["mm"], e + 1)
                        if e >= 2:
                            act.wait_ge(S["dv"], 2 * (e - 1))
                        nc.scalar.activation(sg[:, e % 2, :n], bank[:, e, :n], ACT.Sigmoid, bias=bg[:, e:e + 1]).then_inc(S["sg"], 1)

                @block.vector
                def _(dve):
                    link = Chain(dve, S["dv"])
                    for e in range(4):
                        dve.wait_ge(S["sg"], e + 1)
                        link(nc.vector.tensor_tensor(sg[:, e % 2, :n], sg[:, e % 2, :n], gT[:, e, :n], ALU.mult))
                        if j < 2:
                            z = zbT[:, e, j * 512:(j + 1) * 512].rearrange("p (k i) -> p i k", i=CH)
                            link(nc.vector.tensor_tensor(z, z, sg[:, e % 2, :].rearrange("p (i k) -> p i k", i=CH), ALU.mult))
                        else:
                            z = zbT[:, e, SEQ:NTOK].rearrange("p (b t) -> p t b", t=DT)
                            link(nc.vector.tensor_tensor(z, z, sg[:, e % 2, :n].rearrange("p (t b) -> p t b", t=DT), ALU.mult))
            next_iteration(nc, S.values())

        def tile(n, tok0, i, prompt):
            with nc.Block() as block:
                @block.sync
                def _(sp):
                    src = a["x_prompt"][0, ds(tok0, n), :] if prompt else a["x_sample"].rearrange("b t d -> (b t) d")
                    sp.dma_start(x[:n], src).then_inc(S["x"], 16)
                    sp.wait_ge(S["x1"], 2)
                    sp.dma_start(d["x1"][ds(tok0, n), :], x1[:n]).then_inc(S["st"], 16)
                    sp.wait_ge(S["st"], 16)

                @block.tensor
                def _(pe):
                    pe.wait_ge(s_wo, 16 * KD)
                    pe.wait_ge(S["T"], 1)
                    for k in range(4):
                        t = nc.tensor.transpose(bank[:, 0, k * n:(k + 1) * n], sg[:n, 0, k * P:(k + 1) * P], c["ident"][:n, :n])
                    t.then_inc(S["T"], 1)
                    pe.wait_ge(S["mix"], 2)
                    for hf in range(2):
                        for k in range(KD):
                            lhsT = mixa[:, k, :n] if k < 4 else mixb[:, k - 4, :n]
                            t = nc.tensor.matmul(bank[:n, 1 + hf, :], lhsT, wo[:, k, hf * 512:(hf + 1) * 512], start=k == 0, stop=k == KD - 1)
                        t.then_inc(S["o"], 1)

                @block.scalar
                def _(act):
                    nc.scalar.activation(sg[:n, 0, :], oa[:n, ds(i, 1), :].rearrange("p i e -> p (i e)"), ACT.Copy).then_inc(S["T"], 1)
                    nc.scalar.activation(mixb[:, :, :n], zbT[:, :, ds(tok0, n)], ACT.Copy).then_inc(S["mix"], 1)

                @block.vector
                def _(dve):
                    dve.wait_ge(S["T"], 2)
                    nc.vector.tensor_tensor(mixa[:, :, :n], bank[:, 0, :4 * n].rearrange("p (k t) -> p k t", k=4), zaT[:, :, ds(tok0, n)], ALU.mult).then_inc(S["mix"], 1)
                    dve.wait_ge(S["x"], 16)
                    for hf in range(2):
                        dve.wait_ge(S["o"], hf + 1)
                        cols = slice(hf * 512, (hf + 1) * 512)
                        nc.vector.tensor_tensor(x1[:n, cols], bank[:n, 1 + hf, :], x[:n, cols], ALU.add).then_inc(S["x1"], 1)

        with nc.Fori(0, NTILE) as i:
            tile(P, i * P, i, True)
            next_iteration(nc, S.values())
        tile(NS, SEQ, NTILE, False)


def odd_projection(nc, a, d, c, o):
    kv, ksT, kwT, gate, kTs = (o[k] for k in ("kv", "ksT", "kwT", "gate", "kTs"))
    bank = c["bank"]
    chunks = ((0, 512), (512, 6 * KVW + 3 * NH), (6 * KVW + 3 * NH, 6 * KVW + 3 * NH + 512), (6 * KVW + 3 * NH + 512, ODD_TOK))
    with ExitStack() as ctx:
        ctx.callback(nc.all_engine_barrier)
        def sb(name, shape):
            return ctx.enter_context(nc.sbuf_tensor(name, shape, F32))

        w = sb("op_w", [P, KD, ODD_IN])
        g = sb("op_g", [P, KD])
        x = sb("op_x", [P, D_MODEL])
        h = sb("op_h", [P, D_MODEL])
        hT = sb("op_hT", [P, KD, P])
        tk = sb("op_tk", [P, 6 * KVW])
        zs = sb("op_zs", [P, NW])
        qS = sb("op_q", [P, KD, P])
        st = sb("op_st", [P, 4])
        s_w = cleared(nc, ctx, "op_s_w")
        names = ["x", "ss", "ms", "sd", "rs", "T", "hT", "tok", "q", "tk", "z", "qs", "T2", "kT", "st", "gate", "kv", "nt"]
        S = {n: cleared(nc, ctx, "op_s_" + n) for n in names}
        s_rows = cleared(nc, ctx, "op_s_rows")

        with nc.Block() as block:
            @block.sync
            def _(sp):
                for k in range(KD):
                    sp.dma_start(w[:, k, :], a["w_in_odd"][0, k * P:(k + 1) * P, :]).then_inc(s_w, 16)
                sp.dma_start(g[:], a["norm_odd"][0].rearrange("(k p) -> p k", p=P), allow_slow_non_contiguous=True).then_inc(s_w, 16)
                for gg in range(NG):
                    sp.dma_start(ksT[HD:HD + 1, gg, :], a["c_kpos"]).then_inc(s_w, 16)
                    sp.dma_start(kwT[HD:HD + 1, gg, :], a["c_kpos"]).then_inc(s_w, 16)
                sp.wait_ge(s_w, 16 * (KD + 5))

        def tile(n, tok0, i, prompt):
            with nc.Block() as block:
                @block.sync
                def _(sp):
                    sp.dma_start(x[:n], d["x1"][ds(tok0, n), :]).then_inc(S["x"], 16)
                    sp.wait_ge(S["z"], 2)
                    sp.dma_start(d["z"][ds(tok0, n), :], zs[:n]).then_inc(S["st"], 16)
                    sp.wait_ge(S["qs"], 2)
                    sp.dma_start(d["qT"].rearrange("(e p) t -> p e t", p=P)[:, :, ds(tok0, n)], qS[:, :, :n]).then_inc(S["st"], 16)
                    sp.wait_ge(S["st"], 32)
                    if not prompt:
                        sp.wait_ge(S["tk"], 2)
                        sp.dma_start(a["o_nsa_rows_sample"][0].rearrange("b t k g d -> (b t) (k g d)"), tk[:n, 0:512]).then_inc(s_rows, 16)
                        for b in range(DB):
                            sp.dma_start(a["o_nsa_win_sample"][0, b, WIN - DT:WIN].rearrange("t k g d -> t (k g d)"), tk[DT * b:DT * (b + 1), 512:768]).then_inc(s_rows, 16)
                        sp.dma_start(a["o_nsa_win_sample"][0, :, 0:WIN - DT].rearrange("b t k g d -> b (t k g d)"),
                                     a["state_nsa_win"][0, :, DT:WIN].rearrange("b t k g d -> b (t k g d)")).then_inc(s_rows, 16)
                        sp.dma_start(a["o_nsa_rows_prompt"][0, 0].rearrange("(i p) k g d -> p i (k g d)", p=P), kv[:, :, 0:512]).then_inc(s_rows, 16)
                        sp.dma_start(a["o_nsa_win_prompt"][0, 0].rearrange("(i p) k g d -> p i (k g d)", p=P), kv[:, NTILE - WIN // P:, 512:768]).then_inc(s_rows, 16)
                        sp.wait_ge(s_rows, 16 * (DB + 4))

                @block.gpsimd
                def _(pool):
                    if prompt:
                        pool.wait_ge(S["tk"], 2)
                        nc.gpsimd.tensor_copy(kv[:, ds(i, 1), :].rearrange("p i c -> p (i c)"), tk[:]).then_inc(S["kv"], 1)

                @block.scalar
                def _(act):
                    act.wait_ge(S["x"], 16)
                    nc.scalar.activation(h[:n], x[:n], ACT.Square, accum_out=st[:n, 0:1]).then_inc(S["ss"], 1)
                    act.wait_ge(S["ms"], 1)
                    nc.scalar.activation(st[:n, 2:3], st[:n, 1:2], ACT.Sqrt).then_inc(S["sd"], 1)
                    act.wait_ge(S["tk"], 2)
                    act.wait_ge(S["tok"], 2)
                    nc.scalar.activation(gate[:n, ds(i, 1), :].rearrange("p i c -> p (i c)"), bank[:n, 3, 256:256 + 3 * NH], ACT.Sigmoid).then_inc(S["gate"], 1)
                    for j in range(2):
                        act.wait_ge(S["tok"], 3 + j)
                        nc.scalar.activation(zs[:n, 512 * j:512 * (j + 1)], bank[:n, 4 + j, :], ACT.Silu).then_inc(S["z"], 1)

                @block.tensor
                def _(pe):
                    pe.wait_ge(S["rs"], 2)
                    for k in range(KD):
                        t = nc.tensor.transpose(bank[:, k // 4, (k % 4) * n:(k % 4 + 1) * n], h[:n, k * P:(k + 1) * P], c["ident"][:n, :n])
                    t.then_inc(S["T"], 1)
                    pe.wait_ge(S["hT"], 2)
                    for j, (lo, hi) in enumerate(chunks):
                        for k in range(KD):
                            t = nc.tensor.matmul(bank[:n, 2 + j, 0:hi - lo], hT[:, k, :n], w[:, k, NW + lo:NW + hi], start=k == 0, stop=k == KD - 1)
                        t.then_inc(S["tok"], 1)
                    for e in range(KD):
                        for k in range(KD):
                            t = nc.tensor.matmul(bank[:, 6 + e // 4, (e % 4) * n:(e % 4 + 1) * n], w[:, k, e * P:(e + 1) * P], hT[:, k, :n], start=k == 0, stop=k == KD - 1)
                        if e % 4 == 3:
                            t.then_inc(S["q"], 1)
                    pe.wait_ge(S["tk"], 2)
                    if prompt:
                        for j in range(4):
                            lo = (2 * KVW if j < 2 else 4 * KVW) + (j % 2) * HD
                            t = nc.tensor.transpose(bank[:HD, 0, j * n:(j + 1) * n], tk[:n, lo:lo + HD], c["ident"][:n, :n])
                    else:
                        for j in range(2):
                            t = nc.tensor.transpose(bank[:, 0, j * n:(j + 1) * n], tk[:n, (2 + 2 * j) * KVW:(3 + 2 * j) * KVW], c["ident"][:n, :n])
                    t.then_inc(S["T2"], 1)

                @block.vector
                def _(dve):
                    V = nc.vector
                    dve.wait_ge(S["ss"], 1)
                    V.tensor_scalar(st[:n, 1:2], st[:n, 0:1], 1.0 / D_MODEL, EPS, ALU.mult, ALU.add).then_inc(S["ms"], 1)
                    dve.wait_ge(S["sd"], 1)
                    V.reciprocal(st[:n, 3:4], st[:n, 2:3]).then_inc(S["rs"], 1)
                    dve.wait_ge(S["rs"], 1)
                    V.tensor_scalar(h[:n], x[:n], st[:n, 3:4], None, ALU.mult).then_inc(S["rs"], 1)
                    dve.wait_ge(S["T"], 1)
                    for b in range(2):
                        V.tensor_tensor(hT[:, 4 * b:4 * b + 4, :n], bank[:, b, :4 * n].rearrange("p (k t) -> p k t", k=4),
                                        g[:, 4 * b:4 * b + 4].unsqueeze(2).broadcast_to((P, 4, n)), ALU.mult).then_inc(S["hT"], 1)
                    dve.wait_ge(S["tok"], 1)
                    V.tensor_copy(tk[:n, 0:512], bank[:n, 2, :]).then_inc(S["tk"], 1)
                    dve.wait_ge(S["tok"], 2)
                    V.tensor_copy(tk[:n, 512:768], bank[:n, 3, 0:256]).then_inc(S["tk"], 1)
                    for j in range(2):
                        dve.wait_ge(S["q"], j + 1)
                        V.tensor_scalar(qS[:, 4 * j:4 * j + 4, :n], bank[:, 6 + j, :4 * n].rearrange("p (e t) -> p e t", e=4), NSA_SCALE, None, ALU.mult).then_inc(S["qs"], 1)
                    dve.wait_ge(S["T2"], 1)
                    if prompt:
                        for j, dst in enumerate((ksT, kwT)):
                            V.tensor_copy(dst[:HD, :, ds(tok0, n)], bank[:HD, 0, 2 * j * n:2 * (j + 1) * n].rearrange("p (g t) -> p g t", g=2)).then_inc(S["kT"], 1)
                    else:
                        V.tensor_copy(kTs[:].rearrange("p j t -> p (j t)"), bank[:, 0, 0:2 * n]).then_inc(S["kT"], 1)

        with nc.Fori(0, NTILE) as i:
            tile(P, i * P, i, True)
            next_iteration(nc, S.values())
        tile(NS, SEQ, NTILE, False)


def compress(nc, a, d, c, o):
    kv, kcT, vc, kcp, vcp = (o[k] for k in ("kv", "kcT", "vc", "kcp", "vcp"))
    bank = c["bank"]
    HP = NPAGE // 2
    with ExitStack() as ctx:
        ctx.callback(nc.all_engine_barrier)
        def sb(name, shape):
            return ctx.enter_context(nc.sbuf_tensor(name, shape, F32))

        phi = sb("cm_phi", [P, 2, HD, P])
        phi2 = sb("cm_phi2", [P, 2, HD])
        pe_sb = sb("cm_pe", [P, 2, HD])
        bias = sb("cm_bias", [P, 2])
        pg = sb("cm_pg", [P, 2, HP, 2 * KVW])
        hid = sb("cm_hid", [P, 2, 2 * HP])
        vT = sb("cm_vT", [HD, NG, 2 * NTILE])
        s_w = cleared(nc, ctx, "cm_s_w")
        s_zero = cleared(nc, ctx, "cm_s_zero")
        names = ["acc", "hid", "out", "ev", "dv"]
        S = {n: cleared(nc, ctx, "cm_s_" + n) for n in names}
        s_half = [cleared(nc, ctx, f"cm_s_half{i}") for i in range(2)]

        def load_half(sp, b, hf):
            with sp.Fori(0, HP) as j:
                page = sp.value_load(c["pages"][0:1, ds(b * NPAGE + hf * HP + j, 1)], min_val=0, max_val=POOL - 1)
                sp.dma_start(pg[:, hf, ds(j, 1), :].rearrange("p j c -> p (j c)"),
                             a["cache_nsa_kv"][0, ds(page, 1)].rearrange("a p k g d -> (a p) (k g d)")[:, 0:2 * KVW]).then_inc(s_half[hf], 16)

        def hidden(kind, n, rhs):
            for x in range(HD):
                t = nc.tensor.matmul(bank[:, kind, 0:n], phi[:, kind, x, :], rhs(x), start=x == 0, stop=x == HD - 1)
            return t

        with nc.Block() as block:
            @block.gpsimd
            def _(pool):
                nc.gpsimd.memset(phi[:], 0.0).then_inc(s_zero, 1)

            @block.sync
            def _(sp):
                for hf in range(2):
                    load_half(sp, 0, hf)

            @block.scalar
            def _(act):
                act.wait_ge(s_zero, 1)
                for half in range(2):
                    rows = slice(half * BLK, (half + 1) * BLK)
                    for kind, (p1, p2, pe) in enumerate((("nsa_phi1_k", "nsa_phi2_k", "nsa_pe_k"), ("nsa_phi1_v", "nsa_phi2_v", "nsa_pe_v"))):
                        act.dma_start(phi[rows, kind, :, half * HD:(half + 1) * HD], a[p1][0].rearrange("(r x) m -> r x m", x=HD)).then_inc(s_w, 16)
                        act.dma_start(phi2[rows, kind, :], a[p2][0]).then_inc(s_w, 16)
                        act.dma_start(pe_sb[rows, kind, :], a[pe][0]).then_inc(s_w, 16)
                act.wait_ge(S["acc"], 1)
                nc.scalar.activation(bias[:, 0:1], bank[:, 0, 0:1], ACT.Copy).then_inc(S["hid"], 1)
                nc.scalar.activation(bias[:, 1:2], bank[:, 1, 0:1], ACT.Copy).then_inc(S["hid"], 1)
                act.wait_ge(S["acc"], 3)
                act.wait_ge(S["hid"], 2)
                for kind in range(2):
                    nc.scalar.activation(hid[:, kind, 0:2 * NTILE], bank[:, kind, 0:2 * NTILE], ACT.Silu, bias=bias[:, kind:kind + 1]).then_inc(S["hid"], 1)

            @block.tensor
            def _(pe):
                pe.wait_ge(s_w, 16 * 12)
                for kind in range(2):
                    t = hidden(kind, 1, lambda x: pe_sb[:, kind, x:x + 1])
                t.then_inc(S["acc"], 1)
                pe.wait_ge(S["hid"], 2)
                for kind in range(2):
                    hidden(kind, 2 * NTILE, lambda x: kv[:, :, kind * KVW:(kind + 1) * KVW].rearrange("p i (g x) -> p i g x", g=NG)[:, :, :, x]).then_inc(S["acc"], 1)
                pe.wait_ge(S["hid"], 4)
                for kind in range(2):
                    for half in range(2):
                        rows = slice(half * HD, (half + 1) * HD)
                        t = nc.tensor.matmul(bank[:HD, 4 + half, kind * 2 * NTILE:(kind + 1) * 2 * NTILE], phi2[rows, kind, :], hid[rows, kind, 0:2 * NTILE], start=True, stop=True)
                t.then_inc(S["out"], 1)
                pe.wait_ge(S["ev"], 4)
                for gg in range(NG):
                    t = nc.tensor.transpose(bank[:2 * NTILE, 6, gg * HD:(gg + 1) * HD], vT[:, gg, :], c["ident"][:HD, :HD])
                t.then_inc(S["out"], 1)

            @block.vector
            def _(dve):
                dve.wait_ge(S["out"], 1)
                for half in range(2):
                    for kind, dst in ((0, kcp[:HD]), (1, vT[:])):
                        nc.vector.tensor_copy(dst[:, :, half * NTILE:(half + 1) * NTILE],
                                              bank[:HD, 4 + half, kind * 2 * NTILE:(kind + 1) * 2 * NTILE].rearrange("p (i g) -> p g i", g=NG)).then_inc(S["ev"], 1)
                dve.wait_ge(S["out"], 2)
                nc.vector.tensor_copy(vcp[:], bank[:2 * NTILE, 6, 0:NG * HD]).then_inc(S["ev"], 1)
        next_iteration(nc, S.values())

        with nc.Fori(0, DB) as b:
            with nc.Block() as block:
                @block.sync
                def _(sp):
                    nxt = sp.snap((b + 1) % DB)
                    for hf in range(2):
                        sp.wait_ge(S["acc"], 2 * (hf + 1))
                        sp.sem_clear(s_half[hf])
                        load_half(sp, nxt, hf)

                @block.scalar
                def _(act):
                    for hf in range(2):
                        for kind in range(2):
                            act.wait_ge(S["acc"], 2 * hf + kind + 1)
                            if hf:
                                act.wait_ge(S["out"], kind + 1)
                            nc.scalar.activation(hid[:, kind, :], bank[:, kind, 0:2 * HP], ACT.Silu, bias=bias[:, kind:kind + 1]).then_inc(S["hid"], 1)

                @block.tensor
                def _(pe):
                    def products(hf):
                        for kind in range(2):
                            pe.wait_ge(S["hid"], 2 * hf + kind + 1)
                            for half in range(2):
                                rows = slice(half * HD, (half + 1) * HD)
                                for gg in range(NG):
                                    cols = hid[rows, kind, :].rearrange("p (j g) -> p g j", g=NG)[:, gg, :]
                                    if kind == 0:
                                        t = nc.tensor.matmul(bank[gg * HD:(gg + 1) * HD, 4 + half, hf * HP:(hf + 1) * HP], phi2[rows, 0, :], cols, start=True, stop=True)
                                    else:
                                        t = nc.tensor.matmul(bank[hf * HP:(hf + 1) * HP, 6 + half, gg * HD:(gg + 1) * HD], cols, phi2[rows, 1, :], start=True, stop=True)
                            t.then_inc(S["out"], 1)

                    for hf in range(2):
                        pe.wait_ge(s_half[hf], 16 * HP)
                        for kind in range(2):
                            if hf:
                                pe.wait_ge(S["hid"], kind + 1)
                            hidden(kind, 2 * HP, lambda x: pg[:, hf, :, kind * KVW:(kind + 1) * KVW].rearrange("p j (g x) -> p j g x", g=NG)[:, :, :, x]).then_inc(S["acc"], 1)
                            if kind == 1:
                                products(hf)

                @block.vector
                def _(dve):
                    dve.wait_ge(S["out"], 4)
                    for half in range(2):
                        nc.vector.tensor_copy(kcT[:, ds(b, 1), half * NPAGE:(half + 1) * NPAGE].rearrange("p b j -> p (b j)"), bank[:, 4 + half, 0:NPAGE]).then_inc(S["ev"], 1)
                        nc.vector.tensor_copy(vc[:, ds(b, 1), half, :].rearrange("p b c -> p (b c)"), bank[:NPAGE, 6 + half, 0:KVW]).then_inc(S["ev"], 1)
            next_iteration(nc, S.values())

        with nc.Block() as block:
            @block.sync
            def _(sp):
                for hf in range(2):
                    sp.wait_ge(s_half[hf], 16 * HP)


def nsa_prompt(nc, a, d, c, o):
    kv, ksT, kwT, gate, kcp, vcp, oall = (o[k] for k in ("kv", "ksT", "kwT", "gate", "kcp", "vcp", "oall"))
    bank = c["bank"]
    NC = 2 * NTILE
    with ExitStack() as ctx:
        ctx.callback(nc.all_engine_barrier)
        def sb(name, shape):
            return ctx.enter_context(nc.sbuf_tensor(name, shape, F32))

        qT = sb("np_q", [P, SEQ])
        gh = sb("np_gh", [P, 3, NTILE])
        cmask = sb("np_cmask", [P, NTILE, NC])
        sc = sb("np_sc", [P, NTILE, NC])
        cm = sb("np_cm", [P, 3, NTILE])
        pcT = sb("np_pcT", [NC, SEQ])
        coef = sb("np_coef", [P, 2])
        buf = {"p": sb("np_p", [P, 2, SEQ]), "pT": sb("np_pT", [P, 2, SEQ]), "nmax": sb("np_nmax", [P, 2]),
               "den": sb("np_den", [P, 2]), "rden": sb("np_rden", [P, 2])}
        s_tab = cleared(nc, ctx, "np_s_tab")
        S = {n: cleared(nc, ctx, "np_s_" + n) for n in ["q", "cs", "cx", "ce", "cp", "ct", "ctt", "cv"] + ATT_SEMS}

        with nc.Block() as block:
            @block.sync
            def _(sp):
                sp.dma_start(cmask[:], a["c_cmask"]).then_inc(s_tab, 16)
                for gg in range(NG):
                    sp.dma_start(kcp[HD:HD + 1, gg, :], a["c_cpos"]).then_inc(s_tab, 16)
                sp.wait_ge(s_tab, 48)

        for gg in range(NG):
            with nc.Fori(gg * NR, (gg + 1) * NR) as h:
                with nc.Block() as block:
                    @block.sync
                    def _(sp):
                        sp.dma_start(qT[:HD, :], d["qT"][ds(h * HD, HD), 0:SEQ]).then_inc(S["q"], 16)
                        sp.dma_start(qT[HD:HD + 1, :], a["c_slope"][ds(h, 1), :]).then_inc(S["q"], 16)

                    def pe_before(pe):
                        pe.wait_ge(S["q"], 32)
                        for i in range(NTILE):
                            t = nc.tensor.matmul(bank[:, 7, i * NC:(i + 1) * NC], qT[:HD + 1, i * P:(i + 1) * P], kcp[:HD + 1, gg, :], start=True, stop=True)
                        t.then_inc(S["cs"], 1)
                        pe.wait_ge(S["cp"], 1)
                        for i in range(NTILE):
                            t = nc.tensor.transpose(bank[:NC, 4 + i // 4, (i % 4) * P:(i % 4 + 1) * P], sc[:, i, :], c["ident"][:])
                        t.then_inc(S["ct"], 1)
                        pe.wait_ge(S["ctt"], 1)
                        for i in range(NTILE):
                            t = nc.tensor.matmul(bank[:, 7, i * HD:(i + 1) * HD], pcT[:, i * P:(i + 1) * P], vcp[:, gg * HD:(gg + 1) * HD], start=True, stop=True)
                        t.then_inc(S["cv"], 1)

                    def act_before(act):
                        act.wait_ge(S["cx"], 1)
                        nc.scalar.activation(sc[:], sc[:], ACT.Exp).then_inc(S["ce"], 1)

                    def dve_before(dve, link):
                        V = nc.vector
                        link(V.tensor_copy(gh[:], gate[:, 0:NTILE, :].rearrange("p i (b h) -> p b i h", b=3)[:, :, :, ds(h, 1)].rearrange("p b i h -> p b (i h)")))
                        dve.wait_ge(S["cs"], 1)
                        link(V.tensor_tensor(sc[:], bank[:, 7, 0:NTILE * NC].rearrange("p (i n) -> p i n", i=NTILE), cmask[:], ALU.add))
                        link(V.tensor_reduce(cm[:, 0], sc[:], AX, ALU.max))
                        link(V.tensor_scalar(cm[:, 0], cm[:, 0], -1e20, None, ALU.max))
                        V.tensor_tensor(sc[:], sc[:], cm[:, 0].unsqueeze(2).broadcast_to((P, NTILE, NC)), ALU.subtract).then_inc(S["cx"], 1)
                        dve.wait_ge(S["ce"], 1)
                        link(V.tensor_reduce(cm[:, 1], sc[:], AX, ALU.add))
                        link(V.tensor_scalar(cm[:, 1], cm[:, 1], 1e-30, None, ALU.max))
                        link(V.reciprocal(cm[:, 2], cm[:, 1]))
                        link(V.tensor_tensor(cm[:, 2], cm[:, 2], gh[:, 0], ALU.mult))
                        V.tensor_tensor(sc[:], sc[:], cm[:, 2].unsqueeze(2).broadcast_to((P, NTILE, NC)), ALU.mult).then_inc(S["cp"], 1)
                        dve.wait_ge(S["ct"], 1)
                        V.tensor_copy(pcT[:], bank[:NC, 4:6, :].rearrange("p b t -> p (b t)")).then_inc(S["ctt"], 1)
                        dve.wait_ge(S["cv"], 1)
                        V.tensor_copy(oall[:, :, ds(h * HD, HD)], bank[:, 7, :].rearrange("p (i x) -> p i x", i=NTILE)).then_inc(S["qk"], 1)

                    def finish(i, branch):
                        def f(o_ps, r, link):
                            link(nc.vector.tensor_tensor(coef[:, 0:1], r, gh[:, branch, i:i + 1], ALU.mult))
                            dst = oall[:, i, ds(h * HD, HD)]
                            return nc.vector.scalar_tensor_tensor(out=dst, in0=o_ps, scalar=coef[:, 0:1], in1=dst, op0=ALU.mult, op1=ALU.add)
                        return f

                    units = []
                    for i in range(NTILE):
                        units.append({"q0": i * P, "nblk": i + 1, "kT": ksT[:HD + 1, gg, :], "masks": [(i * P, c["causal"][:])], "finish": finish(i, 1),
                                      "v": lambda b: kv[:, b, 3 * KVW + gg * HD:3 * KVW + (gg + 1) * HD]})
                    for i in range(NTILE):
                        b0 = max(0, i - WIN // P)
                        masks = [((i - b0) * P, c["causal"][:])] + ([(0, c["winlow"][:])] if i >= WIN // P else [])
                        units.append({"q0": i * P, "nblk": i - b0 + 1, "kT": kwT[:HD + 1, gg, b0 * P:], "masks": masks, "finish": finish(i, 2),
                                      "v": lambda b, b0=b0: kv[:, b0 + b, 5 * KVW + gg * HD:5 * KVW + (gg + 1) * HD]})
                    buf.update(pe_before=pe_before, act_before=act_before, dve_before=dve_before, qk_ready=1)
                    attention(nc, c, block, S, buf, units, qT, HD + 1)
                next_iteration(nc, S.values())


def nsa_sample(nc, a, d, c, o):
    kTs, kcT, vc = (o[k] for k in ("kTs", "kcT", "vc"))
    bank = c["bank"]
    NQ = NH * DT
    GP = 4
    NG4 = NPAGE // GP
    SEL = NBLK + 1
    with ExitStack() as ctx:
        ctx.callback(nc.all_engine_barrier)
        def sb(name, shape):
            return ctx.enter_context(nc.sbuf_tensor(name, shape, F32))

        qall = sb("ns_qall", [P, NR, NS])
        q = sb("ns_q", [P, NQ])
        pg = sb("ns_pg", [P, NPAGE, 2 * KVW])
        kT = sb("ns_kT", [P, 2, 512])
        s = sb("ns_s", [NQ, PAST])
        sn = sb("ns_sn", [NQ, 2, DT])
        pT = sb("ns_pT", [P, 2, 512])
        pnT = sb("ns_pnT", [DT, 2, NQ])
        vnew = sb("ns_vnew", [DT, 2, KVW])
        calibi = sb("ns_calibi", [NQ, NBLK])
        bonus = sb("ns_bonus", [NQ, SEL])
        balibi = sb("ns_balibi", [NQ, SEL])
        kalibi = sb("ns_kalibi", [NQ, BLK])
        nalibi = sb("ns_nalibi", [NQ, DT])
        walibi = sb("ns_walibi", [NQ, WIN])
        same = sb("ns_same", [NQ, NQ])
        pc = sb("ns_pc", [NQ, NBLK])
        pcT = sb("ns_pcT", [NPAGE, 2, NQ])
        vcb = sb("ns_vcb", [NPAGE, 2, KVW])
        score = sb("ns_score", [NQ, SEL])
        left = sb("ns_left", [NQ, 2, SEL])
        top = sb("ns_top", [NQ, 2, 8])
        selb = sb("ns_selb", [NQ, SEL])
        st = sb("ns_st", [NQ, 8])
        gmax = sb("ns_gmax", [NQ, NG4 + 1])
        gden = sb("ns_gden", [NQ, NG4 + 1])
        win = sb("ns_win", [P, WIN // P, 2 * KVW])
        sw = sb("ns_sw", [NQ, WIN])
        wden = sb("ns_wden", [NQ, 2])
        wmax = sb("ns_wmax", [NQ, 3])
        wT = sb("ns_wT", [P, WIN // P * NQ])
        kwin = sb("ns_kwin", [P, WIN])
        ob = sb("ns_ob", [NQ, 3, HD])
        s_w = cleared(nc, ctx, "ns_s_w")
        s_zero = cleared(nc, ctx, "ns_s_zero")
        names = ["q", "new", "cs", "cx", "ce", "pc", "pcT", "imp", "sel", "co", "tr", "kT", "sc", "s", "mx", "exp", "pt", "pT", "pv", "ob", "st", "dv",
                 "wt", "wk", "ws", "wx", "we", "wp", "wpT", "wo", "nk", "ep"]
        S = {n: cleared(nc, ctx, "ns_s_" + n) for n in names}
        s_group = [cleared(nc, ctx, f"ns_s_group{i}") for i in range(NG4)]

        def load_group(sp, b, gi):
            for j in range(GP):
                page = sp.value_load(c["pages"][0:1, ds(b * NPAGE + GP * gi + j, 1)], min_val=0, max_val=POOL - 1)
                sp.dma_start(pg[:, GP * gi + j, :], a["cache_nsa_kv"][0, ds(page, 1)].rearrange("a p k g d -> (a p) (k g d)")[:, 2 * KVW:4 * KVW]).then_inc(s_group[gi], 16)

        with nc.Block() as block:
            @block.scalar
            def _(act):
                for dst, key in ((calibi, "c_calibi"), (bonus, "c_bonus"), (balibi, "c_balibi"), (kalibi, "c_kalibi"), (nalibi, "c_nalibi"),
                                 (walibi, "c_walibi"), (same, "c_same")):
                    act.dma_start(dst[:], a[key]).then_inc(s_w, 16)
                for gg in range(NG):
                    act.dma_start(qall[gg * HD:(gg + 1) * HD], d["qT"].rearrange("(g r x) t -> g x r t", g=NG, x=HD)[gg][:, :, SEQ:NTOK]).then_inc(s_w, 16)
                act.wait_ge(s_w, 16 * 9)

            @block.sync
            def _(sp):
                for gi in range(NG4):
                    load_group(sp, 0, gi)

            @block.vector
            def _(dve):
                nc.vector.memset(q[:], 0.0).then_inc(s_zero, 1)
                dve.wait_ge(s_zero, 1)

        with nc.Fori(0, DB) as b:
            with nc.Block() as block:
                @block.sync
                def _(sp):
                    sp.dma_start(win[:], a["state_nsa_win"][0, ds(b, 1)].rearrange("b (i p) k g d -> p (b i) (k g d)", p=P)).then_inc(S["new"], 16)
                    sp.dma_start(vnew[:, 0, :], a["o_nsa_rows_sample"][0, ds(b, 1)].rearrange("b t k g d -> (b t) (k g d)")[:, 3 * KVW:4 * KVW]).then_inc(S["new"], 16)
                    sp.dma_start(vnew[:, 1, :], a["o_nsa_win_sample"][0, ds(b, 1), WIN - DT:WIN].rearrange("b t k g d -> (b t) (k g d)")[:, KVW:2 * KVW]).then_inc(S["new"], 16)
                    nxt = sp.snap((b + 1) % DB)
                    for gi in range(NG4):
                        sp.wait_ge(S["pv"], gi + 1)
                        sp.sem_clear(s_group[gi])
                        load_group(sp, nxt, gi)

                @block.scalar
                def _(act):
                    act.wait_ge(S["cx"], 1)
                    nc.scalar.activation(pc[:], pc[:], ACT.Exp, bias=st[:, 0:1], accum_out=st[:, 1:2]).then_inc(S["ce"], 1)
                    act.wait_ge(S["wx"], 1)
                    nc.scalar.activation(sw[:], sw[:], ACT.Exp, bias=wmax[:, 2:3], accum_out=wden[:, 0:1]).then_inc(S["we"], 1)
                    nc.scalar.activation(sn[:, 1], sn[:, 1], ACT.Exp, bias=wmax[:, 2:3], accum_out=wden[:, 1:2]).then_inc(S["we"], 1)
                    for gi in range(NG4):
                        act.wait_ge(S["tr"], gi + 1)
                        if gi >= 2:
                            act.wait_ge(S["sc"], gi - 1)
                        nc.scalar.activation(kT[:, gi % 2, :], bank[:, gi % 2, :], ACT.Copy).then_inc(S["kT"], 1)
                    act.wait_ge(S["mx"], NG4 + 2)
                    nc.scalar.activation(sn[:, 0], sn[:, 0], ACT.Exp, bias=st[:, 4:5], accum_out=gden[:, NG4:NG4 + 1]).then_inc(S["exp"], 1)
                    for gi in range(NG4):
                        cols = slice(gi * 512, (gi + 1) * 512)
                        nc.scalar.activation(s[:, cols], s[:, cols], ACT.Exp, bias=st[:, 4:5], accum_out=gden[:, gi:gi + 1]).then_inc(S["exp"], 1)
                    act.wait_ge(S["ob"], 6)
                    act.dma_start(d["os"][ds(b, 1)].rearrange("b m k x -> (b m) k x"), ob[:]).then_inc(S["st"], 16)
                    act.wait_ge(S["st"], 16)

                @block.tensor
                def _(pe):
                    ident = c["ident"]
                    pe.wait_ge(S["q"], 2)
                    nc.tensor.matmul(bank[:NQ, 4, 0:NBLK], q[:], kcT[:, ds(b, 1), :].rearrange("p b j -> p (b j)"), start=True, stop=True).then_inc(S["cs"], 1)
                    for j in range(2):
                        t = nc.tensor.matmul(bank[:NQ, 5, j * DT:(j + 1) * DT], q[:], kTs[:, j, ds(b * DT, DT)], start=True, stop=True)
                    t.then_inc(S["nk"], 1)
                    pe.wait_ge(S["new"], 48)
                    for i in range(WIN // P):
                        t = nc.tensor.transpose(bank[:, 6, i * P:(i + 1) * P], win[:, i, 0:KVW], ident[:])
                    t.then_inc(S["wt"], 1)
                    pe.wait_ge(S["wk"], 1)
                    nc.tensor.matmul(bank[:NQ, 7, :], q[:], kwin[:], start=True, stop=True).then_inc(S["ws"], 1)
                    pe.wait_ge(S["pc"], 1)
                    nc.tensor.matmul(bank[:NQ, 4, 0:NBLK], same[:], pc[:], start=True, stop=True).then_inc(S["imp"], 1)
                    for half in range(2):
                        t = nc.tensor.transpose(bank[:NPAGE, 6, half * NQ:(half + 1) * NQ], pc[:, half * NPAGE:(half + 1) * NPAGE], ident[:NQ, :NQ])
                    t.then_inc(S["imp"], 1)

                    def turn(gi):
                        pe.wait_ge(s_group[gi], 16 * GP)
                        if gi >= 2:
                            pe.wait_ge(S["kT"], gi - 1)
                        for j in range(GP):
                            t = nc.tensor.transpose(bank[:, gi % 2, j * P:(j + 1) * P], pg[:, GP * gi + j, 0:KVW], ident[:])
                        t.then_inc(S["tr"], 1)

                    turn(0)
                    for gi in range(NG4):
                        if gi + 1 < NG4:
                            turn(gi + 1)
                        pe.wait_ge(S["kT"], gi + 1)
                        if gi >= 2:
                            pe.wait_ge(S["s"], gi - 1)
                        nc.tensor.matmul(bank[:NQ, 2 + gi % 2, :], q[:], kT[:, gi % 2, :], start=True, stop=True).then_inc(S["sc"], 1)
                        if gi == 2:
                            pe.wait_ge(S["pcT"], 2)
                            for half in range(2):
                                t = nc.tensor.matmul(bank[:NQ, 4, 256:256 + KVW], pcT[:, half, :], vcb[:, half, :], start=half == 0, stop=half == 1)
                            t.then_inc(S["co"], 1)
                            pe.wait_ge(S["we"], 2)
                            for i in range(WIN // P):
                                nc.tensor.transpose(bank[:, 6, i * NQ:(i + 1) * NQ], sw[:, i * P:(i + 1) * P], ident[:NQ, :NQ])
                            nc.tensor.transpose(bank[:DT, 6, 256:256 + NQ], sn[:, 1], ident[:NQ, :NQ]).then_inc(S["wp"], 1)
                            pe.wait_ge(S["wpT"], 2)
                            for i in range(WIN // P):
                                nc.tensor.matmul(bank[:NQ, 7, 0:KVW], wT[:, i * NQ:(i + 1) * NQ], win[:, i, KVW:2 * KVW], start=i == 0, stop=False)
                            nc.tensor.matmul(bank[:NQ, 7, 0:KVW], pnT[:, 1, :], vnew[:, 1, :], start=False, stop=True).then_inc(S["wo"], 1)

                    def probs(gi):
                        pe.wait_ge(S["exp"], gi + 2)
                        if gi >= 2:
                            pe.wait_ge(S["pT"], gi - 1)
                        for j in range(GP):
                            t = nc.tensor.transpose(bank[:, gi % 2, j * NQ:(j + 1) * NQ], s[:, (GP * gi + j) * P:(GP * gi + j + 1) * P], ident[:NQ, :NQ])
                        t.then_inc(S["pt"], 1)

                    pe.wait_ge(S["exp"], 1)
                    nc.tensor.transpose(bank[:DT, 6, 0:NQ], sn[:, 0], ident[:NQ, :NQ]).then_inc(S["pt"], 1)
                    probs(0)
                    for gi in range(NG4):
                        if gi + 1 < NG4:
                            probs(gi + 1)
                        pe.wait_ge(S["pT"], gi + 2)
                        if gi == 0:
                            nc.tensor.matmul(bank[:NQ, 3, 0:KVW], pnT[:, 0, :], vnew[:, 0, :], start=True, stop=False)
                        for j in range(GP):
                            t = nc.tensor.matmul(bank[:NQ, 3, 0:KVW], pT[:, gi % 2, j * NQ:(j + 1) * NQ], pg[:, GP * gi + j, KVW:2 * KVW],
                                                 start=False, stop=gi == NG4 - 1 and j == GP - 1)
                        t.then_inc(S["pv"], 1)

                @block.vector
                def _(dve):
                    link = Chain(dve, S["dv"])
                    V = nc.vector

                    def output(branch, b_ix, r, col=0):
                        for gg in range(NG):
                            rows = slice(gg * NQ // 2, (gg + 1) * NQ // 2)
                            V.tensor_scalar(ob[rows, branch, :], bank[rows, b_ix, col + gg * HD:col + (gg + 1) * HD], r[rows], None, ALU.mult).then_inc(S["ob"], 1)

                    for gg in range(NG):
                        rows = slice(gg * HD, (gg + 1) * HD)
                        V.tensor_copy(q[rows, gg * NQ // 2:(gg + 1) * NQ // 2].rearrange("p (r t) -> p r t", t=DT), qall[rows, :, ds(b * DT, DT)]).then_inc(S["q"], 1)
                    dve.wait_ge(S["cs"], 1)
                    link(V.tensor_tensor(pc[:], bank[:NQ, 4, 0:NBLK], calibi[:], ALU.add))
                    V.tensor_reduce(st[:, 0:1], pc[:], AX, ALU.max, negate=True).then_inc(S["cx"], 1)
                    dve.wait_ge(S["nk"], 1)
                    link(V.tensor_tensor(sn[:], bank[:NQ, 5, 0:2 * DT].rearrange("p (j t) -> p j t", j=2), nalibi[:].unsqueeze(1).broadcast_to((NQ, 2, DT)), ALU.add))
                    dve.wait_ge(S["wt"], 1)
                    V.tensor_copy(kwin[:], bank[:, 6, :]).then_inc(S["wk"], 1)
                    dve.wait_ge(S["ce"], 1)
                    link(V.reciprocal(st[:, 2:3], st[:, 1:2]))
                    V.tensor_scalar(pc[:], pc[:], st[:, 2:3], None, ALU.mult).then_inc(S["pc"], 1)
                    dve.wait_ge(S["ws"], 1)
                    link(V.tensor_tensor(sw[:], bank[:NQ, 7, :], walibi[:], ALU.add))
                    link(V.tensor_reduce(wmax[:, 0:1], sw[:], AX, ALU.max))
                    link(V.tensor_reduce(wmax[:, 1:2], sn[:, 1], AX, ALU.max))
                    V.tensor_reduce(wmax[:, 2:3], wmax[:, 0:2], AX, ALU.max, negate=True).then_inc(S["wx"], 1)
                    dve.wait_ge(S["imp"], 2)
                    link(V.tensor_tensor(score[:, 0:NBLK].rearrange("p (j f) -> p f j", f=2), bank[:NQ, 4, 0:NBLK].rearrange("p (f j) -> p f j", f=2),
                                         bonus[:, 0:NBLK].rearrange("p (j f) -> p f j", f=2), ALU.add))
                    link(V.tensor_copy(score[:, NBLK:SEL], bonus[:, NBLK:SEL]))
                    link(V.max(top[:, 0], score[:]))
                    link(V.match_replace(out=left[:, 0], in_to_replace=top[:, 0], in_values=score[:], imm_value=NEG))
                    link(V.max(top[:, 1], left[:, 0]))
                    link(V.match_replace(out=left[:, 1], in_to_replace=top[:, 1], in_values=left[:, 0], imm_value=NEG))
                    link(V.tensor_scalar(selb[:], left[:, 1], NEG / 2, NEG, ALU.is_gt, ALU.mult))
                    link(V.tensor_tensor(selb[:], selb[:], balibi[:], ALU.add))
                    V.tensor_copy(vcb[:].rearrange("p f c -> p (f c)"), vc[:, ds(b, 1), :, :].rearrange("p b f c -> p (b f c)")).then_inc(S["pcT"], 1)
                    V.tensor_copy(pcT[:].rearrange("p f m -> p (f m)"), bank[:NPAGE, 6, 0:2 * NQ]).then_inc(S["pcT"], 1)
                    link(V.tensor_scalar(sn[:, 0], sn[:, 0], selb[:, NBLK:SEL], None, ALU.add))
                    for gi in range(NG4):
                        cols = s[:, gi * 512:(gi + 1) * 512]
                        dve.wait_ge(S["sc"], gi + 1)
                        V.tensor_tensor(cols.rearrange("p (n k) -> p n k", k=BLK), bank[:NQ, 2 + gi % 2, :].rearrange("p (n k) -> p n k", k=BLK),
                                        kalibi[:].unsqueeze(1).broadcast_to((NQ, 512 // BLK, BLK)), ALU.add).then_inc(S["s"], 1)
                        dve.wait_ge(S["s"], gi + 1)
                        link(V.tensor_tensor(cols.rearrange("p (n k) -> p n k", k=BLK), cols.rearrange("p (n k) -> p n k", k=BLK),
                                             selb[:, gi * 8:(gi + 1) * 8].unsqueeze(2).broadcast_to((NQ, 512 // BLK, BLK)), ALU.add))
                        V.tensor_reduce(gmax[:, gi:gi + 1], cols, AX, ALU.max).then_inc(S["mx"], 1)
                        if gi == 2:
                            dve.wait_ge(S["co"], 1)
                            for gg in range(NG):
                                rows = slice(gg * NQ // 2, (gg + 1) * NQ // 2)
                                V.tensor_copy(ob[rows, 0, :], bank[rows, 4, 256 + gg * HD:256 + (gg + 1) * HD]).then_inc(S["ob"], 1)
                            dve.wait_ge(S["wp"], 1)
                            V.tensor_copy(wT[:], bank[:, 6, 0:WIN // P * NQ]).then_inc(S["wpT"], 1)
                            V.tensor_copy(pnT[:, 1, :], bank[:DT, 6, 256:256 + NQ]).then_inc(S["wpT"], 1)
                            dve.wait_ge(S["we"], 2)
                            link(V.tensor_reduce(st[:, 5:6], wden[:], AX, ALU.add))
                            link(V.reciprocal(st[:, 6:7], st[:, 5:6]))
                            dve.wait_ge(S["wo"], 1)
                            output(2, 7, st[:, 6:7])
                    V.tensor_reduce(gmax[:, NG4:NG4 + 1], sn[:, 0], AX, ALU.max).then_inc(S["mx"], 1)
                    dve.wait_ge(S["mx"], NG4 + 1)
                    V.tensor_reduce(st[:, 4:5], gmax[:], AX, ALU.max, negate=True).then_inc(S["mx"], 1)
                    dve.wait_ge(S["pt"], 1)
                    V.tensor_copy(pnT[:, 0, :], bank[:DT, 6, 0:NQ]).then_inc(S["pT"], 1)
                    for gi in range(NG4):
                        dve.wait_ge(S["pt"], gi + 2)
                        if gi >= 2:
                            dve.wait_ge(S["pv"], gi - 1)
                        V.tensor_copy(pT[:, gi % 2, 0:GP * NQ], bank[:, gi % 2, 0:GP * NQ]).then_inc(S["pT"], 1)
                    dve.wait_ge(S["exp"], NG4 + 1)
                    link(V.tensor_reduce(st[:, 5:6], gden[:], AX, ALU.add))
                    link(V.reciprocal(st[:, 7:8], st[:, 5:6]))
                    dve.wait_ge(S["pv"], NG4)
                    output(1, 3, st[:, 7:8])
            next_iteration(nc, S.values())

        with nc.Block() as block:
            @block.sync
            def _(sp):
                for gi in range(NG4):
                    sp.wait_ge(s_group[gi], 16 * GP)


def odd_output(nc, a, d, c, o):
    gate, oall = o["gate"], o["oall"]
    bank = c["bank"]
    with ExitStack() as ctx:
        ctx.callback(nc.all_engine_barrier)
        def sb(name, shape):
            return ctx.enter_context(nc.sbuf_tensor(name, shape, F32))

        wo = sb("oo_wo", [P, KD, D_MODEL])
        gf = sb("oo_gf", [P, D_MODEL])
        z = sb("oo_z", [P, NW])
        x = sb("oo_x", [P, D_MODEL])
        m = sb("oo_m", [P, NW])
        mT = sb("oo_mT", [P, KD, P])
        y = sb("oo_y", [P, D_MODEL])
        os = sb("oo_os", [NS, 3, NH, HD])
        st = sb("oo_st", [P, 4])
        s_w = cleared(nc, ctx, "oo_s_w")
        s_os = cleared(nc, ctx, "oo_s_os")
        names = ["ld", "m", "T", "mT", "mm", "x2", "ss", "ms", "sd", "y", "st", "dv"]
        S = {n: cleared(nc, ctx, "oo_s_" + n) for n in names}

        with nc.Block() as block:
            @block.sync
            def _(sp):
                for k in range(KD):
                    sp.dma_start(wo[:, k], a["w_out_odd"][0, k * P:(k + 1) * P, :]).then_inc(s_w, 16)
                sp.dma_start(gf[:], a["norm_final"].partition_broadcast(P)).then_inc(s_w, 16)
                for b in range(DB):
                    for k in range(3):
                        sp.dma_start(os[DT * b:DT * (b + 1), k], d["os"][b, :, k, :].rearrange("(h t) x -> t h x", t=DT)).then_inc(s_os, 16)
                sp.wait_ge(s_w, 16 * (KD + 1))
                sp.wait_ge(s_os, 16 * 3 * DB)

        def tile(n, tok0, i, prompt):
            with nc.Block() as block:
                @block.sync
                def _(sp):
                    sp.dma_start(z[:n], d["z"][ds(tok0, n), :]).then_inc(S["ld"], 16)
                    sp.dma_start(x[:n], d["x1"][ds(tok0, n), :]).then_inc(S["ld"], 16)
                    sp.wait_ge(S["y"], 1)
                    dst = a["o_y_prompt"][0, ds(tok0, n), :] if prompt else a["o_y_sample"].rearrange("b t d -> (b t) d")
                    sp.dma_start(dst, y[:n]).then_inc(S["st"], 16)
                    sp.wait_ge(S["st"], 16)

                @block.tensor
                def _(pe):
                    pe.wait_ge(S["m"], 1)
                    for k in range(KD):
                        t = nc.tensor.transpose(bank[:, k // 4, (k % 4) * n:(k % 4 + 1) * n], m[:n, k * P:(k + 1) * P], c["ident"][:n, :n])
                    t.then_inc(S["T"], 1)
                    pe.wait_ge(S["mT"], 2)
                    for hf in range(2):
                        for k in range(KD):
                            t = nc.tensor.matmul(bank[:n, 2 + hf, :], mT[:, k, :n], wo[:, k, hf * 512:(hf + 1) * 512], start=k == 0, stop=k == KD - 1)
                        t.then_inc(S["mm"], 1)

                @block.scalar
                def _(act):
                    act.wait_ge(S["x2"], 2)
                    nc.scalar.activation(y[:n], x[:n], ACT.Square, accum_out=st[:n, 0:1]).then_inc(S["ss"], 1)
                    act.wait_ge(S["ms"], 1)
                    nc.scalar.activation(st[:n, 2:3], st[:n, 1:2], ACT.Sqrt).then_inc(S["sd"], 1)

                @block.vector
                def _(dve):
                    link = Chain(dve, S["dv"])
                    V = nc.vector
                    if not prompt:
                        gs = gate[:NS, NTILE, :].rearrange("p (k h) -> p k h", k=3)
                        for k in range(3):
                            link(V.tensor_tensor(os[:, k], os[:, k], gs[:, k].unsqueeze(2).broadcast_to((NS, NH, HD)), ALU.mult))
                        link(V.tensor_tensor(os[:, 0], os[:, 0], os[:, 1], ALU.add))
                        link(V.tensor_tensor(os[:, 0], os[:, 0], os[:, 2], ALU.add))
                    dve.wait_ge(S["ld"], 32)
                    src = oall[:, ds(i, 1), :].rearrange("p i c -> p (i c)") if prompt else os[:, 0].rearrange("p h x -> p (h x)")
                    V.tensor_tensor(m[:n], src, z[:n], ALU.mult).then_inc(S["m"], 1)
                    dve.wait_ge(S["T"], 1)
                    for b in range(2):
                        V.tensor_copy(mT[:, 4 * b:4 * b + 4, :n], bank[:, b, :4 * n].rearrange("p (k t) -> p k t", k=4)).then_inc(S["mT"], 1)
                    for hf in range(2):
                        dve.wait_ge(S["mm"], hf + 1)
                        cols = slice(hf * 512, (hf + 1) * 512)
                        V.tensor_tensor(x[:n, cols], x[:n, cols], bank[:n, 2 + hf, :], ALU.add).then_inc(S["x2"], 1)
                    dve.wait_ge(S["ss"], 1)
                    V.tensor_scalar(st[:n, 1:2], st[:n, 0:1], 1.0 / D_MODEL, EPS, ALU.mult, ALU.add).then_inc(S["ms"], 1)
                    dve.wait_ge(S["sd"], 1)
                    link(V.reciprocal(st[:n, 3:4], st[:n, 2:3]))
                    dve.wait_ge(S["x2"], 2)
                    V.scalar_tensor_tensor(out=y[:n], in0=x[:n], scalar=st[:n, 3:4], in1=gf[:n], op0=ALU.mult, op1=ALU.mult).then_inc(S["y"], 1)

        with nc.Fori(0, NTILE) as i:
            tile(P, i * P, i, True)
            next_iteration(nc, S.values())
        tile(NS, SEQ, NTILE, False)


def build(nc, a):
    d = {
        "u": nc.dram_tensor("u_scratch", [SW, CH, NCH], F32, kind="Internal").ap(),
        "us": nc.dram_tensor("us_scratch", [SW, DT, DB], F32, kind="Internal").ap(),
        "y": nc.dram_tensor("y_scratch", [SW, CH, NCH], F32, kind="Internal").ap(),
        "ys": nc.dram_tensor("ys_scratch", [SW, DT, DB], F32, kind="Internal").ap(),
        "z": nc.dram_tensor("z_scratch", [NTOK, NW], F32, kind="Internal").ap(),
        "qT": nc.dram_tensor("qT_scratch", [NW, NTOK], F32, kind="Internal").ap(),
        "os": nc.dram_tensor("os_scratch", [DB, NH * DT, 3, HD], F32, kind="Internal").ap(),
        "x1": nc.dram_tensor("x1_scratch", [NTOK, D_MODEL], F32, kind="Internal").ap(),
    }
    with ExitStack() as ctx:
        def sb(name, shape, dt=F32):
            return ctx.enter_context(nc.sbuf_tensor(name, shape, dt))

        c = {"ident": sb("ident", [P, P]), "causal": sb("causal", [P, P]), "winlow": sb("winlow", [P, P]),
             "pages": sb("pages", [1, DB * NPAGE], I32),
             "bank": ctx.enter_context(nc.psum_tensor("bank", [P, 8, 512], F32))}
        load_constants(nc, a, c)
        with ExitStack() as even:
            def ev(name, shape):
                return even.enter_context(nc.sbuf_tensor(name, shape, F32))

            act_t = {"zaT": ev("zaT", [P, 4, NTOK]), "zbT": ev("zbT", [P, 4, NTOK]), "cqT": ev("cqT", [P, 3, NTOK]),
                     "ckvT": ev("ckvT", [P, 2, NTOK]), "krT": ev("krT", [P, NTOK]), "oa": ev("oa", [P, NTILE + 1, MW]),
                     "qlat": ev("qlat", [P, 2, MH, NS]), "qrope": ev("qrope", [P, MH, NS])}
            even_projection(nc, a, d, c, act_t)
            mla_prompt(nc, a, d, c, act_t)
            mla_sample(nc, a, d, c, act_t)
            with ExitStack() as s5:
                def sm(name, shape):
                    return s5.enter_context(nc.sbuf_tensor(name, shape, F32))

                m = {"out": sm("m_out", [P, 2, NPAIR, CH + 1, SC]), "binT": sm("m_binT", [P, 2, NPAIR, P]),
                     "toep": sm("m_toep", [P, SG, P]), "rot": sm("m_rot", [P, 2, NPAIR]), "l8": sm("m_l8", [P, NPAIR]),
                     "l4": sm("m_l4", [P, 2, NPAIR])}
                hlast = sm("m_hlast", [P, 2, NPAIR])
                s5_matrices(nc, a, d, c, m)
                s5_prompt(nc, a, d, c, m, hlast)
                s5_sample(nc, a, d, c, m, hlast)
            even_output(nc, a, d, c, act_t)
        with ExitStack() as odd:
            def od(name, shape):
                return odd.enter_context(nc.sbuf_tensor(name, shape, F32))

            o = {"gate": od("gate", [P, NTILE + 1, 3 * NH]), "kTs": od("kTs", [P, 2, NS]), "kcT": od("kcT", [P, DB, NBLK]),
                 "vc": od("vc", [NPAGE, DB, 2, KVW])}
            with ExitStack() as keys:
                def ky(name, shape):
                    return keys.enter_context(nc.sbuf_tensor(name, shape, F32))

                o.update(kv=ky("kv", [P, NTILE, 6 * KVW]), ksT=ky("ksT", [P, NG, SEQ]), kwT=ky("kwT", [P, NG, SEQ]),
                         kcp=ky("kcp", [P, NG, 2 * NTILE]), vcp=ky("vcp", [2 * NTILE, NG * HD]))
                odd_projection(nc, a, d, c, o)
                compress(nc, a, d, c, o)
                o["oall"] = odd.enter_context(nc.sbuf_tensor("oall", [P, NTILE, NW], F32, side="right"))
                nsa_prompt(nc, a, d, c, o)
            nsa_sample(nc, a, d, c, o)
            odd_output(nc, a, d, c, o)


def constants():
    f = np.float32
    i = np.arange(P)
    pos = np.concatenate([np.arange(SEQ), np.tile(PAST + np.arange(DT), DB)]).astype(f)
    half = ROPE // 2
    inv = (f(10000.0) ** (-np.arange(half, dtype=f) / half)).astype(f)
    ang = (pos[:, None] * inv[None]).astype(f)
    cos, sin = np.cos(ang).astype(f), np.sin(ang).astype(f)
    slope = (f(2.0) ** (f(-8.0) * np.arange(1, NH + 1, dtype=f) / f(NH))).astype(f)
    step = np.arange(DT)
    cpos = ((2 * np.arange(NTILE)[None] + np.arange(2)[:, None]) * BLK + BLK - 1).reshape(-1)
    cpast = ((2 * np.arange(NPAGE)[None] + np.arange(2)[:, None]) * BLK + BLK - 1).reshape(-1)
    qpos = np.arange(NTILE)[None, :, None] * P + i[:, None, None]
    rs = np.repeat(slope, DT)[:, None]
    rt = np.tile(step, NH)[:, None]
    rg = np.repeat(np.arange(NG), NR * DT)[:, None]
    bonus = np.zeros((NH * DT, NBLK + 1), f)
    bonus[:, [0, NBLK - 1, NBLK]] = NR + 1
    w = np.arange(WIN)[None]
    return {
        "c_ident": np.eye(P, dtype=f),
        "c_causal": np.where(i[None] > i[:, None], f(NEG), f(0)).astype(f),
        "c_winlow": np.where(i[None] < i[:, None], f(NEG), f(0)).astype(f),
        "c_rope": np.stack([cos, sin], 1),
        "c_rope_cosT": np.concatenate([cos.T, cos.T]),
        "c_rope_sinT": np.concatenate([-sin.T, sin.T]),
        "c_mla_new": np.tile(np.where(step[None] > step[:, None], f(NEG), f(0)).astype(f), (MH, 1)),
        "c_slope": np.repeat(slope[:, None], SEQ, 1),
        "c_kpos": (np.arange(SEQ, dtype=f) - SEQ)[None],
        "c_cpos": (cpos - SEQ).astype(f)[None],
        "c_cmask": np.where(cpos[None, None] <= qpos, f(0), f(NEG)).astype(f),
        "c_calibi": (rs * (cpast - PAST)[None]).astype(f),
        "c_bonus": bonus,
        "c_balibi": (rs * (np.arange(NBLK + 1) * BLK - PAST)[None]).astype(f),
        "c_kalibi": (rs * np.arange(BLK)[None]).astype(f),
        "c_nalibi": np.where(step[None] <= rt, rs * step[None], NEG).astype(f),
        "c_walibi": np.where(w >= rt, rs * (w - WIN), NEG).astype(f),
        "c_same": ((rg == rg.T) & (rt == rt.T)).astype(f),
    }


INPUTS = ["x_prompt", "x_sample", "cache_mla", "state_s5", "cache_nsa_kv", "state_nsa_win", "page_table",
          "norm_even", "w_in_even", "mla_g_q", "mla_g_kv", "mla_w_uq", "mla_w_uk", "mla_w_uv",
          "s5_lambda_re", "s5_lambda_im", "s5_log_dt", "s5_b_re", "s5_b_im", "s5_c_re", "s5_c_im", "s5_d",
          "s5_w_glu", "s5_b_glu", "w_out_even", "norm_odd", "w_in_odd", "nsa_pe_k", "nsa_pe_v",
          "nsa_phi1_k", "nsa_phi2_k", "nsa_phi1_v", "nsa_phi2_v", "w_out_odd", "norm_final"]
OUTPUTS = {"y_prompt": (1, SEQ, D_MODEL), "y_sample": (DB, DT, D_MODEL), "mla_rows_prompt": (1, 1, SEQ, ROW),
           "mla_rows_sample": (1, DB, DT, ROW), "s5_state_prompt": (1, 1, SG, SN, 2), "s5_state_sample": (1, DB, SG, SN, 2),
           "nsa_rows_prompt": (1, 1, SEQ, 4, NG, HD), "nsa_rows_sample": (1, DB, DT, 4, NG, HD),
           "nsa_win_prompt": (1, 1, WIN, 2, NG, HD), "nsa_win_sample": (1, DB, WIN, 2, NG, HD)}


def kernel(**inputs):
    import concourse.bacc as bacc
    from concourse.bass_utils import run_bass_kernel_spmd

    nc = bacc.Bacc("TRN2", target_bir_lowering=False, num_devices=1)
    arrays = {name: np.ascontiguousarray(inputs[name]) for name in INPUTS}
    for name, table in constants().items():
        arrays[name] = np.ascontiguousarray(table)
    a = {name: nc.dram_tensor(name, x.shape, mybir.dt.from_np(x.dtype), kind="ExternalInput").ap() for name, x in arrays.items()}
    for name, shape in OUTPUTS.items():
        a["o_" + name] = nc.dram_tensor("o_" + name, shape, F32, kind="ExternalOutput").ap()
    build(nc, a)
    result = run_bass_kernel_spmd(nc, [arrays], core_ids=[0]).results[0]
    return tuple(result["o_" + name] for name in OUTPUTS)
```

```python
from contextlib import ExitStack

import numpy as np

import concourse.bass as bass
import concourse.mybir as mybir

F32 = mybir.dt.float32
I32 = mybir.dt.int32
ALU = mybir.AluOpType
ACT = mybir.ActivationFunctionType
AX = mybir.AxisListType.X
ds = bass.ds

P = 128
D_MODEL, SEQ, DB, DT = 1024, 1024, 8, 4
NS = DB * DT
NTOK = SEQ + NS
NTILE = SEQ // P
KD = D_MODEL // P
PAST, PAGE = 8192, 128
NPAGE = PAST // PAGE
POOL = (DB * NPAGE * 5 + 3) // 4
EPS = 1e-6
NEG = -1e30

MH, NOPE, ROPE, MV = 8, 64, 32, 64
QL, KVL = 384, 256
ROW = KVL + ROPE
QD = NOPE + ROPE
MLA_SCALE = QD ** -0.5
LOW = QL + KVL + ROPE
MW, SW = MH * MV, 512
EVEN_IN = LOW + MW + 2 * SW

SG, SC, SN = 32, 16, 64
CH = 8
NCH = SEQ // CH
NPAIR = SG // 2

NH, NG, HD = 16, 2, 64
NR = NH // NG
HQ = HD + 32
NW = NH * HD
KVW = NG * HD
ODD_TOK = 6 * KVW + 3 * NH + NW
ODD_IN = NW + ODD_TOK
NSA_SCALE = HD ** -0.5
BLK, WIN = 64, 512
NBLK = PAST // BLK


class Chain:

    def __init__(self, engine, sem):
        self.engine, self.sem, self.n = engine, sem, 0

    def __call__(self, ins):
        self.n += 1
        ins.then_inc(self.sem, 1)
        self.engine.wait_ge(self.sem, self.n)


def next_iteration(nc, sems):
    for s in sems:
        nc.gpsimd.sem_clear(s)
    nc.all_engine_barrier()


def cleared(nc, ctx, name):
    sem = ctx.enter_context(nc.semaphore(name))
    ctx.callback(nc.gpsimd.sem_clear, sem)
    return sem


def load_constants(nc, a, c):
    with ExitStack() as ctx:
        ctx.callback(nc.all_engine_barrier)
        s_load = cleared(nc, ctx, "s_const")
        block = ctx.enter_context(nc.Block())

        @block.sync
        def _(sp):
            sp.dma_start(c["ident"][:], a["c_ident"]).then_inc(s_load, 16)
            sp.dma_start(c["causal"][:], a["c_causal"]).then_inc(s_load, 16)
            sp.dma_start(c["winlow"][:], a["c_winlow"]).then_inc(s_load, 16)
            sp.dma_start(c["pages"][:], a["page_table"].rearrange("b p -> (b p)").unsqueeze(0)).then_inc(s_load, 16)
            sp.wait_ge(s_load, 64)


class TilePrep:

    def __init__(self, nc, c, S, x, h, hT, st, g):
        self.nc, self.c, self.S, self.x, self.h, self.hT, self.st, self.g = nc, c, S, x, h, hT, st, g

    def load(self, sp, n, src):
        sp.dma_start(self.x[:n], src).then_inc(self.S["x"], 16)

    def squares(self, act, n):
        nc, S, st = self.nc, self.S, self.st
        act.wait_ge(S["x"], 16)
        nc.scalar.activation(self.h[:n], self.x[:n], ACT.Square, accum_out=st[:n, 0:1]).then_inc(S["ss"], 1)
        act.wait_ge(S["ms"], 1)
        nc.scalar.activation(st[:n, 2:3], st[:n, 1:2], ACT.Sqrt).then_inc(S["sd"], 1)

    def norm(self, dve, n):
        nc, S, st = self.nc, self.S, self.st
        dve.wait_ge(S["ss"], 1)
        nc.vector.tensor_scalar(st[:n, 1:2], st[:n, 0:1], 1.0 / D_MODEL, EPS, ALU.mult, ALU.add).then_inc(S["ms"], 1)
        dve.wait_ge(S["sd"], 1)
        nc.vector.reciprocal(st[:n, 3:4], st[:n, 2:3]).then_inc(S["rs"], 1)
        dve.wait_ge(S["rs"], 1)
        nc.vector.tensor_scalar(self.h[:n], self.x[:n], st[:n, 3:4], None, ALU.mult).then_inc(S["rs"], 1)

    def turn(self, pe, n):
        nc, S = self.nc, self.S
        pe.wait_ge(S["rs"], 2)
        for k in range(KD):
            t = nc.tensor.transpose(self.c["bank"][:, k // 4, (k % 4) * n:(k % 4 + 1) * n], self.h[:n, k * P:(k + 1) * P], self.c["ident"][:n, :n])
        t.then_inc(S["T"], 1)

    def turned(self, dve, n):
        nc, S = self.nc, self.S
        dve.wait_ge(S["T"], 1)
        for b in range(2):
            nc.vector.tensor_tensor(self.hT[:, 4 * b:4 * b + 4, :n], self.c["bank"][:, b, :4 * n].rearrange("p (k t) -> p k t", k=4),
                                    self.g[:, 4 * b:4 * b + 4].unsqueeze(2).broadcast_to((P, 4, n)), ALU.mult).then_inc(S["hT"], 1)

    def alone(self, n, src):
        nc, S = self.nc, self.S
        with nc.Block() as block:
            @block.sync
            def _(sp):
                self.load(sp, n, src)

            @block.scalar
            def _(act):
                self.squares(act, n)

            @block.tensor
            def _(pe):
                self.turn(pe, n)

            @block.vector
            def _(dve):
                self.norm(dve, n)
                self.turned(dve, n)
        next_iteration(nc, S.values())


def even_projection(nc, a, d, c, act_t):
    zaT, zbT, cqT, ckvT, krT = (act_t[k] for k in ("zaT", "zbT", "cqT", "ckvT", "krT"))
    with ExitStack() as ctx:
        ctx.callback(nc.all_engine_barrier)
        def sb(name, shape):
            return ctx.enter_context(nc.sbuf_tensor(name, shape, F32))

        w = sb("ev_w", [P, KD, EVEN_IN])
        g = sb("ev_g", [P, KD])
        gq = sb("ev_gq", [P, QL // P])
        gkv = sb("ev_gkv", [P, KVL])
        x = sb("ev_x", [P, D_MODEL])
        h = sb("ev_h", [P, D_MODEL])
        hT = sb("ev_hT", [P, KD, P])
        low = sb("ev_low", [P, LOW])
        cqn = sb("ev_cqn", [P, QL])
        rows = sb("ev_rows", [P, ROW])
        uS = sb("ev_uS", [P, 4, P])
        trig = sb("ev_trig", [P, 2, ROPE // 2])
        rt = sb("ev_rt", [P, 4, ROPE // 2])
        st = sb("ev_st", [P, 8])
        s_w = cleared(nc, ctx, "ev_s_w")
        names = ["x", "ss", "ms", "sd", "rs", "T", "hT", "tok", "fm", "low", "ss2", "cqn", "rows", "T2", "u", "out", "dv", "ac", "trig", "ms2", "sd2"]
        S = {n: cleared(nc, ctx, "ev_s_" + n) for n in names}
        bank = c["bank"]

        with nc.Block() as block:
            @block.sync
            def _(sp):
                for k in range(KD):
                    sp.dma_start(w[:, k, :], a["w_in_even"][0, k * P:(k + 1) * P, :]).then_inc(s_w, 16)
                sp.dma_start(g[:], a["norm_even"][0].rearrange("(k p) -> p k", p=P), allow_slow_non_contiguous=True).then_inc(s_w, 16)
                sp.dma_start(gq[:], a["mla_g_q"][0].rearrange("(k p) -> p k", p=P), allow_slow_non_contiguous=True).then_inc(s_w, 16)
                sp.dma_start(gkv[:], a["mla_g_kv"][0].partition_broadcast(P)).then_inc(s_w, 16)
                sp.wait_ge(s_w, 16 * (KD + 3))

        prep = TilePrep(nc, c, S, x, h, hT, st, g)

        def x_rows(n, tok0, prompt):
            return a["x_prompt"][0, ds(tok0, n), :] if prompt else a["x_sample"].rearrange("b t d -> (b t) d")

        def tile(n, tok0, prompt, i, following=None):
            with nc.Block() as block:
                @block.sync
                def _(sp):
                    sp.dma_start(trig[:n], a["c_rope"][ds(tok0, n)]).then_inc(S["trig"], 16)
                    if prompt:
                        prep.load(sp, P, following(sp))
                    sp.wait_ge(S["rows"], 1)
                    dst = a["o_mla_rows_prompt"][0, 0, ds(tok0, n), :] if prompt else a["o_mla_rows_sample"][0].rearrange("b t r -> (b t) r")
                    sp.dma_start(dst, rows[:n]).then_inc(S["out"], 16)
                    sp.wait_ge(S["u"], 4)
                    for e in range(4):
                        if prompt:
                            dst = d["u"][ds(P * e, P), :, ds(i * (P // CH), P // CH)]
                            sp.dma_start(dst, uS[:, e, :].rearrange("p (j k) -> p j k", j=CH)).then_inc(S["out"], 16)
                        else:
                            sp.dma_start(d["us"][P * e:P * (e + 1)], uS[:, e, :n].rearrange("p (t b) -> p t b", t=DT)).then_inc(S["out"], 16)
                    sp.wait_ge(S["out"], 16 * 5)

                @block.scalar
                def _(act):
                    if prompt:
                        prep.squares(act, P)
                    act.wait_ge(S["low"], 2)
                    nc.scalar.activation(cqn[:n], low[:n, 0:QL], ACT.Square, accum_out=st[:n, 4:5]).then_inc(S["ss2"], 1)
                    nc.scalar.activation(rows[:n, 0:KVL], low[:n, QL:QL + KVL], ACT.Square, accum_out=st[:n, 5:6]).then_inc(S["ss2"], 1)
                    act.wait_ge(S["ms2"], 1)
                    nc.scalar.activation(st[:n, 4:6], st[:n, 6:8], ACT.Sqrt).then_inc(S["sd2"], 1)
                    act.wait_ge(S["fm"], 3)
                    nc.scalar.activation(zaT[:, :, ds(tok0, n)], bank[:, 4, :4 * n].rearrange("p (e t) -> p e t", e=4), ACT.Silu).then_inc(S["ac"], 1)
                    nc.scalar.activation(zbT[:, :, ds(tok0, n)], bank[:, 6, :4 * n].rearrange("p (e t) -> p e t", e=4), ACT.Silu).then_inc(S["ac"], 1)

                @block.tensor
                def _(pe):
                    for b, (lo, hi) in ((2, (0, 512)), (3, (512, LOW))):
                        for k in range(KD):
                            t = nc.tensor.matmul(bank[:n, b, 0:hi - lo], hT[:, k, :n], w[:, k, lo:hi], start=k == 0, stop=k == KD - 1)
                    t.then_inc(S["tok"], 1)
                    for part in range(3):
                        for e in range(4):
                            col = LOW + 512 * part + P * e
                            for k in range(KD):
                                t = nc.tensor.matmul(bank[:, 4 + part, e * n:(e + 1) * n], w[:, k, col:col + P], hT[:, k, :n], start=k == 0, stop=k == KD - 1)
                        t.then_inc(S["fm"], 1)
                        if prompt and part == 1:
                            prep.turn(pe, P)
                    pe.wait_ge(S["cqn"], 1)
                    for k in range(QL // P):
                        t = nc.tensor.transpose(bank[:, 7, k * n:(k + 1) * n], cqn[:n, k * P:(k + 1) * P], c["ident"][:n, :n])
                    pe.wait_ge(S["rows"], 1)
                    for k in range(2):
                        t = nc.tensor.transpose(bank[:, 2, k * n:(k + 1) * n], rows[:n, k * P:(k + 1) * P], c["ident"][:n, :n])
                    t = nc.tensor.transpose(bank[:QD, 2, 2 * n:3 * n], rows[:n, ROW - QD:ROW], c["ident"][:n, :n])
                    t.then_inc(S["T2"], 1)

                @block.vector
                def _(dve):
                    link = Chain(dve, S["dv"])
                    if prompt:
                        prep.norm(dve, P)
                    dve.wait_ge(S["tok"], 1)
                    nc.vector.tensor_copy(low[:n, 0:512], bank[:n, 2, :]).then_inc(S["low"], 1)
                    nc.vector.tensor_copy(low[:n, 512:LOW], bank[:n, 3, 0:LOW - 512]).then_inc(S["low"], 1)
                    dve.wait_ge(S["ss2"], 2)
                    link(nc.vector.tensor_scalar(st[:n, 6:7], st[:n, 4:5], 1.0 / QL, EPS, ALU.mult, ALU.add))
                    nc.vector.tensor_scalar(st[:n, 7:8], st[:n, 5:6], 1.0 / KVL, EPS, ALU.mult, ALU.add).then_inc(S["ms2"], 1)
                    dve.wait_ge(S["low"], 2)
                    dve.wait_ge(S["trig"], 16)
                    hr = ROPE // 2
                    x1, x2 = low[:n, QL + KVL:QL + KVL + hr], low[:n, QL + KVL + hr:LOW]
                    nc.vector.tensor_tensor(rt[:n, 0], x1, trig[:n, 0], ALU.mult)
                    nc.vector.tensor_tensor(rt[:n, 1], x2, trig[:n, 1], ALU.mult)
                    nc.vector.tensor_tensor(rt[:n, 2], x1, trig[:n, 1], ALU.mult)
                    link(nc.vector.tensor_tensor(rt[:n, 3], x2, trig[:n, 0], ALU.mult))
                    nc.vector.tensor_tensor(rows[:n, KVL:KVL + hr], rt[:n, 0], rt[:n, 1], ALU.subtract)
                    link(nc.vector.tensor_tensor(rows[:n, KVL + hr:ROW], rt[:n, 2], rt[:n, 3], ALU.add))
                    dve.wait_ge(S["sd2"], 1)
                    link(nc.vector.reciprocal(st[:n, 6:8], st[:n, 4:6]))
                    nc.vector.tensor_scalar(cqn[:n], low[:n, 0:QL], st[:n, 6:7], None, ALU.mult).then_inc(S["cqn"], 1)
                    nc.vector.scalar_tensor_tensor(out=rows[:n, 0:KVL], in0=low[:n, QL:QL + KVL], scalar=st[:n, 7:8],
                                                   in1=gkv[:n], op0=ALU.mult, op1=ALU.mult).then_inc(S["rows"], 1)
                    dve.wait_ge(S["fm"], 2)
                    for e in range(4):
                        src = bank[:, 5, e * n:(e + 1) * n]
                        if prompt:
                            nc.vector.tensor_copy(uS[:, e, :].rearrange("p (j k) -> p j k", j=CH), src.rearrange("p (k j) -> p j k", j=CH)).then_inc(S["u"], 1)
                        else:
                            nc.vector.tensor_copy(uS[:, e, :n].rearrange("p (t b) -> p t b", t=DT), src.rearrange("p (b t) -> p t b", t=DT)).then_inc(S["u"], 1)
                    if prompt:
                        dve.wait_ge(S["fm"], 3)
                        prep.turned(dve, P)
                    dve.wait_ge(S["T2"], 1)
                    nc.vector.tensor_tensor(cqT[:, :, ds(tok0, n)], bank[:, 7, :3 * n].rearrange("p (k t) -> p k t", k=3),
                                            gq[:].unsqueeze(2).broadcast_to((P, 3, n)), ALU.mult)
                    nc.vector.tensor_copy(ckvT[:, :, ds(tok0, n)], bank[:, 2, :2 * n].rearrange("p (k t) -> p k t", k=2))
                    link(nc.vector.tensor_copy(krT[NOPE:QD, ds(tok0, n)], bank[NOPE:QD, 2, 2 * n:3 * n]))

        prep.alone(P, x_rows(P, 0, True))
        with nc.Fori(0, NTILE) as i:
            tile(P, i * P, True, i, lambda sp: x_rows(P, sp.snap((i + 1) % NTILE) * P, True))
            next_iteration(nc, S.values())
        prep.alone(NS, x_rows(NS, 0, False))
        tile(NS, SEQ, False, None)


def attention(nc, c, block, S, buf, units, qT, kdim):
    bank = c["bank"]
    p, pT, nmax, den, rden = (buf[k] for k in ("p", "pT", "nmax", "den", "rden"))
    n = len(units)
    side = buf.get("side", {})

    def width(u):
        return units[u]["nblk"] * P

    def scores_ps(u):
        return bank[:, 2 * (u % 2):2 * (u % 2) + 2, :].rearrange("p a b -> p (a b)")

    pT_ps = bank[:, 4:6, :].rearrange("p a b -> p (a b)")

    def o_ps(u):
        return bank[:, 6, (u % 2) * HD:(u % 2 + 1) * HD]

    @block.tensor
    def _(pe):
        def scores(u):
            unit = units[u]
            if buf["qk_ready"]:
                pe.wait_ge(S["qk"], buf["qk_ready"])
            if u >= 2:
                pe.wait_ge(S["exp"], u - 1)
            w = width(u)
            for lo in range(0, w, 512):
                hi = min(w, lo + 512)
                t = nc.tensor.matmul(scores_ps(u)[:, lo:hi], qT[:kdim, unit["q0"]:unit["q0"] + P], unit["kT"][:, lo:hi], start=True, stop=True)
            t.then_inc(S["sc"], 1)

        def values(u):
            unit = units[u]
            pe.wait_ge(S["exp"], u + 1)
            if u >= 1:
                pe.wait_ge(S["pT"], u)
            for b in range(unit["nblk"]):
                t = nc.tensor.transpose(pT_ps[:, b * P:(b + 1) * P], p[:, u % 2, b * P:(b + 1) * P], c["ident"][:])
            t.then_inc(S["tr"], 1)

        def weighted(u):
            unit = units[u]
            pe.wait_ge(S["pT"], u + 1)
            if u >= 1:
                pe.wait_ge(S["o"], u)
            for lo in range(0, P, HD):
                for b in range(unit["nblk"]):
                    t = nc.tensor.matmul(o_ps(u)[lo:lo + HD], pT[:, u % 2, b * P + lo:b * P + lo + HD], unit["v"](b), start=b == 0, stop=b == unit["nblk"] - 1)
            t.then_inc(S["pv"], 1)

        buf["pe_before"](pe)
        scores(0)
        for u in range(n):
            if ("pe", u) in side:
                side["pe", u](pe)
            if u + 1 < n:
                scores(u + 1)
            values(u)
            if u >= 1:
                weighted(u - 1)
        weighted(n - 1)

    @block.scalar
    def _(act):
        for u in range(n):
            act.wait_ge(S["mx"], u + 1)
            if u >= 2:
                act.wait_ge(S["tr"], u - 1)
                act.wait_ge(S["rd"], u - 1)
            nc.scalar.activation(p[:, u % 2, :width(u)], scores_ps(u)[:, :width(u)], ACT.Exp, bias=nmax[:, u % 2:u % 2 + 1],
                                 accum_out=den[:, u % 2:u % 2 + 1]).then_inc(S["exp"], 1)
            if ("act", u) in side:
                side["act", u](act)

    @block.vector
    def _(dve):
        link = Chain(dve, S["dv"])

        def maximum(u):
            dve.wait_ge(S["sc"], u + 1)
            for lo, m in units[u]["masks"]:
                link(nc.vector.tensor_tensor(scores_ps(u)[:, lo:lo + P], scores_ps(u)[:, lo:lo + P], m, ALU.add))
            nc.vector.tensor_reduce(nmax[:, u % 2:u % 2 + 1], scores_ps(u)[:, :width(u)], AX, ALU.max, negate=True).then_inc(S["mx"], 1)

        def turned(u):
            dve.wait_ge(S["exp"], u + 1)
            if u >= 2:
                dve.wait_ge(S["o"], u - 1)
            nc.vector.reciprocal(rden[:, u % 2:u % 2 + 1], den[:, u % 2:u % 2 + 1]).then_inc(S["rd"], 1)
            dve.wait_ge(S["tr"], u + 1)
            if u >= 2:
                dve.wait_ge(S["pv"], u - 1)
            nc.vector.tensor_copy(pT[:, u % 2, :width(u)], pT_ps[:, :width(u)]).then_inc(S["pT"], 1)

        def out(u):
            dve.wait_ge(S["pv"], u + 1)
            dve.wait_ge(S["rd"], u + 1)
            units[u]["finish"](o_ps(u), rden[:, u % 2:u % 2 + 1], link).then_inc(S["o"], 1)

        buf["dve_before"](dve, link)
        maximum(0)
        for u in range(n):
            if ("dve", u) in side:
                side["dve", u](dve, link)
            if u + 1 < n:
                maximum(u + 1)
            turned(u)
            if u >= 1:
                out(u - 1)
        out(n - 1)
        dve.wait_ge(S["o"], n)


ATT_SEMS = ["qk", "sc", "mx", "exp", "tr", "rd", "pT", "pv", "o", "dv"]


def mla_prompt(nc, a, d, c, act_t):
    cqT, ckvT, krT, oa, qlat, qrope = (act_t[k] for k in ("cqT", "ckvT", "krT", "oa", "qlat", "qrope"))
    bank = c["bank"]
    with ExitStack() as ctx:
        ctx.callback(nc.all_engine_barrier)
        def sb(name, shape):
            return ctx.enter_context(nc.sbuf_tensor(name, shape, F32))

        cosT = sb("mp_cos", [P, NTOK])
        sinT = sb("mp_sin", [P, NTOK])
        rt = sb("mp_rt", [P, 2, 512])
        wq = sb("mp_wq", [P, 3, QD + ROPE])
        wk = sb("mp_wk", [P, 2, NOPE])
        wkT = sb("mp_wkT", [NOPE, 2, P])
        wv = sb("mp_wv", [P, 2, MV])
        qT = sb("mp_qT", [P, NTOK])
        v = sb("mp_v", [P, NTILE, MV])
        buf = {"p": sb("mp_p", [P, 2, SEQ]), "pT": sb("mp_pT", [P, 2, SEQ]), "nmax": sb("mp_nmax", [P, 2]),
               "den": sb("mp_den", [P, 2]), "rden": sb("mp_rden", [P, 2])}
        S = {n: cleared(nc, ctx, "mp_s_" + n) for n in ["tab", "w", "pre", "ev"] + ATT_SEMS}
        half = ROPE // 2

        with nc.Block() as block:
            @block.sync
            def _(sp):
                sp.dma_start(cosT[NOPE:QD], a["c_rope_cosT"]).then_inc(S["tab"], 16)
                sp.dma_start(sinT[NOPE:QD], a["c_rope_sinT"]).then_inc(S["tab"], 16)
                sp.wait_ge(S["tab"], 32)

        with nc.Fori(0, MH) as h:
            with nc.Block() as block:
                @block.sync
                def _(sp):
                    uq = a["mla_w_uq"][0].rearrange("(k p) h e -> p k h e", p=P)
                    sp.dma_start(wq[:, :, 0:QD], uq[:, :, ds(h, 1), :].rearrange("p k h e -> p k (h e)")).then_inc(S["w"], 16)
                    for lo, src in ((QD, NOPE + half), (QD + half, NOPE)):
                        sp.dma_start(wq[:, :, lo:lo + half], uq[:, :, ds(h, 1), src:src + half].rearrange("p k h e -> p k (h e)")).then_inc(S["w"], 16)
                    for dst, src in ((wk, a["mla_w_uk"]), (wv, a["mla_w_uv"])):
                        sp.dma_start(dst[:], src[0].rearrange("(k p) h e -> p k h e", p=P)[:, :, ds(h, 1), :].rearrange("p k h e -> p k (h e)")).then_inc(S["w"], 16)

                parts = ((0, 512), (512, 512), (SEQ, NS))

                def pe_before(pe):
                    pe.wait_ge(S["w"], 80)
                    for j, (t0, n) in enumerate(parts):
                        for k in range(3):
                            nc.tensor.matmul(bank[:QD, 2 * j, :n], wq[:, k, 0:QD], cqT[:, k, t0:t0 + n], start=k == 0, stop=k == 2)
                        for k in range(3):
                            t = nc.tensor.matmul(bank[NOPE:QD, 2 * j + 1, :n], wq[:, k, QD:QD + ROPE], cqT[:, k, t0:t0 + n], start=k == 0, stop=k == 2)
                        t.then_inc(S["pre"], 1)
                    for i in range(NTILE):
                        for k in range(2):
                            t = nc.tensor.matmul(bank[:, 6, i * MV:(i + 1) * MV], ckvT[:, k, i * P:(i + 1) * P], wv[:, k, :], start=k == 0, stop=k == 1)
                    for k in range(2):
                        t = nc.tensor.transpose(bank[:NOPE, 7, k * P:(k + 1) * P], wk[:, k, :], c["ident"][:])
                    t.then_inc(S["pre"], 1)
                    pe.wait_ge(S["ev"], 2)
                    for j in range(2):
                        for k in range(2):
                            t = nc.tensor.matmul(bank[:NOPE, 2 * j, :], wk[:, k, :], ckvT[:, k, j * 512:(j + 1) * 512], start=k == 0, stop=k == 1)
                        t.then_inc(S["pre"], 1)
                    pe.wait_ge(S["ev"], 5)
                    for k in range(2):
                        t = nc.tensor.matmul(bank[:, 4, k * NS:(k + 1) * NS], wkT[:, k, :], qT[:NOPE, SEQ:NTOK], start=True, stop=True)
                    t.then_inc(S["pre"], 1)

                def dve_before(dve, link):
                    for j, (t0, n) in enumerate(parts):
                        dve.wait_ge(S["pre"], j + 1)
                        nc.vector.tensor_scalar(qT[:NOPE, t0:t0 + n], bank[:NOPE, 2 * j, :n], MLA_SCALE, None, ALU.mult)
                        nc.vector.scalar_tensor_tensor(out=rt[NOPE:QD, 0, :n], in0=bank[NOPE:QD, 2 * j, :n], scalar=MLA_SCALE,
                                                       in1=cosT[NOPE:QD, t0:t0 + n], op0=ALU.mult, op1=ALU.mult)
                        link(nc.vector.scalar_tensor_tensor(out=rt[NOPE:QD, 1, :n], in0=bank[NOPE:QD, 2 * j + 1, :n], scalar=MLA_SCALE,
                                                            in1=sinT[NOPE:QD, t0:t0 + n], op0=ALU.mult, op1=ALU.mult))
                        nc.vector.tensor_tensor(qT[NOPE:QD, t0:t0 + n], rt[NOPE:QD, 0, :n], rt[NOPE:QD, 1, :n], ALU.add).then_inc(S["ev"], 1)
                        dve.wait_ge(S["ev"], j + 1)
                    dve.wait_ge(S["pre"], 4)
                    nc.vector.tensor_copy(v[:].rearrange("p i e -> p (i e)"), bank[:, 6, :]).then_inc(S["ev"], 1)
                    nc.vector.tensor_copy(wkT[:].rearrange("p k e -> p (k e)"), bank[:NOPE, 7, 0:2 * P]).then_inc(S["ev"], 1)
                    for j in range(2):
                        dve.wait_ge(S["pre"], 5 + j)
                        nc.vector.tensor_copy(krT[:NOPE, j * 512:(j + 1) * 512], bank[:NOPE, 2 * j, :]).then_inc(S["qk"], 1)
                    dve.wait_ge(S["pre"], 7)
                    link(nc.vector.tensor_copy(qlat[:, :, ds(h, 1), :].rearrange("p k h t -> p k (h t)"), bank[:, 4, 0:2 * NS].rearrange("p (k t) -> p k t", k=2)))
                    nc.vector.tensor_copy(qrope[NOPE:QD, ds(h, 1), :].rearrange("p h t -> p (h t)"), qT[NOPE:QD, SEQ:NTOK]).then_inc(S["qk"], 1)

                def finish(i):
                    def f(o, r, link):
                        return nc.vector.tensor_scalar(oa[:, i, ds(h * MV, MV)], o, r, None, ALU.mult)
                    return f

                units = [{"q0": i * P, "nblk": i + 1, "kT": krT[:QD, :], "v": (lambda b: v[:, b, :]),
                          "masks": [(i * P, c["causal"][:])], "finish": finish(i)} for i in range(NTILE)]
                buf.update(pe_before=pe_before, dve_before=dve_before, qk_ready=3)
                attention(nc, c, block, S, buf, units, qT, QD)
            next_iteration(nc, [s for n, s in S.items() if n != "tab"])


def mla_sample(nc, a, d, c, act_t):
    ckvT, krT, oa, qlat, qrope = (act_t[k] for k in ("ckvT", "krT", "oa", "qlat", "qrope"))
    bank = c["bank"]
    NQ = MH * DT
    GP = 4
    NG4 = NPAGE // GP
    with ExitStack() as ctx:
        ctx.callback(nc.all_engine_barrier)
        def sb(name, shape):
            return ctx.enter_context(nc.sbuf_tensor(name, shape, F32))

        pg = sb("ms_pg", [P, NPAGE, ROW])
        kT = sb("ms_kT", [P, 2, 2, GP * P])
        rT = sb("ms_rT", [P, 2, GP * P])
        s = sb("ms_s", [NQ, PAST])
        sn = sb("ms_sn", [NQ, DT])
        mask = sb("ms_mask", [NQ, DT])
        q = sb("ms_q", [P, 2, NQ])
        qr = sb("ms_qr", [P, NQ])
        knew = sb("ms_knew", [P, DT])
        new = sb("ms_new", [DT, ROW])
        gmax = sb("ms_gmax", [NQ, NG4 + 1])
        nmax = sb("ms_nmax", [NQ, 1])
        gden = sb("ms_gden", [NQ, NG4 + 1])
        den = sb("ms_den", [NQ, 2])
        pT = sb("ms_pT", [P, 2, 512])
        pnT = sb("ms_pnT", [DT, NQ])
        ol = sb("ms_ol", [NQ, KVL])
        olT = sb("ms_olT", [P, 2, MH, DB, DT])
        s_w = cleared(nc, ctx, "ms_s_w")
        s_page = cleared(nc, ctx, "ms_s_page")
        names = ["new", "q", "tr", "kT", "kR", "sc", "s", "mx", "exp", "pt", "pT", "pv", "ol", "olt", "dv", "done"]
        S = {n: cleared(nc, ctx, "ms_s_" + n) for n in names}
        s_group = [cleared(nc, ctx, f"ms_s_group{i}") for i in range(NG4)]

        def load_group(eng, b, gi):
            pages = [eng.value_load(c["pages"][0:1, ds(b * NPAGE + GP * gi + j, 1)], min_val=0, max_val=POOL - 1) for j in range(GP)]
            for j, page in enumerate(pages):
                eng.dma_start(pg[:, GP * gi + j, :], a["cache_mla"][0, ds(page, 1)].rearrange("a p r -> (a p) r")).then_inc(s_group[gi], 16)

        def load_rest(eng, b):
            for gi in range(NG4 // 2, NG4):
                load_group(eng, b, gi)

        def load_next(eng, b, queue):
            nxt = eng.snap((b + 1) % DB)
            for gi in range(queue, NG4 // 2, 2):
                eng.wait_ge(S["pv"], gi + 1)
                eng.sem_clear(s_group[gi])
                load_group(eng, nxt, gi)

        with nc.Block() as block:
            @block.sync
            def _(sp):
                sp.dma_start(mask[:], a["c_mla_new"]).then_inc(s_w, 16)
                sp.wait_ge(s_w, 16)
                for gi in range(0, NG4 // 2, 2):
                    load_group(sp, 0, gi)

            @block.scalar
            def _(act):
                for gi in range(1, NG4 // 2, 2):
                    load_group(act, 0, gi)

            @block.vector
            def _(dve):
                nc.vector.memset(qr[:NOPE], 0.0).then_inc(S["done"], 1)
                nc.vector.memset(knew[:NOPE], 0.0).then_inc(S["done"], 1)
                dve.wait_ge(S["done"], 2)

        with nc.Fori(0, DB) as b:
            with nc.Block() as block:
                @block.sync
                def _(sp):
                    sp.dma_start(new[:], a["o_mla_rows_sample"][0, ds(b, 1)].rearrange("b t r -> (b t) r")).then_inc(S["new"], 16)
                    load_rest(sp, b)
                    load_next(sp, b, 0)

                @block.scalar
                def _(act):
                    for gi in range(NG4):
                        act.wait_ge(S["tr"], gi + 1)
                        if gi >= 2:
                            act.wait_ge(S["sc"], gi - 1)
                        nc.scalar.activation(rT[:QD, gi % 2, :], bank[:QD, 3 * (gi % 2) + 2, :], ACT.Copy).then_inc(S["kR"], 1)
                        if gi >= 1:
                            act.wait_ge(S["sc"], gi)
                            nc.scalar.activation(s[:, (gi - 1) * 512:gi * 512], bank[:NQ, 6 + (gi - 1) % 2, :], ACT.Copy).then_inc(S["s"], 1)
                    act.wait_ge(S["sc"], NG4)
                    nc.scalar.activation(s[:, (NG4 - 1) * 512:], bank[:NQ, 6 + (NG4 - 1) % 2, :], ACT.Copy).then_inc(S["s"], 1)
                    act.wait_ge(S["mx"], NG4 + 2)
                    act.wait_ge(S["s"], NG4)
                    nc.scalar.activation(sn[:], sn[:], ACT.Exp, bias=nmax[:], accum_out=gden[:, NG4:NG4 + 1]).then_inc(S["exp"], 1)
                    for gi in range(NG4):
                        nc.scalar.activation(s[:, gi * 512:(gi + 1) * 512], s[:, gi * 512:(gi + 1) * 512], ACT.Exp, bias=nmax[:],
                                             accum_out=gden[:, gi:gi + 1]).then_inc(S["exp"], 1)
                    load_next(act, b, 1)

                @block.tensor
                def _(pe):
                    def turn(gi):
                        pe.wait_ge(s_group[gi], 16 * GP)
                        if gi >= 2:
                            pe.wait_ge(S["kT"], 2 * (gi - 1))
                            pe.wait_ge(S["kR"], gi - 1)
                        for j in range(GP):
                            for k in range(2):
                                nc.tensor.transpose(bank[:, 3 * (gi % 2) + k, j * P:(j + 1) * P], pg[:, GP * gi + j, k * P:(k + 1) * P], c["ident"][:])
                            t = nc.tensor.transpose(bank[:QD, 3 * (gi % 2) + 2, j * P:(j + 1) * P], pg[:, GP * gi + j, ROW - QD:ROW], c["ident"][:])
                        t.then_inc(S["tr"], 1)

                    def score(gi):
                        pe.wait_ge(S["kT"], 2 * (gi + 1))
                        pe.wait_ge(S["kR"], gi + 1)
                        if gi >= 2:
                            pe.wait_ge(S["s"], gi - 1)
                        o = bank[:NQ, 6 + gi % 2, :]
                        for k in range(2):
                            nc.tensor.matmul(o, q[:, k, :], kT[:, gi % 2, k, :], start=k == 0, stop=False)
                        nc.tensor.matmul(o, qr[:QD, :], rT[:QD, gi % 2, :], start=False, stop=True).then_inc(S["sc"], 1)

                    turn(0)
                    pe.wait_ge(S["q"], 1)
                    for gi in range(NG4):
                        if gi + 1 < NG4:
                            turn(gi + 1)
                        score(gi)
                    pe.wait_ge(S["kT"], 2 * NG4)
                    o = bank[:NQ, 0, 0:DT]
                    for k in range(2):
                        nc.tensor.matmul(o, q[:, k, :], ckvT[:, k, ds(SEQ + b * DT, DT)], start=k == 0, stop=False)
                    nc.tensor.matmul(o, qr[:QD, :], knew[:QD, :], start=False, stop=True).then_inc(S["sc"], 1)

                    def probs(gi):
                        pe.wait_ge(S["exp"], gi + 2)
                        if gi >= 2:
                            pe.wait_ge(S["pT"], gi - 1)
                        for j in range(GP):
                            t = nc.tensor.transpose(bank[:, 1 + gi % 2, j * NQ:(j + 1) * NQ], s[:, (GP * gi + j) * P:(GP * gi + j + 1) * P], c["ident"][:NQ, :NQ])
                        t.then_inc(S["pt"], 1)

                    pe.wait_ge(S["exp"], 1)
                    nc.tensor.transpose(bank[:DT, 3, 0:NQ], sn[:], c["ident"][:NQ, :NQ]).then_inc(S["pt"], 1)
                    probs(0)
                    for gi in range(NG4):
                        if gi + 1 < NG4:
                            probs(gi + 1)
                        pe.wait_ge(S["pT"], gi + 2)
                        if gi == 0:
                            pe.wait_ge(S["new"], 16)
                            nc.tensor.matmul(bank[:NQ, 4, 0:KVL], pnT[:], new[:, 0:KVL], start=True, stop=False)
                        for j in range(GP):
                            t = nc.tensor.matmul(bank[:NQ, 4, 0:KVL], pT[:, gi % 2, j * NQ:(j + 1) * NQ], pg[:, GP * gi + j, 0:KVL],
                                                 start=False, stop=gi == NG4 - 1 and j == GP - 1)
                        t.then_inc(S["pv"], 1)
                    pe.wait_ge(S["ol"], 1)
                    for k in range(2):
                        t = nc.tensor.transpose(bank[:, 5, k * NQ:(k + 1) * NQ], ol[:, k * P:(k + 1) * P], c["ident"][:NQ, :NQ])
                    t.then_inc(S["olt"], 1)

                @block.vector
                def _(dve):
                    link = Chain(dve, S["dv"])
                    for k in range(2):
                        nc.vector.tensor_copy(q[:, k, :].rearrange("p (h t) -> p h t", t=DT), qlat[:, k, :, ds(b * DT, DT)])
                    nc.vector.tensor_copy(knew[NOPE:QD, :], krT[NOPE:QD, ds(SEQ + b * DT, DT)])
                    nc.vector.tensor_copy(qr[NOPE:QD, :].rearrange("p (h t) -> p h t", t=DT), qrope[NOPE:QD, :, ds(b * DT, DT)]).then_inc(S["q"], 1)
                    for gi in range(NG4):
                        dve.wait_ge(S["tr"], gi + 1)
                        if gi >= 2:
                            dve.wait_ge(S["sc"], gi - 1)
                        for k in range(2):
                            nc.vector.tensor_copy(kT[:, gi % 2, k, :], bank[:, 3 * (gi % 2) + k, :]).then_inc(S["kT"], 1)
                        if gi >= 1:
                            dve.wait_ge(S["s"], gi)
                            nc.vector.tensor_reduce(gmax[:, gi - 1:gi], s[:, (gi - 1) * 512:gi * 512], AX, ALU.max).then_inc(S["mx"], 1)
                    dve.wait_ge(S["s"], NG4)
                    nc.vector.tensor_reduce(gmax[:, NG4 - 1:NG4], s[:, (NG4 - 1) * 512:NG4 * 512], AX, ALU.max).then_inc(S["mx"], 1)
                    dve.wait_ge(S["sc"], NG4 + 1)
                    link(nc.vector.tensor_tensor(sn[:], bank[:NQ, 0, 0:DT], mask[:], ALU.add))
                    nc.vector.tensor_reduce(gmax[:, NG4:NG4 + 1], sn[:], AX, ALU.max).then_inc(S["mx"], 1)
                    dve.wait_ge(S["mx"], NG4 + 1)
                    nc.vector.tensor_reduce(nmax[:], gmax[:], AX, ALU.max, negate=True).then_inc(S["mx"], 1)
                    dve.wait_ge(S["pt"], 1)
                    nc.vector.tensor_copy(pnT[:], bank[:DT, 3, 0:NQ]).then_inc(S["pT"], 1)
                    for gi in range(NG4):
                        dve.wait_ge(S["pt"], gi + 2)
                        if gi >= 2:
                            dve.wait_ge(S["pv"], gi - 1)
                        nc.vector.tensor_copy(pT[:, gi % 2, 0:GP * NQ], bank[:, 1 + gi % 2, 0:GP * NQ]).then_inc(S["pT"], 1)
                    dve.wait_ge(S["exp"], NG4 + 1)
                    link(nc.vector.tensor_reduce(den[:, 0:1], gden[:], AX, ALU.add))
                    link(nc.vector.reciprocal(den[:, 1:2], den[:, 0:1]))
                    dve.wait_ge(S["pv"], NG4)
                    nc.vector.tensor_scalar(ol[:], bank[:NQ, 4, 0:KVL], den[:, 1:2], None, ALU.mult).then_inc(S["ol"], 1)
                    dve.wait_ge(S["olt"], 1)
                    for k in range(2):
                        link(nc.vector.tensor_copy(olT[:, k, :, ds(b, 1), :].rearrange("p h b t -> p h (b t)"),
                                                   bank[:, 5, k * NQ:(k + 1) * NQ].rearrange("p (h t) -> p h t", h=MH)))
            next_iteration(nc, [*S.values(), *s_group[NG4 // 2:]])

        wv = [pg[:, 2 * k:2 * k + 2, :].rearrange("p j r -> p (j r)")[:, 0:MW] for k in range(2)]
        with nc.Block() as block:
            @block.sync
            def _(sp):
                for gi in range(NG4 // 2):
                    sp.wait_ge(s_group[gi], 16 * GP)
                for k in range(2):
                    sp.dma_start(wv[k], a["mla_w_uv"][0, k * P:(k + 1) * P].rearrange("p h e -> p (h e)")).then_inc(s_w, 16)

            @block.tensor
            def _(pe):
                pe.wait_ge(s_w, 48)
                for h in range(MH):
                    for k in range(2):
                        t = nc.tensor.matmul(bank[:NS, 0, h * MV:(h + 1) * MV], olT[:, k, h].rearrange("p b t -> p (b t)"), wv[k][:, h * MV:(h + 1) * MV],
                                             start=k == 0, stop=k == 1)
                t.then_inc(S["pv"], 1)

            @block.vector
            def _(dve):
                dve.wait_ge(S["pv"], 1)
                nc.vector.tensor_copy(oa[:NS, NTILE, :], bank[:NS, 0, :]).then_inc(S["ol"], 1)
                dve.wait_ge(S["ol"], 1)


def s5_matrices(nc, a, d, c, m):
    bank = c["bank"]
    with ExitStack() as ctx:
        ctx.callback(nc.all_engine_barrier)
        def sb(name, shape):
            return ctx.enter_context(nc.sbuf_tensor(name, shape, F32))

        lam = sb("sm_lam", [P, 2, NPAIR])
        ldt = sb("sm_ldt", [P, NPAIR])
        b_in = sb("sm_b", [P, 2, NPAIR, SC])
        c_in = sb("sm_c", [P, 2, 2, P])
        cT = sb("sm_cT", [P, 2, NPAIR, SC])
        dskip = sb("sm_d", [SC, SG])
        w = sb("sm_w", [P, 12, NPAIR])
        pw = sb("sm_pw", [P, 2, CH + 1, NPAIR])
        pr = sb("sm_pr", [P, 2, CH, NPAIR])
        bb = sb("sm_bb", [P, 2, NPAIR, SC])
        t1 = sb("sm_t1", [P, NPAIR, CH + 1, SC])
        t2 = sb("sm_t2", [P, NPAIR, CH + 1, SC])
        xb = sb("sm_xb", [P, 2, NPAIR, CH, SC])
        kern = sb("sm_kern", [SC, SG, P])
        s_lam = cleared(nc, ctx, "sm_s_lam")
        s_b = cleared(nc, ctx, "sm_s_b")
        s_c = cleared(nc, ctx, "sm_s_c")
        s_dv = cleared(nc, ctx, "sm_s_dv")
        s_cT = cleared(nc, ctx, "sm_s_cT")
        s_act = cleared(nc, ctx, "sm_s_act")
        s_arg = cleared(nc, ctx, "sm_s_arg")
        s_xb = cleared(nc, ctx, "sm_s_xb")
        s_out = cleared(nc, ctx, "sm_s_out")
        s_tb = cleared(nc, ctx, "sm_s_tb")
        s_te = cleared(nc, ctx, "sm_s_te")
        s_k = cleared(nc, ctx, "sm_s_k")
        s_ke = cleared(nc, ctx, "sm_s_ke")
        s_kern = cleared(nc, ctx, "sm_s_kern")
        s_zero = cleared(nc, ctx, "sm_s_zero")
        s_toep = cleared(nc, ctx, "sm_s_toep")
        out, binT, toep = m["out"], m["binT"], m["toep"]

        def load_c(eng, i, key):
            for k in range(NPAIR):
                eng.dma_start(c_in[SC * (k % 8):SC * (k % 8 + 1), i, k // 8, :].rearrange("p (r n) -> p r n", r=2),
                              a[key][0, 2 * k:2 * k + 2].rearrange("r p n -> p r n")).then_inc(s_c, 16)

        with nc.Block() as block:
            @block.sync
            def _(sp):
                for r in range(2):
                    rows = slice(r * SN, (r + 1) * SN)
                    for i, key in enumerate(("s5_lambda_re", "s5_lambda_im")):
                        sp.dma_start(lam[rows, i], a[key][0].rearrange("(k r) n -> r n k", r=2)[r], allow_slow_non_contiguous=True).then_inc(s_lam, 16)
                    sp.dma_start(ldt[rows], a["s5_log_dt"][0].rearrange("(k r) -> r k", r=2)[r].partition_broadcast(SN), allow_slow_non_contiguous=True).then_inc(s_lam, 16)
                for r in range(2):
                    rows = slice(r * SN, (r + 1) * SN)
                    for i, key in enumerate(("s5_b_re", "s5_b_im")):
                        sp.dma_start(b_in[rows, i], a[key][0].rearrange("(k r) n q -> r n k q", r=2)[r]).then_inc(s_b, 16)
                load_c(sp, 0, "s5_c_re")
                sp.dma_start(dskip[:], a["s5_d"][0].rearrange("g p -> p g"), allow_slow_non_contiguous=True).then_inc(s_c, 16)
                sp.wait_ge(s_kern, 1)
                sp.wait_ge(s_zero, 1)
                for j in range(CH):
                    sp.dma_start(toep[SC * j:SC * (j + 1), :, SC * j:P], kern[:, :, 0:P - SC * j]).then_inc(s_toep, 16)
                sp.wait_ge(s_toep, 16 * CH)

            @block.gpsimd
            def _(pool):
                nc.gpsimd.memset(toep[:], 0.0).then_inc(s_zero, 1)

            @block.scalar
            def _(act):
                act.wait_ge(s_lam, 16 * 6)
                nc.scalar.activation(w[:, 0], ldt[:], ACT.Exp).then_inc(s_act, 1)
                act.wait_ge(s_arg, 1)
                nc.scalar.activation(w[:, 2], w[:, 1], ACT.Exp).then_inc(s_act, 1)
                act.wait_ge(s_arg, 2)
                nc.scalar.activation(m["rot"][:, 1], w[:, 4], ACT.Sin).then_inc(s_act, 1)
                nc.scalar.activation(w[:, 5], w[:, 4], ACT.Sin, scale=0.5).then_inc(s_act, 1)
                load_c(act, 1, "s5_c_im")

            @block.tensor
            def _(pe):
                pe.wait_ge(s_c, 16 * (2 * NPAIR + 1))
                for i in range(2):
                    for hf in range(2):
                        t = nc.tensor.transpose(bank[:, 0, (2 * i + hf) * P:(2 * i + hf + 1) * P], c_in[:, i, hf, :], c["ident"][:])
                t.then_inc(s_cT, 1)
                pe.wait_ge(s_xb, 2)
                for i in range(2):
                    for k in range(NPAIR):
                        t = nc.tensor.transpose(bank[:, 4 * i + k // 4, (k % 4) * P:(k % 4 + 1) * P], xb[:, i, k].rearrange("p j q -> p (j q)"), c["ident"][:])
                        if k % 4 == 3:
                            t.then_inc(s_tb, 1)
                pe.wait_ge(s_out, 2)
                pe.wait_ge(s_te, 8)
                for r in range(2):
                    rows = slice(r * SN, (r + 1) * SN)
                    for k in range(NPAIR):
                        for i in range(2):
                            t = nc.tensor.matmul(bank[:SC, 4 * r + k // 4, (k % 4) * P:(k % 4 + 1) * P], bb[rows, i, k, :],
                                                 out[rows, i, k, 0:CH, :].rearrange("p t q -> p (t q)"), start=i == 0, stop=i == 1)
                        if k % 4 == 3:
                            t.then_inc(s_k, 1)

            @block.vector
            def _(dve):
                link = Chain(dve, s_dv)
                V = nc.vector

                def cmul(o_re, o_im, a_re, a_im, b_re, b_im, u1, u2):
                    link(V.tensor_tensor(u1, a_re, b_re, ALU.mult))
                    link(V.tensor_tensor(u2, a_im, b_im, ALU.mult))
                    link(V.tensor_tensor(o_re, u1, u2, ALU.subtract))
                    link(V.tensor_tensor(u1, a_re, b_im, ALU.mult))
                    link(V.tensor_tensor(u2, a_im, b_re, ALU.mult))
                    link(V.tensor_tensor(o_im, u1, u2, ALU.add))

                dve.wait_ge(s_act, 1)
                V.tensor_tensor(w[:, 1], lam[:, 0], w[:, 0], ALU.mult).then_inc(s_arg, 1)
                turn = 6.283185307179586
                hi = 6.28125
                magic = 12582912.0
                link(V.tensor_tensor(w[:, 3], lam[:, 1], w[:, 0], ALU.mult))
                link(V.tensor_scalar(w[:, 6], w[:, 3], 1.0 / turn, None, ALU.mult))
                link(V.tensor_scalar(w[:, 6], w[:, 6], magic, magic, ALU.add, ALU.subtract))
                link(V.scalar_tensor_tensor(out=w[:, 3], in0=w[:, 6], scalar=-hi, in1=w[:, 3], op0=ALU.mult, op1=ALU.add))
                link(V.scalar_tensor_tensor(out=w[:, 3], in0=w[:, 6], scalar=-(turn - hi), in1=w[:, 3], op0=ALU.mult, op1=ALU.add))
                V.tensor_scalar(w[:, 4], w[:, 3], 3.1415925, -3.1415925, ALU.min, ALU.max).then_inc(s_arg, 1)
                dve.wait_ge(s_act, 4)
                link(V.tensor_tensor(w[:, 6], w[:, 5], w[:, 5], ALU.mult))
                link(V.tensor_scalar(m["rot"][:, 0], w[:, 6], -2.0, 1.0, ALU.mult, ALU.add))
                link(V.memset(pw[:, 0, 0], 1.0))
                link(V.memset(pw[:, 1, 0], 0.0))
                for i in range(2):
                    link(V.tensor_tensor(pw[:, i, 1], m["rot"][:, i], w[:, 2], ALU.mult))
                n = 1
                while n < CH:
                    cmul(pw[:, 0, n + 1:2 * n + 1], pw[:, 1, n + 1:2 * n + 1], pw[:, 0, 1:n + 1], pw[:, 1, 1:n + 1],
                         pw[:, 0, n:n + 1].broadcast_to((P, n, NPAIR)), pw[:, 1, n:n + 1].broadcast_to((P, n, NPAIR)),
                         t1[:, 0:n, 0, :], t2[:, 0:n, 0, :])
                    n *= 2
                for i in range(2):
                    link(V.tensor_copy(m["l4"][:, i], pw[:, i, DT]))
                    for j in range(CH):
                        link(V.tensor_copy(pr[:, i, j], pw[:, i, CH - 1 - j]))
                link(V.tensor_tensor(w[:, 7], w[:, 2], w[:, 2], ALU.mult))
                link(V.tensor_tensor(w[:, 8], w[:, 7], w[:, 7], ALU.mult))
                link(V.tensor_tensor(m["l8"][:], w[:, 8], w[:, 8], ALU.mult))
                link(V.tensor_tensor(w[:, 5], lam[:, 0], lam[:, 0], ALU.mult))
                link(V.tensor_tensor(w[:, 6], lam[:, 1], lam[:, 1], ALU.mult))
                link(V.tensor_tensor(w[:, 5], w[:, 5], w[:, 6], ALU.add))
                link(V.reciprocal(w[:, 7], w[:, 5]))
                link(V.tensor_scalar(w[:, 8], pw[:, 0, 1], -1.0, None, ALU.add))
                link(V.tensor_tensor(w[:, 9], lam[:, 0], w[:, 7], ALU.mult))
                link(V.scalar_tensor_tensor(out=w[:, 10], in0=lam[:, 1], scalar=-1.0, in1=w[:, 7], op0=ALU.mult, op1=ALU.mult))
                cmul(w[:, 0], w[:, 1], w[:, 8], pw[:, 1, 1], w[:, 9], w[:, 10], w[:, 5], w[:, 6])
                fr = [w[:, i].unsqueeze(2).broadcast_to((P, NPAIR, SC)) for i in range(2)]
                dve.wait_ge(s_b, 16 * 4)
                cmul(bb[:, 0], bb[:, 1], b_in[:, 0], b_in[:, 1], fr[0], fr[1], t1[:, :, 0, :], t2[:, :, 0, :])
                bx = [bb[:, i].unsqueeze(2).broadcast_to((P, NPAIR, CH, SC)) for i in range(2)]
                px = [pr[:, i].rearrange("p j k -> p k j").unsqueeze(3).broadcast_to((P, NPAIR, CH, SC)) for i in range(2)]
                cmul(xb[:, 0], xb[:, 1], bx[0], bx[1], px[0], px[1], t1[:, :, 0:CH, :], t2[:, :, 0:CH, :])
                dve.wait_ge(s_cT, 1)
                link(V.tensor_copy(cT[:].rearrange("p i k q -> p (i k q)"), bank[:, 0, :]))
                V.memset(w[:, 11], 0.0).then_inc(s_xb, 2)
                cx = [cT[:, i].unsqueeze(2).broadcast_to((P, NPAIR, CH + 1, SC)) for i in range(2)]
                px = [pw[:, i].rearrange("p j k -> p k j").unsqueeze(3).broadcast_to((P, NPAIR, CH + 1, SC)) for i in range(2)]
                link(V.tensor_tensor(t1[:], cx[0], px[0], ALU.mult))
                link(V.tensor_tensor(t2[:], cx[1], px[1], ALU.mult))
                link(V.tensor_tensor(out[:, 0], t1[:], t2[:], ALU.subtract))
                link(V.tensor_tensor(t1[:], cx[0], px[1], ALU.mult))
                link(V.tensor_tensor(t2[:], cx[1], px[0], ALU.mult))
                V.scalar_tensor_tensor(out=out[:, 1], in0=t1[:], scalar=-1.0, in1=t2[:], op0=ALU.mult, op1=ALU.subtract).then_inc(s_out, 2)
                for g4 in range(8):
                    dve.wait_ge(s_tb, g4 + 1)
                    V.tensor_copy(binT[:, g4 // 4, 4 * (g4 % 4):4 * (g4 % 4) + 4, :].rearrange("p k n -> p (k n)"), bank[:, g4, :]).then_inc(s_te, 1)
                for g4 in range(8):
                    dve.wait_ge(s_k, g4 + 1)
                    link(V.tensor_copy(kern[:].rearrange("q (k r) n -> q r k n", r=2)[:, g4 // 4, 4 * (g4 % 4):4 * (g4 % 4) + 4, :],
                                       bank[:SC, g4, :].rearrange("q (k n) -> q k n", k=4)))
                link(V.tensor_tensor(t1[:SC].rearrange("q k t p -> q (k t p)")[:, 0:SG * SC].rearrange("q (g p) -> q g p", g=SG),
                                     c["ident"][:SC, :SC].unsqueeze(1).broadcast_to((SC, SG, SC)),
                                     dskip[:].unsqueeze(2).broadcast_to((SC, SG, SC)), ALU.mult))
                V.tensor_tensor(kern[:, :, 0:SC], kern[:, :, 0:SC],
                                t1[:SC].rearrange("q k t p -> q (k t p)")[:, 0:SG * SC].rearrange("q (g p) -> q g p", g=SG), ALU.add).then_inc(s_kern, 1)


def s5_prompt(nc, a, d, c, m, hlast):
    bank = c["bank"]
    HK = NPAIR // 2
    HG = SG // 2
    out, binT, toep = m["out"], m["binT"], m["toep"]
    with ExitStack() as ctx:
        ctx.callback(nc.all_engine_barrier)
        def sb(name, shape):
            return ctx.enter_context(nc.sbuf_tensor(name, shape, F32))

        u = sb("sp_u", [P, HG, NCH])
        e = sb("sp_e", [P, 2, HK, NCH])
        e8 = sb("sp_e8", [P, 4, HK])
        decay = sb("sp_decay", [P, HK, NCH])
        t1 = sb("sp_t1", [P, HK, NCH])
        t2 = sb("sp_t2", [P, HK, NCH])
        s = sb("sp_s", [P, 2, HK, NCH])
        hs = sb("sp_h", [P, 2, HK, NCH + 1])
        y = sb("sp_y", [P, HG, NCH])
        names = ["u", "s", "ev", "h", "y", "g", "st", "dv"]
        S = {n: cleared(nc, ctx, "sp_s_" + n) for n in names}

        for hf in range(2):
            k0 = HK * hf
            with nc.Block() as block:
                @block.sync
                def _(sp):
                    for j in range(CH):
                        sp.dma_start(u[SC * j:SC * (j + 1)], d["u"].rearrange("(g q) j k -> q g j k", q=SC)[:, HG * hf:HG * (hf + 1), j, :]).then_inc(S["u"], 16)
                    for q4 in range(4):
                        sp.wait_ge(S["g"], q4 + 1)
                        for i in range(CH):
                            sp.dma_start(d["y"].rearrange("(k r p) i c -> p r k i c", p=SC, r=2)[:, q4 // 2, k0 + 4 * (q4 % 2):k0 + 4 * (q4 % 2) + 4, i, :],
                                         y[SC * i:SC * (i + 1), 4 * q4:4 * q4 + 4, :]).then_inc(S["st"], 16)
                    sp.wait_ge(S["st"], 16 * CH * 4)

                @block.tensor
                def _(pe):
                    pe.wait_ge(S["u"], 16 * CH)
                    for kk in range(HK):
                        for i in range(2):
                            for r in range(2):
                                t = nc.tensor.matmul(bank[r * SN:(r + 1) * SN, 2 * (kk // 4) + i, (kk % 4) * NCH:(kk % 4 + 1) * NCH],
                                                     binT[:, i, k0 + kk, r * SN:(r + 1) * SN], u[:, 2 * kk + r, :], start=True, stop=True)
                        if kk % 4 == 3:
                            t.then_inc(S["s"], 1)
                    pe.wait_ge(S["h"], 1)
                    for j in range(HG):
                        kk, r = j % HK, j // HK
                        g = 2 * kk + r
                        rows = slice(r * SN, (r + 1) * SN)
                        o = bank[:, 4 + j // 4, (j % 4) * NCH:(j % 4 + 1) * NCH]
                        nc.tensor.matmul(o, toep[:, HG * hf + g, :], u[:, g, :], start=True, stop=False)
                        for i in range(2):
                            t = nc.tensor.matmul(o, out[rows, i, k0 + kk, 1:CH + 1, :].rearrange("p t q -> p (t q)"), hs[rows, i, kk, 0:NCH],
                                                 start=False, stop=i == 1)
                        if j % 4 == 3:
                            t.then_inc(S["y"], 1)

                @block.scalar
                def _(act):
                    for q4 in range(4):
                        act.wait_ge(S["y"], q4 + 1)
                        nc.scalar.activation(y[:, 4 * q4:4 * q4 + 4, :].rearrange("p g k -> p (g k)"), bank[:, 4 + q4, :], ACT.Gelu_apprx_tanh).then_inc(S["g"], 1)

                @block.vector
                def _(dve):
                    link = Chain(dve, S["dv"])
                    V = nc.vector

                    def cmul(o_re, o_im, a_re, a_im, b_re, b_im, u1, u2):
                        link(V.tensor_tensor(u1, a_re, b_re, ALU.mult))
                        link(V.tensor_tensor(u2, a_im, b_im, ALU.mult))
                        link(V.tensor_tensor(o_re, u1, u2, ALU.subtract))
                        link(V.tensor_tensor(u1, a_re, b_im, ALU.mult))
                        link(V.tensor_tensor(u2, a_im, b_re, ALU.mult))
                        link(V.tensor_tensor(o_im, u1, u2, ALU.add))

                    rot = [m["rot"][:, i, k0:k0 + HK] for i in range(2)]
                    cmul(e8[:, 0], e8[:, 1], rot[0], rot[1], rot[0], rot[1], t1[:, :, 0], t2[:, :, 0])
                    cmul(e8[:, 2], e8[:, 3], e8[:, 0], e8[:, 1], e8[:, 0], e8[:, 1], t1[:, :, 0], t2[:, :, 0])
                    cmul(e[:, 0, :, 0], e[:, 1, :, 0], e8[:, 2], e8[:, 3], e8[:, 2], e8[:, 3], t1[:, :, 0], t2[:, :, 0])
                    n = 1
                    while n < NCH:
                        last = [e[:, i, :, n - 1:n].broadcast_to((P, HK, n)) for i in range(2)]
                        cmul(e[:, 0, :, n:2 * n], e[:, 1, :, n:2 * n], e[:, 0, :, 0:n], e[:, 1, :, 0:n], last[0], last[1], t1[:, :, 0:n], t2[:, :, 0:n])
                        n *= 2
                    link(V.tensor_copy(decay[:], m["l8"][:, k0:k0 + HK].unsqueeze(2).broadcast_to((P, HK, NCH))))
                    link(V.memset(decay[:, :, 0:1], 0.0))
                    link(V.memset(hs[:, :, :, 0:1], 0.0))
                    for b2 in range(2):
                        dve.wait_ge(S["s"], b2 + 1)
                        sr, si = (bank[:, 2 * b2 + i, :].rearrange("p (k c) -> p k c", k=4) for i in range(2))
                        kk = slice(4 * b2, 4 * b2 + 4)
                        link(V.tensor_tensor(t1[:, kk], sr, e[:, 0, kk], ALU.mult))
                        link(V.tensor_tensor(t2[:, kk], si, e[:, 1, kk], ALU.mult))
                        link(V.tensor_tensor(s[:, 0, kk], t1[:, kk], t2[:, kk], ALU.add))
                        link(V.tensor_tensor(t1[:, kk], si, e[:, 0, kk], ALU.mult))
                        link(V.tensor_tensor(t2[:, kk], sr, e[:, 1, kk], ALU.mult))
                        link(V.tensor_tensor(s[:, 1, kk], t1[:, kk], t2[:, kk], ALU.subtract))
                    flat = "p k c -> p (k c)"
                    link(V.tensor_tensor_scan(t1[:].rearrange(flat), decay[:].rearrange(flat), s[:, 0].rearrange(flat), 0.0, ALU.mult, ALU.add))
                    link(V.tensor_tensor_scan(t2[:].rearrange(flat), decay[:].rearrange(flat), s[:, 1].rearrange(flat), 0.0, ALU.mult, ALU.add))
                    link(V.tensor_tensor(s[:, 0], t1[:], e[:, 0], ALU.mult))
                    link(V.tensor_tensor(s[:, 1], t2[:], e[:, 1], ALU.mult))
                    link(V.tensor_tensor(hs[:, 0, :, 1:NCH + 1], s[:, 0], s[:, 1], ALU.subtract))
                    link(V.tensor_tensor(s[:, 0], t1[:], e[:, 1], ALU.mult))
                    link(V.tensor_tensor(s[:, 1], t2[:], e[:, 0], ALU.mult))
                    V.tensor_tensor(hs[:, 1, :, 1:NCH + 1], s[:, 0], s[:, 1], ALU.add).then_inc(S["h"], 1)
                    dve.wait_ge(S["h"], 1)
                    link(V.tensor_copy(hlast[:, :, k0:k0 + HK], hs[:, :, :, NCH]))
            next_iteration(nc, S.values())


def s5_sample(nc, a, d, c, m, hlast):
    bank = c["bank"]
    out, binT, toep = m["out"], m["binT"], m["toep"]
    LO = P - DT * SC
    with ExitStack() as ctx:
        ctx.callback(nc.all_engine_barrier)
        def sb(name, shape):
            return ctx.enter_context(nc.sbuf_tensor(name, shape, F32))

        u = sb("ss_u", [P, SG, DB])
        st_in = sb("ss_in", [P, P, 2])
        h0 = sb("ss_h0", [P, 2, NPAIR, DB])
        hl = sb("ss_hl", [P, 2, DB, NPAIR])
        t = sb("ss_t", [P, 4, NPAIR, DB])
        y = sb("ss_y", [P, SG, DB])
        st_s = sb("ss_os", [P, P, 2])
        st_p = sb("ss_op", [NPAIR, P, 2])
        names = ["ld", "h0t", "h0", "y", "g", "hl", "stt", "so", "st", "dv"]
        S = {n: cleared(nc, ctx, "ss_s_" + n) for n in names}

        with nc.Block() as block:
            @block.sync
            def _(sp):
                for t4 in range(DT):
                    sp.dma_start(u[LO + SC * t4:LO + SC * (t4 + 1)], d["us"].rearrange("(g q) t b -> q g t b", q=SC)[:, :, t4, :]).then_inc(S["ld"], 16)
                sp.dma_start(st_in[:], a["state_s5"][0].rearrange("b (k r) n c -> (b k) (r n) c", r=2)).then_inc(S["ld"], 16)
                sp.wait_ge(S["g"], 2)
                for t4 in range(DT):
                    sp.dma_start(d["ys"].rearrange("(g p) t b -> p g t b", p=SC)[:, :, t4, :], y[LO + SC * t4:LO + SC * (t4 + 1)]).then_inc(S["st"], 16)
                sp.wait_ge(S["so"], 2)
                sp.dma_start(a["o_s5_state_sample"][0].rearrange("b (k r) n c -> (b k) (r n) c", r=2), st_s[:]).then_inc(S["st"], 16)
                sp.dma_start(a["o_s5_state_prompt"][0, 0].rearrange("(k r) n c -> k (r n) c", r=2), st_p[:]).then_inc(S["st"], 16)
                sp.wait_ge(S["st"], 16 * (DT + 2))

            @block.tensor
            def _(pe):
                pe.wait_ge(S["ld"], 16 * (DT + 1))
                for i in range(2):
                    x = nc.tensor.transpose(bank[:, 0, i * P:(i + 1) * P], st_in[:, :, i], c["ident"][:])
                x.then_inc(S["h0t"], 1)
                pe.wait_ge(S["h0"], 3)
                for g in range(SG):
                    k, r = g // 2, g % 2
                    rows = slice(r * SN, (r + 1) * SN)
                    o = bank[LO:P, 6 + r, k * DB:(k + 1) * DB]
                    nc.tensor.matmul(o, toep[:, g, LO:P], u[:, g, :], start=True, stop=False)
                    for i in range(2):
                        nc.tensor.matmul(o, out[rows, i, k, 1:DT + 1, :].rearrange("p t q -> p (t q)"), h0[rows, i, k, :], start=False, stop=i == 1)
                    for i in range(2):
                        x = nc.tensor.matmul(bank[rows, 2 + i, k * DB:(k + 1) * DB], binT[:, i, k, rows], u[:, g, :], start=True, stop=True)
                x.then_inc(S["y"], 1)
                pe.wait_ge(S["hl"], 2)
                for i in range(2):
                    nc.tensor.transpose(bank[:, 4, i * P:(i + 1) * P], hl[:, i].rearrange("p b k -> p (b k)"), c["ident"][:])
                    x = nc.tensor.transpose(bank[:NPAIR, 5, i * P:(i + 1) * P], hlast[:, i, :], c["ident"][:])
                x.then_inc(S["stt"], 1)

            @block.scalar
            def _(act):
                act.wait_ge(S["y"], 1)
                for r in range(2):
                    nc.scalar.activation(y[LO:P].rearrange("p (k r) b -> p r k b", r=2)[:, r], bank[LO:P, 6 + r, 0:NPAIR * DB].rearrange("p (k b) -> p k b", b=DB),
                                         ACT.Gelu_apprx_tanh).then_inc(S["g"], 1)

            @block.vector
            def _(dve):
                link = Chain(dve, S["dv"])
                V = nc.vector
                V.memset(u[0:LO], 0.0).then_inc(S["h0"], 1)
                dve.wait_ge(S["h0t"], 1)
                for i in range(2):
                    V.tensor_copy(h0[:, i], bank[:, 0, i * P:(i + 1) * P].rearrange("p (b k) -> p k b", b=DB)).then_inc(S["h0"], 1)
                dve.wait_ge(S["y"], 1)
                dve.wait_ge(S["h0"], 3)
                l4 = [m["l4"][:, i].unsqueeze(2).broadcast_to((P, NPAIR, DB)) for i in range(2)]
                for j, (x, l) in enumerate(((0, 0), (1, 1), (0, 1), (1, 0))):
                    link(V.tensor_tensor(t[:, j], h0[:, x], l4[l], ALU.mult))
                link(V.tensor_tensor(t[:, 0], t[:, 0], t[:, 1], ALU.subtract))
                link(V.tensor_tensor(t[:, 2], t[:, 2], t[:, 3], ALU.add))
                for i in range(2):
                    V.tensor_tensor(hl[:, i].rearrange("p b k -> p k b"), t[:, 2 * i], bank[:, 2 + i, 0:NPAIR * DB].rearrange("p (k b) -> p k b", b=DB), ALU.add).then_inc(S["hl"], 1)
                dve.wait_ge(S["stt"], 1)
                V.tensor_copy(st_s[:].rearrange("p n c -> p c n"), bank[:, 4, 0:2 * P].rearrange("p (c n) -> p c n", c=2)).then_inc(S["so"], 1)
                V.tensor_copy(st_p[:].rearrange("p n c -> p c n"), bank[:NPAIR, 5, 0:2 * P].rearrange("p (c n) -> p c n", c=2)).then_inc(S["so"], 1)


def even_output(nc, a, d, c, act_t):
    zaT, zbT, oa = act_t["zaT"], act_t["zbT"], act_t["oa"]
    bank = c["bank"]
    with ExitStack() as ctx:
        ctx.callback(nc.all_engine_barrier)
        def sb(name, shape):
            return ctx.enter_context(nc.sbuf_tensor(name, shape, F32))

        gT = sb("eo_g", [P, 4, 512])
        sg = sb("eo_sg", [P, 2, 512])
        wg = sb("eo_wg", [P, 4, SW])
        bg = sb("eo_bg", [P, 4])
        wo = sb("eo_wo", [P, KD, D_MODEL])
        mixa = sb("eo_mixa", [P, 4, P])
        mixb = sb("eo_mixb", [P, 4, P])
        x = sb("eo_x", [P, D_MODEL])
        x1 = sb("eo_x1", [P, D_MODEL])
        s_wg = cleared(nc, ctx, "eo_s_wg")
        s_wo = cleared(nc, ctx, "eo_s_wo")
        names = ["g", "mm", "sg", "dv", "x", "T", "mix", "o", "x1", "st"]
        S = {n: cleared(nc, ctx, "eo_s_" + n) for n in names}

        with nc.Block() as block:
            @block.sync
            def _(sp):
                sp.dma_start(wg[:], a["s5_w_glu"][0].rearrange("(k p) n -> p k n", p=P)).then_inc(s_wg, 16)
                sp.dma_start(bg[:], a["s5_b_glu"][0].rearrange("(k p) -> p k", p=P), allow_slow_non_contiguous=True).then_inc(s_wg, 16)
                for k in range(KD):
                    sp.dma_start(wo[:, k], a["w_out_even"][0, k * P:(k + 1) * P, :]).then_inc(s_wo, 16)

        for j, n in ((0, 512), (1, 512), (2, NS)):
            with nc.Block() as block:
                @block.sync
                def _(sp):
                    sp.wait_ge(s_wg, 32)
                    if j < 2:
                        for i in range(CH):
                            src = d["y"].rearrange("(e p) i k -> p e i k", p=P)[:, :, i, j * 64:(j + 1) * 64]
                            sp.dma_start(gT[:, :, i * 64:(i + 1) * 64], src).then_inc(S["g"], 16)
                    else:
                        sp.dma_start(gT[:, :, 0:NS], d["ys"].rearrange("(e p) t b -> p e (t b)", p=P)).then_inc(S["g"], 16)

                @block.tensor
                def _(pe):
                    pe.wait_ge(S["g"], 16 * (CH if j < 2 else 1))
                    pe.wait_ge(s_wg, 32)
                    for e in range(4):
                        for k in range(4):
                            t = nc.tensor.matmul(bank[:, e, :n], wg[:, k, e * P:(e + 1) * P], gT[:, k, :n], start=k == 0, stop=k == 3)
                        t.then_inc(S["mm"], 1)

                @block.scalar
                def _(act):
                    for e in range(4):
                        act.wait_ge(S["mm"], e + 1)
                        if e >= 2:
                            act.wait_ge(S["dv"], 2 * (e - 1))
                        nc.scalar.activation(sg[:, e % 2, :n], bank[:, e, :n], ACT.Sigmoid, bias=bg[:, e:e + 1]).then_inc(S["sg"], 1)

                @block.vector
                def _(dve):
                    link = Chain(dve, S["dv"])
                    for e in range(4):
                        dve.wait_ge(S["sg"], e + 1)
                        link(nc.vector.tensor_tensor(sg[:, e % 2, :n], sg[:, e % 2, :n], gT[:, e, :n], ALU.mult))
                        if j < 2:
                            z = zbT[:, e, j * 512:(j + 1) * 512].rearrange("p (k i) -> p i k", i=CH)
                            link(nc.vector.tensor_tensor(z, z, sg[:, e % 2, :].rearrange("p (i k) -> p i k", i=CH), ALU.mult))
                        else:
                            z = zbT[:, e, SEQ:NTOK].rearrange("p (b t) -> p t b", t=DT)
                            link(nc.vector.tensor_tensor(z, z, sg[:, e % 2, :n].rearrange("p (t b) -> p t b", t=DT), ALU.mult))
            next_iteration(nc, S.values())

        def iteration(after=None, now=None, before=None):
            with nc.Block() as block:
                @block.sync
                def _(sp):
                    if now:
                        sp.dma_start(x[:now[0]], now[3]).then_inc(S["x"], 16)
                    if before:
                        sp.dma_start(d["x1"][ds(before[1], before[0]), :], x1[:before[0]]).then_inc(S["st"], 16)
                        sp.wait_ge(S["st"], 16)

                @block.tensor
                def _(pe):
                    pe.wait_ge(s_wo, 16 * KD)
                    for hf in range(2):
                        if now:
                            n = now[0]
                            for k in range(KD):
                                lhsT = mixa[:, k, :n] if k < 4 else mixb[:, k - 4, :n]
                                t = nc.tensor.matmul(bank[:n, 1 + hf, :], lhsT, wo[:, k, hf * 512:(hf + 1) * 512], start=k == 0, stop=k == KD - 1)
                            t.then_inc(S["o"], 1)
                        if after and hf == 0:
                            n = after[0]
                            pe.wait_ge(S["T"], 1)
                            for k in range(4):
                                t = nc.tensor.transpose(bank[:, 0, k * n:(k + 1) * n], sg[:n, 0, k * P:(k + 1) * P], c["ident"][:n, :n])
                            t.then_inc(S["T"], 1)

                @block.scalar
                def _(act):
                    if after:
                        n, tok0, i = after[:3]
                        nc.scalar.activation(sg[:n, 0, :], oa[:n, ds(i, 1), :].rearrange("p i e -> p (i e)"), ACT.Copy).then_inc(S["T"], 1)
                        if now:
                            act.wait_ge(S["o"], 2)
                        nc.scalar.activation(mixb[:, :, :n], zbT[:, :, ds(tok0, n)], ACT.Copy).then_inc(S["mix"], 1)

                @block.vector
                def _(dve):
                    if now:
                        n = now[0]
                        dve.wait_ge(S["x"], 16)
                        if before:
                            dve.wait_ge(S["st"], 16)
                        for hf in range(2):
                            dve.wait_ge(S["o"], hf + 1)
                            cols = slice(hf * 512, (hf + 1) * 512)
                            nc.vector.tensor_tensor(x1[:n, cols], bank[:n, 1 + hf, :], x[:n, cols], ALU.add).then_inc(S["x1"], 1)
                    if after:
                        n, tok0 = after[:2]
                        dve.wait_ge(S["T"], 2)
                        nc.vector.tensor_tensor(mixa[:, :, :n], bank[:, 0, :4 * n].rearrange("p (k t) -> p k t", k=4), zaT[:, :, ds(tok0, n)], ALU.mult).then_inc(S["mix"], 1)
            next_iteration(nc, S.values())

        def prompt(i):
            return P, i * P, i, a["x_prompt"][0, ds(i * P, P), :]

        sample = NS, SEQ, NTILE, a["x_sample"].rearrange("b t d -> (b t) d")
        iteration(after=prompt(0))
        iteration(after=prompt(1), now=prompt(0))
        with nc.Fori(1, NTILE - 1) as i:
            iteration(after=(P, (i + 1) * P, i + 1), now=prompt(i), before=(P, (i - 1) * P, i - 1))
        iteration(after=sample, now=prompt(NTILE - 1), before=prompt(NTILE - 2))
        iteration(now=sample, before=prompt(NTILE - 1))
        iteration(before=sample)


def odd_projection(nc, a, d, c, o):
    kv, ksT, kwT, gate, kTs = (o[k] for k in ("kv", "ksT", "kwT", "gate", "kTs"))
    bank = c["bank"]
    chunks = ((0, 512), (512, 6 * KVW + 3 * NH), (6 * KVW + 3 * NH, 6 * KVW + 3 * NH + 512), (6 * KVW + 3 * NH + 512, ODD_TOK))
    with ExitStack() as ctx:
        ctx.callback(nc.all_engine_barrier)
        def sb(name, shape):
            return ctx.enter_context(nc.sbuf_tensor(name, shape, F32))

        w = sb("op_w", [P, KD, ODD_IN])
        g = sb("op_g", [P, KD])
        x = sb("op_x", [P, D_MODEL])
        h = sb("op_h", [P, D_MODEL])
        hT = sb("op_hT", [P, KD, P])
        tk = sb("op_tk", [P, 6 * KVW])
        zs = sb("op_zs", [P, NW])
        qS = sb("op_q", [P, KD, P])
        st = sb("op_st", [P, 4])
        s_w = cleared(nc, ctx, "op_s_w")
        names = ["x", "ss", "ms", "sd", "rs", "T", "hT", "tok", "q", "tk", "z", "qs", "T2", "kT", "st", "gate", "kv", "nt"]
        S = {n: cleared(nc, ctx, "op_s_" + n) for n in names}
        s_rows = cleared(nc, ctx, "op_s_rows")
        s_zero = cleared(nc, ctx, "op_s_zero")

        with nc.Block() as block:
            @block.vector
            def _(dve):
                for dst in (ksT, kwT):
                    nc.vector.memset(dst[HD:HQ], 0.0).then_inc(s_zero, 1)

            @block.sync
            def _(sp):
                for k in range(KD):
                    sp.dma_start(w[:, k, :], a["w_in_odd"][0, k * P:(k + 1) * P, :]).then_inc(s_w, 16)
                sp.dma_start(g[:], a["norm_odd"][0].rearrange("(k p) -> p k", p=P), allow_slow_non_contiguous=True).then_inc(s_w, 16)
                sp.wait_ge(s_zero, 2)
                for gg in range(NG):
                    sp.dma_start(ksT[HD:HD + 1, gg, :], a["c_kpos"]).then_inc(s_w, 16)
                    sp.dma_start(kwT[HD:HD + 1, gg, :], a["c_kpos"]).then_inc(s_w, 16)
                sp.wait_ge(s_w, 16 * (KD + 5))

        prep = TilePrep(nc, c, S, x, h, hT, st, g)

        def tile(n, tok0, i, prompt, following=None):
            with nc.Block() as block:
                @block.sync
                def _(sp):
                    if prompt:
                        prep.load(sp, P, following(sp))
                    else:
                        sp.dma_start(a["o_nsa_rows_prompt"][0, 0].rearrange("(i p) k g d -> p i (k g d)", p=P), kv[:, :, 0:512]).then_inc(s_rows, 16)
                        sp.dma_start(a["o_nsa_win_prompt"][0, 0].rearrange("(i p) k g d -> p i (k g d)", p=P), kv[:, NTILE - WIN // P:, 512:768]).then_inc(s_rows, 16)
                    sp.wait_ge(S["z"], 2)
                    sp.dma_start(d["z"][ds(tok0, n), :], zs[:n]).then_inc(S["st"], 16)
                    sp.wait_ge(S["qs"], 2)
                    sp.dma_start(d["qT"].rearrange("(e p) t -> p e t", p=P)[:, :, ds(tok0, n)], qS[:, :, :n]).then_inc(S["st"], 16)
                    sp.wait_ge(S["st"], 32)
                    if not prompt:
                        sp.wait_ge(S["tk"], 2)
                        sp.dma_start(a["o_nsa_rows_sample"][0].rearrange("b t k g d -> (b t) (k g d)"), tk[:n, 0:512]).then_inc(s_rows, 16)
                        for b in range(DB):
                            sp.dma_start(a["o_nsa_win_sample"][0, b, WIN - DT:WIN].rearrange("t k g d -> t (k g d)"), tk[DT * b:DT * (b + 1), 512:768]).then_inc(s_rows, 16)
                        sp.wait_ge(s_rows, 16 * (DB + 3))

                @block.gpsimd
                def _(pool):
                    if prompt:
                        pool.wait_ge(S["tk"], 2)
                        nc.gpsimd.tensor_copy(kv[:, ds(i, 1), :].rearrange("p i c -> p (i c)"), tk[:]).then_inc(S["kv"], 1)

                @block.scalar
                def _(act):
                    if prompt:
                        prep.squares(act, P)
                    act.wait_ge(S["tk"], 2)
                    act.wait_ge(S["tok"], 2)
                    nc.scalar.activation(gate[:n, ds(i, 1), :].rearrange("p i c -> p (i c)"), bank[:n, 3, 256:256 + 3 * NH], ACT.Sigmoid).then_inc(S["gate"], 1)
                    for j in range(2):
                        act.wait_ge(S["tok"], 3 + j)
                        nc.scalar.activation(zs[:n, 512 * j:512 * (j + 1)], bank[:n, 4 + j, :], ACT.Silu).then_inc(S["z"], 1)

                @block.tensor
                def _(pe):
                    for j, (lo, hi) in enumerate(chunks):
                        for k in range(KD):
                            t = nc.tensor.matmul(bank[:n, 2 + j, 0:hi - lo], hT[:, k, :n], w[:, k, NW + lo:NW + hi], start=k == 0, stop=k == KD - 1)
                        t.then_inc(S["tok"], 1)
                    if prompt:
                        prep.turn(pe, P)
                    for e in range(KD):
                        for k in range(KD):
                            t = nc.tensor.matmul(bank[:, 6 + e // 4, (e % 4) * n:(e % 4 + 1) * n], w[:, k, e * P:(e + 1) * P], hT[:, k, :n], start=k == 0, stop=k == KD - 1)
                        if e % 4 == 3:
                            t.then_inc(S["q"], 1)
                    pe.wait_ge(S["tk"], 2)
                    if prompt:
                        for j in range(4):
                            lo = (2 * KVW if j < 2 else 4 * KVW) + (j % 2) * HD
                            t = nc.tensor.transpose(bank[:HD, 2, j * n:(j + 1) * n], tk[:n, lo:lo + HD], c["ident"][:n, :n])
                    else:
                        for j in range(2):
                            t = nc.tensor.transpose(bank[:, 2, j * n:(j + 1) * n], tk[:n, (2 + 2 * j) * KVW:(3 + 2 * j) * KVW], c["ident"][:n, :n])
                    t.then_inc(S["T2"], 1)

                @block.vector
                def _(dve):
                    V = nc.vector
                    if prompt:
                        prep.norm(dve, P)
                    dve.wait_ge(S["tok"], 1)
                    V.tensor_copy(tk[:n, 0:512], bank[:n, 2, :]).then_inc(S["tk"], 1)
                    dve.wait_ge(S["tok"], 2)
                    V.tensor_copy(tk[:n, 512:768], bank[:n, 3, 0:256]).then_inc(S["tk"], 1)
                    for j in range(2):
                        dve.wait_ge(S["q"], j + 1)
                        V.tensor_scalar(qS[:, 4 * j:4 * j + 4, :n], bank[:, 6 + j, :4 * n].rearrange("p (e t) -> p e t", e=4), NSA_SCALE, None, ALU.mult).then_inc(S["qs"], 1)
                    if prompt:
                        prep.turned(dve, P)
                    dve.wait_ge(S["T2"], 1)
                    if prompt:
                        for j, dst in enumerate((ksT, kwT)):
                            V.tensor_copy(dst[:HD, :, ds(tok0, n)], bank[:HD, 2, 2 * j * n:2 * (j + 1) * n].rearrange("p (g t) -> p g t", g=2)).then_inc(S["kT"], 1)
                    else:
                        V.tensor_copy(kTs[:].rearrange("p j t -> p (j t)"), bank[:, 2, 0:2 * n]).then_inc(S["kT"], 1)

        prep.alone(P, d["x1"][0:P, :])
        with nc.Fori(0, NTILE) as i:
            tile(P, i * P, i, True, lambda sp: d["x1"][ds(sp.snap((i + 1) % NTILE) * P, P), :])
            next_iteration(nc, S.values())
        prep.alone(NS, d["x1"][SEQ:NTOK, :])
        tile(NS, SEQ, NTILE, False)


def compress(nc, a, d, c, o):
    kv, kcT, vc, kcp, vcp = (o[k] for k in ("kv", "kcT", "vc", "kcp", "vcp"))
    bank = c["bank"]
    HP = NPAGE // 2
    with ExitStack() as ctx:
        ctx.callback(nc.all_engine_barrier)
        def sb(name, shape):
            return ctx.enter_context(nc.sbuf_tensor(name, shape, F32))

        phi = sb("cm_phi", [P, 2, HD, P])
        phi2 = sb("cm_phi2", [P, 2, HD])
        pe_sb = sb("cm_pe", [P, 2, HD])
        bias = sb("cm_bias", [P, 2])
        pg = sb("cm_pg", [P, 2, HP, 2 * KVW])
        hid = sb("cm_hid", [P, 2, 2 * HP])
        vT = sb("cm_vT", [HD, NG, 2 * NTILE])
        s_w = cleared(nc, ctx, "cm_s_w")
        s_zero = cleared(nc, ctx, "cm_s_zero")
        names = ["acc", "hid", "out", "ev", "dv"]
        S = {n: cleared(nc, ctx, "cm_s_" + n) for n in names}
        s_half = [[cleared(nc, ctx, f"cm_s_half{i}{j}") for j in range(2)] for i in range(2)]
        QP = HP // 2
        UN = 4

        def load_half(eng, queue, b, hf):
            for j in range(queue * QP, (queue + 1) * QP, UN):
                pages = [eng.value_load(c["pages"][0:1, ds(b * NPAGE + hf * HP + j + i, 1)], min_val=0, max_val=POOL - 1) for i in range(UN)]
                for i, page in enumerate(pages):
                    eng.dma_start(pg[:, hf, j + i, :],
                                  a["cache_nsa_kv"][0, ds(page, 1)].rearrange("a p k g d -> (a p) (k g d)")[:, 0:2 * KVW]).then_inc(s_half[hf][queue], 16)

        def hidden(kind, n, rhs):
            for half in range(2):
                cols = slice(half * HD, (half + 1) * HD)
                for x in range(HD):
                    t = nc.tensor.matmul(bank[cols, kind, 0:n], phi[:, kind, x, cols], rhs(x), start=x == 0, stop=x == HD - 1)
            return t

        with nc.Block() as block:
            @block.gpsimd
            def _(pool):
                nc.gpsimd.memset(phi[BLK:, :, :, 0:HD], 0.0).then_inc(s_zero, 1)

            def load_weights(eng, half):
                rows = slice(half * BLK, (half + 1) * BLK)
                for kind, (p1, p2, pe) in enumerate((("nsa_phi1_k", "nsa_phi2_k", "nsa_pe_k"), ("nsa_phi1_v", "nsa_phi2_v", "nsa_pe_v"))):
                    eng.dma_start(phi[rows, kind, :, half * HD:(half + 1) * HD], a[p1][0].rearrange("(r x) m -> r x m", x=HD)).then_inc(s_w, 16)
                    eng.dma_start(phi2[rows, kind, :], a[p2][0]).then_inc(s_w, 16)
                    eng.dma_start(pe_sb[rows, kind, :], a[pe][0]).then_inc(s_w, 16)

            @block.sync
            def _(sp):
                load_weights(sp, 0)
                load_half(sp, 0, 0, 0)

            @block.scalar
            def _(act):
                load_weights(act, 1)
                load_half(act, 1, 0, 0)
                act.wait_ge(S["acc"], 1)
                nc.scalar.activation(bias[:, 0:1], bank[:, 0, 0:1], ACT.Copy).then_inc(S["hid"], 1)
                nc.scalar.activation(bias[:, 1:2], bank[:, 1, 0:1], ACT.Copy).then_inc(S["hid"], 1)
                act.wait_ge(S["acc"], 3)
                act.wait_ge(S["hid"], 2)
                for kind in range(2):
                    nc.scalar.activation(hid[:, kind, 0:2 * NTILE], bank[:, kind, 0:2 * NTILE], ACT.Silu, bias=bias[:, kind:kind + 1]).then_inc(S["hid"], 1)

            @block.tensor
            def _(pe):
                pe.wait_ge(s_w, 16 * 12)
                pe.wait_ge(s_zero, 2)
                for kind in range(2):
                    t = hidden(kind, 1, lambda x: pe_sb[:, kind, x:x + 1])
                t.then_inc(S["acc"], 1)
                pe.wait_ge(S["hid"], 2)
                for kind in range(2):
                    hidden(kind, 2 * NTILE, lambda x: kv[:, :, kind * KVW:(kind + 1) * KVW].rearrange("p i (g x) -> p i g x", g=NG)[:, :, :, x]).then_inc(S["acc"], 1)
                pe.wait_ge(S["hid"], 4)
                for kind in range(2):
                    for half in range(2):
                        rows = slice(half * HD, (half + 1) * HD)
                        t = nc.tensor.matmul(bank[:HD, 4 + half, kind * 2 * NTILE:(kind + 1) * 2 * NTILE], phi2[rows, kind, :], hid[rows, kind, 0:2 * NTILE], start=True, stop=True)
                t.then_inc(S["out"], 1)
                pe.wait_ge(S["ev"], 4)
                for gg in range(NG):
                    t = nc.tensor.transpose(bank[:2 * NTILE, 6, gg * HD:(gg + 1) * HD], vT[:, gg, :], c["ident"][:HD, :HD])
                t.then_inc(S["out"], 1)

            @block.vector
            def _(dve):
                nc.vector.memset(phi[:BLK, :, :, HD:], 0.0).then_inc(s_zero, 1)
                nc.vector.memset(vcp[:], 0.0).then_inc(S["dv"], 1)
                dve.wait_ge(S["dv"], 1)
                dve.wait_ge(S["out"], 1)
                for half in range(2):
                    for kind, dst in ((0, kcp[:HD]), (1, vT[:])):
                        nc.vector.tensor_copy(dst[:, :, half * NTILE:(half + 1) * NTILE],
                                              bank[:HD, 4 + half, kind * 2 * NTILE:(kind + 1) * 2 * NTILE].rearrange("p (i g) -> p g i", g=NG)).then_inc(S["ev"], 1)
                dve.wait_ge(S["out"], 2)
                nc.vector.tensor_copy(vcp[:2 * NTILE], bank[:2 * NTILE, 6, 0:NG * HD]).then_inc(S["ev"], 1)
        next_iteration(nc, S.values())

        with nc.Fori(0, DB) as b:
            with nc.Block() as block:
                @block.sync
                def _(sp):
                    load_half(sp, 0, b, 1)
                    sp.wait_ge(S["acc"], 2)
                    sp.sem_clear(s_half[0][0])
                    load_half(sp, 0, sp.snap((b + 1) % DB), 0)

                @block.scalar
                def _(act):
                    load_half(act, 1, b, 1)
                    for hf in range(2):
                        for kind in range(2):
                            act.wait_ge(S["acc"], 2 * hf + kind + 1)
                            if hf:
                                act.wait_ge(S["out"], kind + 1)
                            nc.scalar.activation(hid[:, kind, :], bank[:, kind, 0:2 * HP], ACT.Silu, bias=bias[:, kind:kind + 1]).then_inc(S["hid"], 1)
                        if hf == 0:
                            act.sem_clear(s_half[0][1])
                            load_half(act, 1, act.snap((b + 1) % DB), 0)

                @block.tensor
                def _(pe):
                    def products(hf):
                        for kind in range(2):
                            pe.wait_ge(S["hid"], 2 * hf + kind + 1)
                            for half in range(2):
                                rows = slice(half * HD, (half + 1) * HD)
                                for gg in range(NG):
                                    cols = hid[rows, kind, :].rearrange("p (j g) -> p g j", g=NG)[:, gg, :]
                                    if kind == 0:
                                        t = nc.tensor.matmul(bank[gg * HD:(gg + 1) * HD, 4 + half, hf * HP:(hf + 1) * HP], phi2[rows, 0, :], cols, start=True, stop=True)
                                    else:
                                        t = nc.tensor.matmul(bank[hf * HP:(hf + 1) * HP, 6 + half, gg * HD:(gg + 1) * HD], cols, phi2[rows, 1, :], start=True, stop=True)
                            t.then_inc(S["out"], 1)

                    for hf in range(2):
                        pe.wait_ge(s_half[hf][0], 16 * QP)
                        pe.wait_ge(s_half[hf][1], 16 * QP)
                        for kind in range(2):
                            if hf:
                                pe.wait_ge(S["hid"], kind + 1)
                            hidden(kind, 2 * HP, lambda x: pg[:, hf, :, kind * KVW:(kind + 1) * KVW].rearrange("p j (g x) -> p j g x", g=NG)[:, :, :, x]).then_inc(S["acc"], 1)
                            if kind == 1:
                                products(hf)

                @block.vector
                def _(dve):
                    dve.wait_ge(S["out"], 4)
                    for half in range(2):
                        nc.vector.tensor_copy(kcT[:, ds(b, 1), half * NPAGE:(half + 1) * NPAGE].rearrange("p b j -> p (b j)"), bank[:, 4 + half, 0:NPAGE]).then_inc(S["ev"], 1)
                        nc.vector.tensor_copy(vc[:, ds(b, 1), half, :].rearrange("p b c -> p (b c)"), bank[:NPAGE, 6 + half, 0:KVW]).then_inc(S["ev"], 1)
            next_iteration(nc, [*S.values(), *s_half[1]])

        with nc.Block() as block:
            @block.sync
            def _(sp):
                for queue in range(2):
                    sp.wait_ge(s_half[0][queue], 16 * QP)


def nsa_prompt(nc, a, d, c, o):
    kv, ksT, kwT, gate, kcp, vcp, oall = (o[k] for k in ("kv", "ksT", "kwT", "gate", "kcp", "vcp", "oall"))
    bank = c["bank"]
    NC = 2 * NTILE
    with ExitStack() as ctx:
        ctx.callback(nc.all_engine_barrier)
        def sb(name, shape):
            return ctx.enter_context(nc.sbuf_tensor(name, shape, F32))

        qT = sb("np_q", [P, SEQ])
        gh = sb("np_gh", [P, 3, NTILE])
        cmask = sb("np_cmask", [P, NTILE, NC])
        sc = sb("np_sc", [P, NTILE, NC])
        cm = sb("np_cm", [P, 3, NTILE])
        pcT = sb("np_pcT", [P, SEQ])
        coef = sb("np_coef", [P, 2])
        buf = {"p": sb("np_p", [P, 2, SEQ]), "pT": sb("np_pT", [P, 2, SEQ]), "nmax": sb("np_nmax", [P, 2]),
               "den": sb("np_den", [P, 2]), "rden": sb("np_rden", [P, 2])}
        s_tab = cleared(nc, ctx, "np_s_tab")
        s_win = cleared(nc, ctx, "np_s_win")
        s_zero = cleared(nc, ctx, "np_s_zero")
        S = {n: cleared(nc, ctx, "np_s_" + n) for n in ["q", "cs", "cx", "ce", "cp", "ct", "ctt", "cv"] + ATT_SEMS}

        with nc.Block() as block:
            @block.sync
            def _(sp):
                sp.dma_start(cmask[:], a["c_cmask"]).then_inc(s_tab, 16)
                sp.wait_ge(s_zero, 2)
                for gg in range(NG):
                    sp.dma_start(kcp[HD:HD + 1, gg, :], a["c_cpos"]).then_inc(s_tab, 16)
                sp.dma_start(a["o_nsa_win_sample"][0, :, 0:WIN - DT].rearrange("b t k g d -> b (t k g d)"),
                             a["state_nsa_win"][0, :, DT:WIN].rearrange("b t k g d -> b (t k g d)")).then_inc(s_win, 16)
                sp.wait_ge(s_tab, 48)

            @block.vector
            def _(dve):
                nc.vector.memset(qT[HD:HQ], 0.0).then_inc(s_zero, 1)
                nc.vector.memset(kcp[HD:HQ], 0.0).then_inc(s_zero, 1)
                nc.vector.memset(pcT[:], 0.0).then_inc(s_zero, 1)
                dve.wait_ge(s_zero, 3)

        for gg in range(NG):
            with nc.Fori(gg * NR, (gg + 1) * NR) as h:
                with nc.Block() as block:
                    @block.sync
                    def _(sp):
                        sp.dma_start(qT[:HD, :], d["qT"][ds(h * HD, HD), 0:SEQ]).then_inc(S["q"], 16)
                        sp.dma_start(qT[HD:HD + 1, :], a["c_slope"][ds(h, 1), :]).then_inc(S["q"], 16)

                    def pe_before(pe):
                        pe.wait_ge(S["q"], 32)
                        for i in range(NTILE):
                            t = nc.tensor.matmul(bank[:, 7, i * NC:(i + 1) * NC], qT[:HQ, i * P:(i + 1) * P], kcp[:HQ, gg, :], start=True, stop=True)
                        t.then_inc(S["cs"], 1)

                    def dve_before(dve, link):
                        link(nc.vector.tensor_copy(gh[:], gate[:, 0:NTILE, :].rearrange("p i (b h) -> p b i h", b=3)[:, :, :, ds(h, 1)].rearrange("p b i h -> p b (i h)")))

                    def cmp_max(dve, link):
                        V = nc.vector
                        dve.wait_ge(S["cs"], 1)
                        link(V.tensor_tensor(sc[:], bank[:, 7, 0:NTILE * NC].rearrange("p (i n) -> p i n", i=NTILE), cmask[:], ALU.add))
                        link(V.tensor_reduce(cm[:, 0], sc[:], AX, ALU.max))
                        link(V.tensor_scalar(cm[:, 0], cm[:, 0], -1e20, None, ALU.max))
                        V.tensor_tensor(sc[:], sc[:], cm[:, 0].unsqueeze(2).broadcast_to((P, NTILE, NC)), ALU.subtract).then_inc(S["cx"], 1)

                    def cmp_exp(act):
                        act.wait_ge(S["cx"], 1)
                        nc.scalar.activation(sc[:], sc[:], ACT.Exp).then_inc(S["ce"], 1)

                    def cmp_norm(dve, link):
                        V = nc.vector
                        dve.wait_ge(S["ce"], 1)
                        link(V.tensor_reduce(cm[:, 1], sc[:], AX, ALU.add))
                        link(V.tensor_scalar(cm[:, 1], cm[:, 1], 1e-30, None, ALU.max))
                        link(V.reciprocal(cm[:, 2], cm[:, 1]))
                        link(V.tensor_tensor(cm[:, 2], cm[:, 2], gh[:, 0], ALU.mult))
                        V.tensor_tensor(sc[:], sc[:], cm[:, 2].unsqueeze(2).broadcast_to((P, NTILE, NC)), ALU.mult).then_inc(S["cp"], 1)

                    def cmp_turn(half):
                        def f(pe):
                            pe.wait_ge(S["cp"], 1)
                            if half:
                                pe.wait_ge(S["ctt"], 1)
                            for i in range(4):
                                t = nc.tensor.transpose(bank[:NC, 7, i * P:(i + 1) * P], sc[:, 4 * half + i, :], c["ident"][:])
                            t.then_inc(S["ct"], 1)
                        return f

                    def cmp_turned(half):
                        def f(dve, link):
                            dve.wait_ge(S["ct"], half + 1)
                            nc.vector.tensor_copy(pcT[:NC, half * 512:(half + 1) * 512], bank[:NC, 7, :]).then_inc(S["ctt"], 1)
                        return f

                    def cmp_values(pe):
                        pe.wait_ge(S["ctt"], 2)
                        for i in range(NTILE):
                            for lo in range(0, P, HD):
                                t = nc.tensor.matmul(bank[lo:lo + HD, 7, i * HD:(i + 1) * HD], pcT[:, i * P + lo:i * P + lo + HD], vcp[:, gg * HD:(gg + 1) * HD], start=True, stop=True)
                        t.then_inc(S["cv"], 1)

                    def cmp_add(dve, link):
                        dve.wait_ge(S["cv"], 1)
                        dve.wait_ge(S["o"], NTILE + 1)
                        dst = oall[:, :, ds(h * HD, HD)]
                        link(nc.vector.tensor_tensor(dst, bank[:, 7, :].rearrange("p (i x) -> p i x", i=NTILE), dst, ALU.add))

                    side = {("dve", 0): cmp_max, ("act", 0): cmp_exp, ("dve", 1): cmp_norm, ("pe", 2): cmp_turn(0), ("dve", 3): cmp_turned(0),
                            ("pe", 4): cmp_turn(1), ("dve", 5): cmp_turned(1), ("pe", 6): cmp_values, ("dve", NTILE + 2): cmp_add}

                    def finish(i, branch):
                        def f(o_ps, r, link):
                            link(nc.vector.tensor_tensor(coef[:, 0:1], r, gh[:, branch, i:i + 1], ALU.mult))
                            dst = oall[:, i, ds(h * HD, HD)]
                            if branch == 1:
                                return nc.vector.tensor_scalar(dst, o_ps, coef[:, 0:1], None, ALU.mult)
                            return nc.vector.scalar_tensor_tensor(out=dst, in0=o_ps, scalar=coef[:, 0:1], in1=dst, op0=ALU.mult, op1=ALU.add)
                        return f

                    units = []
                    for i in range(NTILE):
                        units.append({"q0": i * P, "nblk": i + 1, "kT": ksT[:HQ, gg, :], "masks": [(i * P, c["causal"][:])], "finish": finish(i, 1),
                                      "v": lambda b: kv[:, b, 3 * KVW + gg * HD:3 * KVW + (gg + 1) * HD]})
                    for i in range(NTILE):
                        b0 = max(0, i - WIN // P)
                        masks = [((i - b0) * P, c["causal"][:])] + ([(0, c["winlow"][:])] if i >= WIN // P else [])
                        units.append({"q0": i * P, "nblk": i - b0 + 1, "kT": kwT[:HQ, gg, b0 * P:], "masks": masks, "finish": finish(i, 2),
                                      "v": lambda b, b0=b0: kv[:, b0 + b, 5 * KVW + gg * HD:5 * KVW + (gg + 1) * HD]})
                    buf.update(pe_before=pe_before, dve_before=dve_before, qk_ready=0, side=side)
                    attention(nc, c, block, S, buf, units, qT, HQ)
                next_iteration(nc, S.values())

        with nc.Block() as block:
            @block.sync
            def _(sp):
                sp.wait_ge(s_win, 16)


def nsa_sample(nc, a, d, c, o):
    kTs, kcT, vc = (o[k] for k in ("kTs", "kcT", "vc"))
    bank = c["bank"]
    NQ = NH * DT
    GP = 4
    NG4 = NPAGE // GP
    AHEAD = 8
    ACT_GROUPS = 3
    SIDE = 6
    SEL = NBLK + 1
    with ExitStack() as ctx:
        ctx.callback(nc.all_engine_barrier)
        def sb(name, shape):
            return ctx.enter_context(nc.sbuf_tensor(name, shape, F32))

        qall = sb("ns_qall", [P, NR, NS])
        q = sb("ns_q", [P, NQ])
        pg = sb("ns_pg", [P, NPAGE, 2 * KVW])
        kT = sb("ns_kT", [P, 2, 512])
        s = sb("ns_s", [NQ, PAST])
        sn = sb("ns_sn", [NQ, 2, DT])
        pT = sb("ns_pT", [P, 2, 512])
        pnT = sb("ns_pnT", [DT, 2, NQ])
        vnew = sb("ns_vnew", [DT, 2, KVW])
        calibi = sb("ns_calibi", [NQ, NBLK])
        bonus = sb("ns_bonus", [NQ, SEL])
        balibi = sb("ns_balibi", [NQ, SEL])
        kalibi = sb("ns_kalibi", [NQ, BLK])
        nalibi = sb("ns_nalibi", [NQ, DT])
        walibi = sb("ns_walibi", [NQ, WIN])
        same = sb("ns_same", [NQ, NQ])
        pc = sb("ns_pc", [NQ, NBLK])
        pcT = sb("ns_pcT", [NPAGE, 2, NQ])
        vcb = sb("ns_vcb", [NPAGE, 2, KVW])
        score = sb("ns_score", [NQ, SEL])
        left = sb("ns_left", [NQ, 2, SEL])
        top = sb("ns_top", [NQ, 2, 8])
        selb = sb("ns_selb", [NQ, SEL])
        st = sb("ns_st", [NQ, 8])
        gmax = sb("ns_gmax", [NQ, NG4 + 1])
        gden = sb("ns_gden", [NQ, NG4 + 1])
        win = sb("ns_win", [P, WIN // P, 2 * KVW])
        sw = sb("ns_sw", [NQ, WIN])
        wden = sb("ns_wden", [NQ, 2])
        wmax = sb("ns_wmax", [NQ, 3])
        wT = sb("ns_wT", [P, WIN // P * NQ])
        kwin = sb("ns_kwin", [P, WIN])
        ob = sb("ns_ob", [NQ, 3, HD])
        s_w = cleared(nc, ctx, "ns_s_w")
        s_zero = cleared(nc, ctx, "ns_s_zero")
        names = ["q", "new", "cs", "cx", "ce", "pc", "pcT", "imp", "sel", "co", "tr", "kT", "sc", "s", "mx", "exp", "pt", "pT", "pv", "ob", "st", "dv",
                 "wt", "wk", "ws", "wx", "we", "wp", "wpT", "wo", "nk", "sb"]
        S = {n: cleared(nc, ctx, "ns_s_" + n) for n in names}
        s_group = [cleared(nc, ctx, f"ns_s_group{i}") for i in range(NG4)]

        def load_group(eng, b, gi, js=range(GP)):
            pages = [eng.value_load(c["pages"][0:1, ds(b * NPAGE + GP * gi + j, 1)], min_val=0, max_val=POOL - 1) for j in js]
            for j, page in zip(js, pages):
                eng.dma_start(pg[:, GP * gi + j, :], a["cache_nsa_kv"][0, ds(page, 1)].rearrange("a p k g d -> (a p) (k g d)")[:, 2 * KVW:4 * KVW]).then_inc(s_group[gi], 16)

        def load_rest(eng, b):
            for gi in range(AHEAD, NG4 - ACT_GROUPS):
                load_group(eng, b, gi)

        def load_next(eng, b, queue):
            nxt = eng.snap((b + 1) % DB)
            for gi in range(queue, AHEAD, 2):
                eng.wait_ge(S["pv"], gi + 1)
                eng.sem_clear(s_group[gi])
                load_group(eng, nxt, gi)

        with nc.Block() as block:
            @block.scalar
            def _(act):
                for dst, key in ((calibi, "c_calibi"), (bonus, "c_bonus"), (balibi, "c_balibi"), (kalibi, "c_kalibi"), (nalibi, "c_nalibi"),
                                 (walibi, "c_walibi"), (same, "c_same")):
                    act.dma_start(dst[:], a[key]).then_inc(s_w, 16)
                for gg in range(NG):
                    act.dma_start(qall[gg * HD:(gg + 1) * HD], d["qT"].rearrange("(g r x) t -> g x r t", g=NG, x=HD)[gg][:, :, SEQ:NTOK]).then_inc(s_w, 16)
                for gi in range(1, AHEAD, 2):
                    load_group(act, 0, gi)
                act.wait_ge(s_w, 16 * 9)

            @block.sync
            def _(sp):
                for gi in range(0, AHEAD, 2):
                    load_group(sp, 0, gi)

            @block.vector
            def _(dve):
                nc.vector.memset(q[:], 0.0).then_inc(s_zero, 1)
                dve.wait_ge(s_zero, 1)

        with nc.Fori(0, DB) as b:
            with nc.Block() as block:
                @block.sync
                def _(sp):
                    sp.dma_start(win[:], a["state_nsa_win"][0, ds(b, 1)].rearrange("b (i p) k g d -> p (b i) (k g d)", p=P)).then_inc(S["new"], 16)
                    sp.dma_start(vnew[:, 0, :], a["o_nsa_rows_sample"][0, ds(b, 1)].rearrange("b t k g d -> (b t) (k g d)")[:, 3 * KVW:4 * KVW]).then_inc(S["new"], 16)
                    sp.dma_start(vnew[:, 1, :], a["o_nsa_win_sample"][0, ds(b, 1), WIN - DT:WIN].rearrange("b t k g d -> (b t) (k g d)")[:, KVW:2 * KVW]).then_inc(S["new"], 16)
                    load_rest(sp, b)
                    load_next(sp, b, 0)

                @block.gpsimd
                def _(pool):
                    pool.wait_ge(S["sel"], 1)
                    for gi in range(NG4):
                        pool.wait_ge(S["s"], gi + 1)
                        cols = s[:, gi * 512:(gi + 1) * 512].rearrange("p (n k) -> p n k", k=BLK)
                        nc.gpsimd.tensor_tensor(cols, cols, selb[:, gi * 8:(gi + 1) * 8].unsqueeze(2).broadcast_to((NQ, 512 // BLK, BLK)), ALU.add).then_inc(S["sb"], 1)

                @block.scalar
                def _(act):
                    act.wait_ge(S["cx"], 1)
                    nc.scalar.activation(pc[:], pc[:], ACT.Exp, bias=st[:, 0:1], accum_out=st[:, 1:2]).then_inc(S["ce"], 1)

                    def keys(gi):
                        act.wait_ge(S["tr"], gi + 1)
                        if gi >= 2:
                            act.wait_ge(S["sc"], gi - 1)
                        nc.scalar.activation(kT[:, gi % 2, :], bank[:, gi % 2, :], ACT.Copy).then_inc(S["kT"], 1)

                    keys(0)
                    act.wait_ge(S["wx"], 1)
                    nc.scalar.activation(sw[:], sw[:], ACT.Exp, bias=wmax[:, 2:3], accum_out=wden[:, 0:1]).then_inc(S["we"], 1)
                    nc.scalar.activation(sn[:, 1], sn[:, 1], ACT.Exp, bias=wmax[:, 2:3], accum_out=wden[:, 1:2]).then_inc(S["we"], 1)
                    late = [(NG4 - ACT_GROUPS + n // GP, n % GP) for n in range(ACT_GROUPS * GP)]
                    for gi in range(1, NG4):
                        keys(gi)
                        if gi >= 2 and gi - 2 < len(late):
                            load_group(act, b, late[gi - 2][0], [late[gi - 2][1]])
                    act.wait_ge(S["mx"], NG4 + 2)
                    nc.scalar.activation(sn[:, 0], sn[:, 0], ACT.Exp, bias=st[:, 4:5], accum_out=gden[:, NG4:NG4 + 1]).then_inc(S["exp"], 1)
                    for gi in range(NG4):
                        cols = slice(gi * 512, (gi + 1) * 512)
                        nc.scalar.activation(s[:, cols], s[:, cols], ACT.Exp, bias=st[:, 4:5], accum_out=gden[:, gi:gi + 1]).then_inc(S["exp"], 1)
                    load_next(act, b, 1)
                    act.wait_ge(S["ob"], 6)
                    act.dma_start(d["os"][ds(b, 1)].rearrange("b m k x -> (b m) k x"), ob[:]).then_inc(S["st"], 16)
                    act.wait_ge(S["st"], 16)

                @block.tensor
                def _(pe):
                    ident = c["ident"]
                    pe.wait_ge(S["q"], 2)
                    nc.tensor.matmul(bank[:NQ, 4, 0:NBLK], q[:], kcT[:, ds(b, 1), :].rearrange("p b j -> p (b j)"), start=True, stop=True).then_inc(S["cs"], 1)
                    for j in range(2):
                        t = nc.tensor.matmul(bank[:NQ, 5, j * DT:(j + 1) * DT], q[:], kTs[:, j, ds(b * DT, DT)], start=True, stop=True)
                    t.then_inc(S["nk"], 1)
                    def turn(gi):
                        pe.wait_ge(s_group[gi], 16 * GP)
                        if gi >= 2:
                            pe.wait_ge(S["kT"], gi - 1)
                        for j in range(GP):
                            t = nc.tensor.transpose(bank[:, gi % 2, j * P:(j + 1) * P], pg[:, GP * gi + j, 0:KVW], ident[:])
                        t.then_inc(S["tr"], 1)

                    def score(gi):
                        pe.wait_ge(S["kT"], gi + 1)
                        if gi >= 2:
                            pe.wait_ge(S["s"], gi - 1)
                        nc.tensor.matmul(bank[:NQ, 2 + gi % 2, :], q[:], kT[:, gi % 2, :], start=True, stop=True).then_inc(S["sc"], 1)

                    turn(0)
                    pe.wait_ge(S["new"], 48)
                    for i in range(WIN // P):
                        t = nc.tensor.transpose(bank[:, 6, i * P:(i + 1) * P], win[:, i, 0:KVW], ident[:])
                    t.then_inc(S["wt"], 1)
                    pe.wait_ge(S["wk"], 1)
                    nc.tensor.matmul(bank[:NQ, 7, :], q[:], kwin[:], start=True, stop=True).then_inc(S["ws"], 1)
                    turn(1)
                    score(0)
                    pe.wait_ge(S["pc"], 1)
                    nc.tensor.matmul(bank[:NQ, 4, 0:NBLK], same[:], pc[:], start=True, stop=True).then_inc(S["imp"], 1)
                    for half in range(2):
                        t = nc.tensor.transpose(bank[:NPAGE, 6, half * NQ:(half + 1) * NQ], pc[:, half * NPAGE:(half + 1) * NPAGE], ident[:NQ, :NQ])
                    t.then_inc(S["imp"], 1)

                    for gi in range(1, NG4):
                        if gi + 1 < NG4:
                            turn(gi + 1)
                        score(gi)
                        if gi == SIDE:
                            pe.wait_ge(S["pcT"], 2)
                            for half in range(2):
                                t = nc.tensor.matmul(bank[:NQ, 4, 256:256 + KVW], pcT[:, half, :], vcb[:, half, :], start=half == 0, stop=half == 1)
                            t.then_inc(S["co"], 1)
                            pe.wait_ge(S["we"], 2)
                            for i in range(WIN // P):
                                nc.tensor.transpose(bank[:, 6, i * NQ:(i + 1) * NQ], sw[:, i * P:(i + 1) * P], ident[:NQ, :NQ])
                            nc.tensor.transpose(bank[:DT, 6, 256:256 + NQ], sn[:, 1], ident[:NQ, :NQ]).then_inc(S["wp"], 1)
                            pe.wait_ge(S["wpT"], 2)
                            for i in range(WIN // P):
                                nc.tensor.matmul(bank[:NQ, 7, 0:KVW], wT[:, i * NQ:(i + 1) * NQ], win[:, i, KVW:2 * KVW], start=i == 0, stop=False)
                            nc.tensor.matmul(bank[:NQ, 7, 0:KVW], pnT[:, 1, :], vnew[:, 1, :], start=False, stop=True).then_inc(S["wo"], 1)

                    def probs(gi):
                        pe.wait_ge(S["exp"], gi + 2)
                        if gi >= 2:
                            pe.wait_ge(S["pT"], gi - 1)
                        for j in range(GP):
                            t = nc.tensor.transpose(bank[:, gi % 2, j * NQ:(j + 1) * NQ], s[:, (GP * gi + j) * P:(GP * gi + j + 1) * P], ident[:NQ, :NQ])
                        t.then_inc(S["pt"], 1)

                    pe.wait_ge(S["exp"], 1)
                    nc.tensor.transpose(bank[:DT, 6, 0:NQ], sn[:, 0], ident[:NQ, :NQ]).then_inc(S["pt"], 1)
                    probs(0)
                    for gi in range(NG4):
                        if gi + 1 < NG4:
                            probs(gi + 1)
                        pe.wait_ge(S["pT"], gi + 2)
                        if gi == 0:
                            nc.tensor.matmul(bank[:NQ, 3, 0:KVW], pnT[:, 0, :], vnew[:, 0, :], start=True, stop=False)
                        for j in range(GP):
                            t = nc.tensor.matmul(bank[:NQ, 3, 0:KVW], pT[:, gi % 2, j * NQ:(j + 1) * NQ], pg[:, GP * gi + j, KVW:2 * KVW],
                                                 start=False, stop=gi == NG4 - 1 and j == GP - 1)
                        t.then_inc(S["pv"], 1)

                @block.vector
                def _(dve):
                    link = Chain(dve, S["dv"])
                    V = nc.vector

                    def output(branch, b_ix, r, col=0):
                        for gg in range(NG):
                            rows = slice(gg * NQ // 2, (gg + 1) * NQ // 2)
                            V.tensor_scalar(ob[rows, branch, :], bank[rows, b_ix, col + gg * HD:col + (gg + 1) * HD], r[rows], None, ALU.mult).then_inc(S["ob"], 1)

                    for gg in range(NG):
                        rows = slice(gg * HD, (gg + 1) * HD)
                        V.tensor_copy(q[rows, gg * NQ // 2:(gg + 1) * NQ // 2].rearrange("p (r t) -> p r t", t=DT), qall[rows, :, ds(b * DT, DT)]).then_inc(S["q"], 1)
                    dve.wait_ge(S["cs"], 1)
                    link(V.tensor_tensor(pc[:], bank[:NQ, 4, 0:NBLK], calibi[:], ALU.add))
                    V.tensor_reduce(st[:, 0:1], pc[:], AX, ALU.max, negate=True).then_inc(S["cx"], 1)
                    dve.wait_ge(S["nk"], 1)
                    link(V.tensor_tensor(sn[:], bank[:NQ, 5, 0:2 * DT].rearrange("p (j t) -> p j t", j=2), nalibi[:].unsqueeze(1).broadcast_to((NQ, 2, DT)), ALU.add))
                    dve.wait_ge(S["wt"], 1)
                    V.tensor_copy(kwin[:], bank[:, 6, :]).then_inc(S["wk"], 1)
                    dve.wait_ge(S["ce"], 1)
                    link(V.reciprocal(st[:, 2:3], st[:, 1:2]))
                    V.tensor_scalar(pc[:], pc[:], st[:, 2:3], None, ALU.mult).then_inc(S["pc"], 1)
                    dve.wait_ge(S["ws"], 1)
                    link(V.tensor_tensor(sw[:], bank[:NQ, 7, :], walibi[:], ALU.add))
                    link(V.tensor_reduce(wmax[:, 0:1], sw[:], AX, ALU.max))
                    link(V.tensor_reduce(wmax[:, 1:2], sn[:, 1], AX, ALU.max))
                    V.tensor_reduce(wmax[:, 2:3], wmax[:, 0:2], AX, ALU.max, negate=True).then_inc(S["wx"], 1)
                    def add_keys(gi):
                        dve.wait_ge(S["sc"], gi + 1)
                        V.tensor_tensor(s[:, gi * 512:(gi + 1) * 512].rearrange("p (n k) -> p n k", k=BLK), bank[:NQ, 2 + gi % 2, :].rearrange("p (n k) -> p n k", k=BLK),
                                        kalibi[:].unsqueeze(1).broadcast_to((NQ, 512 // BLK, BLK)), ALU.add).then_inc(S["s"], 1)

                    def maximum(gi):
                        dve.wait_ge(S["sb"], gi + 1)
                        V.tensor_reduce(gmax[:, gi:gi + 1], s[:, gi * 512:(gi + 1) * 512], AX, ALU.max).then_inc(S["mx"], 1)

                    add_keys(0)
                    dve.wait_ge(S["imp"], 2)
                    link(V.tensor_tensor(score[:, 0:NBLK].rearrange("p (j f) -> p f j", f=2), bank[:NQ, 4, 0:NBLK].rearrange("p (f j) -> p f j", f=2),
                                         bonus[:, 0:NBLK].rearrange("p (j f) -> p f j", f=2), ALU.add))
                    link(V.tensor_copy(score[:, NBLK:SEL], bonus[:, NBLK:SEL]))
                    link(V.max(top[:, 0], score[:]))
                    link(V.match_replace(out=left[:, 0], in_to_replace=top[:, 0], in_values=score[:], imm_value=NEG))
                    link(V.max(top[:, 1], left[:, 0]))
                    link(V.match_replace(out=left[:, 1], in_to_replace=top[:, 1], in_values=left[:, 0], imm_value=NEG))
                    link(V.tensor_scalar(selb[:], left[:, 1], NEG / 2, NEG, ALU.is_gt, ALU.mult))
                    V.tensor_tensor(selb[:], selb[:], balibi[:], ALU.add).then_inc(S["sel"], 1)
                    dve.wait_ge(S["sel"], 1)
                    V.tensor_copy(vcb[:].rearrange("p f c -> p (f c)"), vc[:, ds(b, 1), :, :].rearrange("p b f c -> p (b f c)")).then_inc(S["pcT"], 1)
                    V.tensor_copy(pcT[:].rearrange("p f m -> p (f m)"), bank[:NPAGE, 6, 0:2 * NQ]).then_inc(S["pcT"], 1)
                    link(V.tensor_scalar(sn[:, 0], sn[:, 0], selb[:, NBLK:SEL], None, ALU.add))
                    for gi in range(1, NG4):
                        add_keys(gi)
                        maximum(gi - 1)
                        if gi == SIDE:
                            dve.wait_ge(S["co"], 1)
                            for gg in range(NG):
                                rows = slice(gg * NQ // 2, (gg + 1) * NQ // 2)
                                V.tensor_copy(ob[rows, 0, :], bank[rows, 4, 256 + gg * HD:256 + (gg + 1) * HD]).then_inc(S["ob"], 1)
                            dve.wait_ge(S["wp"], 1)
                            V.tensor_copy(wT[:], bank[:, 6, 0:WIN // P * NQ]).then_inc(S["wpT"], 1)
                            V.tensor_copy(pnT[:, 1, :], bank[:DT, 6, 256:256 + NQ]).then_inc(S["wpT"], 1)
                            dve.wait_ge(S["we"], 2)
                            link(V.tensor_reduce(st[:, 5:6], wden[:], AX, ALU.add))
                            link(V.reciprocal(st[:, 6:7], st[:, 5:6]))
                            dve.wait_ge(S["wo"], 1)
                            output(2, 7, st[:, 6:7])
                    maximum(NG4 - 1)
                    V.tensor_reduce(gmax[:, NG4:NG4 + 1], sn[:, 0], AX, ALU.max).then_inc(S["mx"], 1)
                    dve.wait_ge(S["mx"], NG4 + 1)
                    V.tensor_reduce(st[:, 4:5], gmax[:], AX, ALU.max, negate=True).then_inc(S["mx"], 1)
                    dve.wait_ge(S["pt"], 1)
                    V.tensor_copy(pnT[:, 0, :], bank[:DT, 6, 0:NQ]).then_inc(S["pT"], 1)
                    for gi in range(NG4):
                        dve.wait_ge(S["pt"], gi + 2)
                        if gi >= 2:
                            dve.wait_ge(S["pv"], gi - 1)
                        V.tensor_copy(pT[:, gi % 2, 0:GP * NQ], bank[:, gi % 2, 0:GP * NQ]).then_inc(S["pT"], 1)
                    dve.wait_ge(S["exp"], NG4 + 1)
                    link(V.tensor_reduce(st[:, 5:6], gden[:], AX, ALU.add))
                    link(V.reciprocal(st[:, 7:8], st[:, 5:6]))
                    dve.wait_ge(S["pv"], NG4)
                    output(1, 3, st[:, 7:8])
            next_iteration(nc, [*S.values(), *s_group[AHEAD:]])

        with nc.Block() as block:
            @block.sync
            def _(sp):
                for gi in range(AHEAD):
                    sp.wait_ge(s_group[gi], 16 * GP)


def odd_output(nc, a, d, c, o):
    gate, oall = o["gate"], o["oall"]
    bank = c["bank"]
    with ExitStack() as ctx:
        ctx.callback(nc.all_engine_barrier)
        def sb(name, shape):
            return ctx.enter_context(nc.sbuf_tensor(name, shape, F32))

        wo = sb("oo_wo", [P, KD, D_MODEL])
        gf = sb("oo_gf", [P, D_MODEL])
        z = sb("oo_z", [P, NW])
        x = sb("oo_x", [P, D_MODEL])
        m = sb("oo_m", [P, NW])
        mT = sb("oo_mT", [P, KD, P])
        x2 = sb("oo_x2", [P, D_MODEL])
        y = sb("oo_y", [P, D_MODEL])
        os = sb("oo_os", [NS, 3, NH, HD])
        st = sb("oo_st", [P, 4])
        s_w = cleared(nc, ctx, "oo_s_w")
        s_os = cleared(nc, ctx, "oo_s_os")
        names = ["z", "x", "m", "T", "mT", "mm", "x2", "ss", "ms", "sd", "y", "st", "dv"]
        S = {n: cleared(nc, ctx, "oo_s_" + n) for n in names}

        with nc.Block() as block:
            @block.sync
            def _(sp):
                for k in range(KD):
                    sp.dma_start(wo[:, k], a["w_out_odd"][0, k * P:(k + 1) * P, :]).then_inc(s_w, 16)
                sp.dma_start(gf[:], a["norm_final"].partition_broadcast(P)).then_inc(s_w, 16)
                for b in range(DB):
                    for k in range(3):
                        sp.dma_start(os[DT * b:DT * (b + 1), k], d["os"][b, :, k, :].rearrange("(h t) x -> t h x", t=DT)).then_inc(s_os, 16)
                sp.wait_ge(s_w, 16 * (KD + 1))
                sp.wait_ge(s_os, 16 * 3 * DB)

        def prep_load(sp, n, tok0):
            sp.dma_start(z[:n], d["z"][ds(tok0, n), :]).then_inc(S["z"], 16)

        def prep_gate(dve, n, src):
            dve.wait_ge(S["z"], 16)
            nc.vector.tensor_tensor(m[:n], src, z[:n], ALU.mult).then_inc(S["m"], 1)

        def prep_turn(pe, n):
            pe.wait_ge(S["m"], 1)
            for k in range(KD):
                t = nc.tensor.transpose(bank[:, k // 4, (k % 4) * n:(k % 4 + 1) * n], m[:n, k * P:(k + 1) * P], c["ident"][:n, :n])
            t.then_inc(S["T"], 1)

        def prep_turned(dve, n):
            dve.wait_ge(S["T"], 1)
            for b in range(2):
                nc.vector.tensor_copy(mT[:, 4 * b:4 * b + 4, :n], bank[:, b, :4 * n].rearrange("p (k t) -> p k t", k=4)).then_inc(S["mT"], 1)

        def main_load(sp, n, tok0):
            sp.dma_start(x[:n], d["x1"][ds(tok0, n), :]).then_inc(S["x"], 16)

        def main_products(pe, n):
            for hf in range(2):
                for k in range(KD):
                    t = nc.tensor.matmul(bank[:n, 2 + hf, :], mT[:, k, :n], wo[:, k, hf * 512:(hf + 1) * 512], start=k == 0, stop=k == KD - 1)
                t.then_inc(S["mm"], 1)

        def main_add(dve, n):
            dve.wait_ge(S["x"], 16)
            for hf in range(2):
                dve.wait_ge(S["mm"], hf + 1)
                cols = slice(hf * 512, (hf + 1) * 512)
                nc.vector.tensor_tensor(x2[:n, cols], x[:n, cols], bank[:n, 2 + hf, :], ALU.add).then_inc(S["x2"], 1)

        def final_squares(act, n):
            nc.scalar.activation(y[:n], x2[:n], ACT.Square, accum_out=st[:n, 0:1]).then_inc(S["ss"], 1)
            act.wait_ge(S["ms"], 1)
            nc.scalar.activation(st[:n, 2:3], st[:n, 1:2], ACT.Sqrt).then_inc(S["sd"], 1)

        def final_norm(dve, link, n):
            V = nc.vector
            dve.wait_ge(S["ss"], 1)
            V.tensor_scalar(st[:n, 1:2], st[:n, 0:1], 1.0 / D_MODEL, EPS, ALU.mult, ALU.add).then_inc(S["ms"], 1)
            dve.wait_ge(S["sd"], 1)
            link(V.reciprocal(st[:n, 3:4], st[:n, 2:3]))
            V.scalar_tensor_tensor(out=y[:n], in0=x2[:n], scalar=st[:n, 3:4], in1=gf[:n], op0=ALU.mult, op1=ALU.mult).then_inc(S["y"], 1)

        def final_store(sp, n, dst):
            sp.wait_ge(S["y"], 1)
            sp.dma_start(dst, y[:n]).then_inc(S["st"], 16)
            sp.wait_ge(S["st"], 16)

        def iteration(after=None, now=None, before=None):
            with nc.Block() as block:
                @block.sync
                def _(sp):
                    if now:
                        main_load(sp, now[0], now[1])
                    if after:
                        prep_load(sp, after[0], after[1])
                    if before:
                        final_store(sp, before[0], before[1](sp))

                @block.tensor
                def _(pe):
                    if now:
                        main_products(pe, now[0])
                    if after:
                        prep_turn(pe, after[0])

                @block.scalar
                def _(act):
                    if before:
                        final_squares(act, before[0])

                @block.vector
                def _(dve):
                    link = Chain(dve, S["dv"])
                    if after:
                        prep_gate(dve, after[0], after[2](dve, link))
                    if before:
                        final_norm(dve, link, before[0])
                        dve.wait_ge(S["y"], 1)
                    if now:
                        main_add(dve, now[0])
                    if after:
                        if now:
                            dve.wait_ge(S["mm"], 2)
                        prep_turned(dve, after[0])
            next_iteration(nc, S.values())

        def prompt_rows(i):
            return lambda dve, link: oall[:, ds(i, 1), :].rearrange("p i c -> p (i c)")

        def sample_rows(dve, link):
            V = nc.vector
            gs = gate[:NS, NTILE, :].rearrange("p (k h) -> p k h", k=3)
            for k in range(3):
                link(V.tensor_tensor(os[:, k], os[:, k], gs[:, k].unsqueeze(2).broadcast_to((NS, NH, HD)), ALU.mult))
            link(V.tensor_tensor(os[:, 0], os[:, 0], os[:, 1], ALU.add))
            link(V.tensor_tensor(os[:, 0], os[:, 0], os[:, 2], ALU.add))
            return os[:, 0].rearrange("p h x -> p (h x)")

        def prompt_out(i):
            return lambda sp: a["o_y_prompt"][0, ds(sp.snap(i * P) if not isinstance(i, int) else i * P, P), :]

        iteration(after=(P, 0, prompt_rows(0)))
        iteration(after=(P, P, prompt_rows(1)), now=(P, 0))
        with nc.Fori(1, NTILE - 1) as i:
            iteration(after=(P, (i + 1) * P, prompt_rows(i + 1)), now=(P, i * P), before=(P, prompt_out(i - 1)))
        iteration(after=(NS, SEQ, sample_rows), now=(P, (NTILE - 1) * P), before=(P, prompt_out(NTILE - 2)))
        iteration(now=(NS, SEQ), before=(P, prompt_out(NTILE - 1)))
        iteration(before=(NS, lambda sp: a["o_y_sample"].rearrange("b t d -> (b t) d")))


def build(nc, a):
    d = {
        "u": nc.dram_tensor("u_scratch", [SW, CH, NCH], F32, kind="Internal").ap(),
        "us": nc.dram_tensor("us_scratch", [SW, DT, DB], F32, kind="Internal").ap(),
        "y": nc.dram_tensor("y_scratch", [SW, CH, NCH], F32, kind="Internal").ap(),
        "ys": nc.dram_tensor("ys_scratch", [SW, DT, DB], F32, kind="Internal").ap(),
        "z": nc.dram_tensor("z_scratch", [NTOK, NW], F32, kind="Internal").ap(),
        "qT": nc.dram_tensor("qT_scratch", [NW, NTOK], F32, kind="Internal").ap(),
        "os": nc.dram_tensor("os_scratch", [DB, NH * DT, 3, HD], F32, kind="Internal").ap(),
        "x1": nc.dram_tensor("x1_scratch", [NTOK, D_MODEL], F32, kind="Internal").ap(),
    }
    with ExitStack() as ctx:
        def sb(name, shape, dt=F32):
            return ctx.enter_context(nc.sbuf_tensor(name, shape, dt))

        c = {"ident": sb("ident", [P, P]), "causal": sb("causal", [P, P]), "winlow": sb("winlow", [P, P]),
             "pages": sb("pages", [1, DB * NPAGE], I32),
             "bank": ctx.enter_context(nc.psum_tensor("bank", [P, 8, 512], F32))}
        load_constants(nc, a, c)
        with ExitStack() as even:
            def ev(name, shape):
                return even.enter_context(nc.sbuf_tensor(name, shape, F32))

            act_t = {"zaT": ev("zaT", [P, 4, NTOK]), "zbT": ev("zbT", [P, 4, NTOK]), "cqT": ev("cqT", [P, 3, NTOK]),
                     "ckvT": ev("ckvT", [P, 2, NTOK]), "krT": ev("krT", [P, NTOK]), "oa": ev("oa", [P, NTILE + 1, MW]),
                     "qlat": ev("qlat", [P, 2, MH, NS]), "qrope": ev("qrope", [P, MH, NS])}
            even_projection(nc, a, d, c, act_t)
            mla_prompt(nc, a, d, c, act_t)
            mla_sample(nc, a, d, c, act_t)
            with ExitStack() as s5:
                def sm(name, shape):
                    return s5.enter_context(nc.sbuf_tensor(name, shape, F32))

                m = {"out": sm("m_out", [P, 2, NPAIR, CH + 1, SC]), "binT": sm("m_binT", [P, 2, NPAIR, P]),
                     "toep": sm("m_toep", [P, SG, P]), "rot": sm("m_rot", [P, 2, NPAIR]), "l8": sm("m_l8", [P, NPAIR]),
                     "l4": sm("m_l4", [P, 2, NPAIR])}
                hlast = sm("m_hlast", [P, 2, NPAIR])
                s5_matrices(nc, a, d, c, m)
                s5_prompt(nc, a, d, c, m, hlast)
                s5_sample(nc, a, d, c, m, hlast)
            even_output(nc, a, d, c, act_t)
        with ExitStack() as odd:
            def od(name, shape):
                return odd.enter_context(nc.sbuf_tensor(name, shape, F32))

            o = {"gate": od("gate", [P, NTILE + 1, 3 * NH]), "kTs": od("kTs", [P, 2, NS]), "kcT": od("kcT", [P, DB, NBLK]),
                 "vc": od("vc", [NPAGE, DB, 2, KVW])}
            with ExitStack() as keys:
                def ky(name, shape):
                    return keys.enter_context(nc.sbuf_tensor(name, shape, F32))

                o.update(kv=ky("kv", [P, NTILE, 6 * KVW]), ksT=ky("ksT", [P, NG, SEQ]), kwT=ky("kwT", [P, NG, SEQ]),
                         kcp=ky("kcp", [P, NG, 2 * NTILE]), vcp=ky("vcp", [P, NG * HD]))
                odd_projection(nc, a, d, c, o)
                compress(nc, a, d, c, o)
                o["oall"] = odd.enter_context(nc.sbuf_tensor("oall", [P, NTILE, NW], F32, side="right"))
                nsa_prompt(nc, a, d, c, o)
            nsa_sample(nc, a, d, c, o)
            odd_output(nc, a, d, c, o)


def constants():
    f = np.float32
    i = np.arange(P)
    pos = np.concatenate([np.arange(SEQ), np.tile(PAST + np.arange(DT), DB)]).astype(f)
    half = ROPE // 2
    inv = (f(10000.0) ** (-np.arange(half, dtype=f) / half)).astype(f)
    ang = (pos[:, None] * inv[None]).astype(f)
    cos, sin = np.cos(ang).astype(f), np.sin(ang).astype(f)
    slope = (f(2.0) ** (f(-8.0) * np.arange(1, NH + 1, dtype=f) / f(NH))).astype(f)
    step = np.arange(DT)
    cpos = ((2 * np.arange(NTILE)[None] + np.arange(2)[:, None]) * BLK + BLK - 1).reshape(-1)
    cpast = ((2 * np.arange(NPAGE)[None] + np.arange(2)[:, None]) * BLK + BLK - 1).reshape(-1)
    qpos = np.arange(NTILE)[None, :, None] * P + i[:, None, None]
    rs = np.repeat(slope, DT)[:, None]
    rt = np.tile(step, NH)[:, None]
    rg = np.repeat(np.arange(NG), NR * DT)[:, None]
    bonus = np.zeros((NH * DT, NBLK + 1), f)
    bonus[:, [0, NBLK - 1, NBLK]] = NR + 1
    w = np.arange(WIN)[None]
    return {
        "c_ident": np.eye(P, dtype=f),
        "c_causal": np.where(i[None] > i[:, None], f(NEG), f(0)).astype(f),
        "c_winlow": np.where(i[None] < i[:, None], f(NEG), f(0)).astype(f),
        "c_rope": np.stack([cos, sin], 1),
        "c_rope_cosT": np.concatenate([cos.T, cos.T]),
        "c_rope_sinT": np.concatenate([-sin.T, sin.T]),
        "c_mla_new": np.tile(np.where(step[None] > step[:, None], f(NEG), f(0)).astype(f), (MH, 1)),
        "c_slope": np.repeat(slope[:, None], SEQ, 1),
        "c_kpos": (np.arange(SEQ, dtype=f) - SEQ)[None],
        "c_cpos": (cpos - SEQ).astype(f)[None],
        "c_cmask": np.where(cpos[None, None] <= qpos, f(0), f(NEG)).astype(f),
        "c_calibi": (rs * (cpast - PAST)[None]).astype(f),
        "c_bonus": bonus,
        "c_balibi": (rs * (np.arange(NBLK + 1) * BLK - PAST)[None]).astype(f),
        "c_kalibi": (rs * np.arange(BLK)[None]).astype(f),
        "c_nalibi": np.where(step[None] <= rt, rs * step[None], NEG).astype(f),
        "c_walibi": np.where(w >= rt, rs * (w - WIN), NEG).astype(f),
        "c_same": ((rg == rg.T) & (rt == rt.T)).astype(f),
    }


INPUTS = ["x_prompt", "x_sample", "cache_mla", "state_s5", "cache_nsa_kv", "state_nsa_win", "page_table",
          "norm_even", "w_in_even", "mla_g_q", "mla_g_kv", "mla_w_uq", "mla_w_uk", "mla_w_uv",
          "s5_lambda_re", "s5_lambda_im", "s5_log_dt", "s5_b_re", "s5_b_im", "s5_c_re", "s5_c_im", "s5_d",
          "s5_w_glu", "s5_b_glu", "w_out_even", "norm_odd", "w_in_odd", "nsa_pe_k", "nsa_pe_v",
          "nsa_phi1_k", "nsa_phi2_k", "nsa_phi1_v", "nsa_phi2_v", "w_out_odd", "norm_final"]
OUTPUTS = {"y_prompt": (1, SEQ, D_MODEL), "y_sample": (DB, DT, D_MODEL), "mla_rows_prompt": (1, 1, SEQ, ROW),
           "mla_rows_sample": (1, DB, DT, ROW), "s5_state_prompt": (1, 1, SG, SN, 2), "s5_state_sample": (1, DB, SG, SN, 2),
           "nsa_rows_prompt": (1, 1, SEQ, 4, NG, HD), "nsa_rows_sample": (1, DB, DT, 4, NG, HD),
           "nsa_win_prompt": (1, 1, WIN, 2, NG, HD), "nsa_win_sample": (1, DB, WIN, 2, NG, HD)}


def kernel(**inputs):
    import concourse.bacc as bacc
    from concourse.bass_utils import run_bass_kernel_spmd

    nc = bacc.Bacc("TRN2", target_bir_lowering=False, num_devices=1)
    arrays = {name: np.ascontiguousarray(inputs[name]) for name in INPUTS}
    for name, table in constants().items():
        arrays[name] = np.ascontiguousarray(table)
    a = {name: nc.dram_tensor(name, x.shape, mybir.dt.from_np(x.dtype), kind="ExternalInput").ap() for name, x in arrays.items()}
    for name, shape in OUTPUTS.items():
        a["o_" + name] = nc.dram_tensor("o_" + name, shape, F32, kind="ExternalOutput").ap()
    build(nc, a)
    result = run_bass_kernel_spmd(nc, [arrays], core_ids=[0]).results[0]
    return tuple(result["o_" + name] for name in OUTPUTS)
```
